# Optimizing a Trainium2 kernel written in Bass

```python
import jax, jax.numpy as jnp
from jax import lax
import numpy as np

D_MODEL = 1024
BATCH = 1
SEQ = 1024
DEPTH = 1

N_META = 16
Q_BLOCK = 128
EPS = 1e-6
FOX_HEADS = 8
FOX_HEAD_DIM = 64
FOX_W = FOX_HEADS * FOX_HEAD_DIM
MLA_HEADS = 8
MLA_Q_RANK = 256
MLA_KV_RANK = 128
MLA_NOPE_DIM = 64
MLA_ROPE_DIM = 32
MLA_QK_DIM = MLA_NOPE_DIM + MLA_ROPE_DIM
MLA_V_DIM = 64
MLA_W = MLA_HEADS * MLA_V_DIM
ROPE_THETA = 10000.0
D_FF = 2816
N_BRANCH = 2
IN_SIZES = (FOX_W, FOX_W, FOX_W, FOX_HEADS, MLA_Q_RANK, MLA_KV_RANK, MLA_ROPE_DIM, N_BRANCH * D_MODEL)
IN_W = FOX_W * 3 + FOX_HEADS + MLA_Q_RANK + MLA_KV_RANK + MLA_ROPE_DIM + N_BRANCH * D_MODEL

kernel_name = "hybrid_fox_mla_macaron_meta"

def rms_norm(x, gain):
    xf = x.astype(jnp.float32)
    y = xf * lax.rsqrt(jnp.mean(xf * xf, axis=-1, keepdims=True) + EPS)
    return (y * gain.astype(jnp.float32)).astype(x.dtype)

def swiglu_ffn(u, w_gu, w_down):
    g, up = jnp.split(u @ w_gu, 2, axis=-1)
    return (jax.nn.silu(g) * up) @ w_down

def rope(x, cos, sin):
    xf = x.astype(jnp.float32)
    x1, x2 = jnp.split(xf, 2, axis=-1)
    out = jnp.concatenate([x1 * cos - x2 * sin, x1 * sin + x2 * cos], axis=-1)
    return out.astype(x.dtype)

def block_causal_attention(q, k, v, log_forget_cum=None):
    L = q.shape[2]
    scale = q.shape[-1] ** -0.5
    bounds = [(0, N_META)] + [(N_META + i * Q_BLOCK, N_META + (i + 1) * Q_BLOCK)
                              for i in range((L - N_META) // Q_BLOCK)]
    outs = []
    for qs, qe in bounds:
        qb = q[:, :, qs:qe].astype(jnp.float32)
        kb = k[:, :, :qe].astype(jnp.float32)
        s = jnp.einsum("bhqd,bhkd->bhqk", qb, kb) * scale
        if log_forget_cum is not None:
            s = s + log_forget_cum[:, :, qs:qe, None] - log_forget_cum[:, :, None, :qe]
        mask = jnp.arange(qs, qe)[:, None] >= jnp.arange(qe)[None, :]
        p = jax.nn.softmax(jnp.where(mask, s, -jnp.inf), axis=-1)
        outs.append(jnp.einsum("bhqk,bhkd->bhqd", p.astype(v.dtype), v[:, :, :qe]))
    return jnp.concatenate(outs, axis=2)

def split_heads(t, n_heads):
    B, L, _ = t.shape
    return t.reshape(B, L, n_heads, -1).transpose(0, 2, 1, 3)

def merge_heads(t):
    B, H, L, dh = t.shape
    return t.transpose(0, 2, 1, 3).reshape(B, L, H * dh)

def token_mixing(u, w_in, b_forget, b_gate, fox_q_norm, fox_k_norm, mla_cq_norm, mla_w_uq,
                 mla_ckv_norm, mla_w_ukv, mla_q_norm, mla_k_norm, w_branch_fox, w_branch_mla,
                 w_out):
    B, L, _ = u.shape
    cuts = list(np.cumsum(IN_SIZES)[:-1])
    fq, fk, fv, f_logit, c_q, c_kv, k_rope, gate_logit = jnp.split(u @ w_in, cuts, axis=-1)

    fq = rms_norm(split_heads(fq, FOX_HEADS), fox_q_norm)
    fk = rms_norm(split_heads(fk, FOX_HEADS), fox_k_norm)
    fv = split_heads(fv, FOX_HEADS)
    log_f = jax.nn.log_sigmoid(f_logit.astype(jnp.float32) + b_forget.astype(jnp.float32))
    log_f_cum = jnp.cumsum(log_f.transpose(0, 2, 1), axis=-1)
    o_fox = merge_heads(block_causal_attention(fq, fk, fv, log_f_cum)) @ w_branch_fox

    q = split_heads(rms_norm(c_q, mla_cq_norm) @ mla_w_uq, MLA_HEADS)
    kv = split_heads(rms_norm(c_kv, mla_ckv_norm) @ mla_w_ukv, MLA_HEADS)
    k_nope, v = jnp.split(kv, [MLA_NOPE_DIM], axis=-1)
    k_rope_h = jnp.broadcast_to(k_rope[:, None], (B, MLA_HEADS, L, MLA_ROPE_DIM))
    k = jnp.concatenate([k_nope, k_rope_h], axis=-1)
    q = rms_norm(q, mla_q_norm)
    k = rms_norm(k, mla_k_norm)
    pos = jnp.arange(L, dtype=jnp.float32)
    inv_freq = ROPE_THETA ** (-jnp.arange(0, MLA_ROPE_DIM, 2, dtype=jnp.float32) / MLA_ROPE_DIM)
    ang = pos[:, None] * inv_freq[None, :]
    cos, sin = jnp.cos(ang), jnp.sin(ang)
    q = jnp.concatenate([q[..., :MLA_NOPE_DIM], rope(q[..., MLA_NOPE_DIM:], cos, sin)], axis=-1)
    k = jnp.concatenate([k[..., :MLA_NOPE_DIM], rope(k[..., MLA_NOPE_DIM:], cos, sin)], axis=-1)
    o_mla = merge_heads(block_causal_attention(q, k, v)) @ w_branch_mla

    g_fox, g_mla = jnp.split(jax.nn.sigmoid(gate_logit + b_gate), N_BRANCH, axis=-1)
    return (g_fox * o_fox + g_mla * o_mla) @ w_out

def setup_inputs(seed: int = 0) -> dict:
    key = jax.random.key(seed)
    ks = iter(jax.random.split(key, 32))

    def w(shape, fan_in):
        return jax.random.normal(next(ks), shape, jnp.float32) * fan_in ** -0.5

    def gain(shape):
        return 1.0 + 0.1 * jax.random.normal(next(ks), shape, jnp.float32)

    def bias(shape, scale=0.1, center=0.0):
        return center + scale * jax.random.normal(next(ks), shape, jnp.float32)

    Dp = DEPTH
    return {
        "x": jax.random.normal(next(ks), (BATCH, SEQ, D_MODEL), jnp.float32),
        "meta_tokens": jax.random.normal(next(ks), (N_META, D_MODEL), jnp.float32),
        "ffn1_norm": gain((Dp, D_MODEL)),
        "ffn1_w_gu": w((Dp, D_MODEL, 2 * D_FF), D_MODEL),
        "ffn1_w_down": w((Dp, D_FF, D_MODEL), D_FF),
        "mix_norm": gain((Dp, D_MODEL)),
        "w_in": w((Dp, D_MODEL, IN_W), D_MODEL),
        "b_forget": bias((Dp, FOX_HEADS), 0.1, 2.0),
        "b_gate": bias((Dp, N_BRANCH * D_MODEL)),
        "fox_q_norm": gain((Dp, FOX_HEAD_DIM)),
        "fox_k_norm": gain((Dp, FOX_HEAD_DIM)),
        "mla_cq_norm": gain((Dp, MLA_Q_RANK)),
        "mla_w_uq": w((Dp, MLA_Q_RANK, MLA_HEADS * MLA_QK_DIM), MLA_Q_RANK),
        "mla_ckv_norm": gain((Dp, MLA_KV_RANK)),
        "mla_w_ukv": w((Dp, MLA_KV_RANK, MLA_HEADS * (MLA_NOPE_DIM + MLA_V_DIM)), MLA_KV_RANK),
        "mla_q_norm": gain((Dp, MLA_QK_DIM)),
        "mla_k_norm": gain((Dp, MLA_QK_DIM)),
        "w_branch_fox": w((Dp, FOX_W, D_MODEL), FOX_W),
        "w_branch_mla": w((Dp, MLA_W, D_MODEL), MLA_W),
        "w_out": w((Dp, D_MODEL, D_MODEL), D_MODEL),
        "ffn2_norm": gain((Dp, D_MODEL)),
        "ffn2_w_gu": w((Dp, D_MODEL, 2 * D_FF), D_MODEL),
        "ffn2_w_down": w((Dp, D_FF, D_MODEL), D_FF),
    }

def reference(x, meta_tokens, ffn1_norm, ffn1_w_gu, ffn1_w_down, mix_norm, w_in, b_forget, b_gate,
              fox_q_norm, fox_k_norm, mla_cq_norm, mla_w_uq, mla_ckv_norm, mla_w_ukv, mla_q_norm,
              mla_k_norm, w_branch_fox, w_branch_mla, w_out, ffn2_norm, ffn2_w_gu, ffn2_w_down):
    B = x.shape[0]
    meta = jnp.broadcast_to(meta_tokens.astype(x.dtype)[None], (B, N_META, D_MODEL))
    h = jnp.concatenate([meta, x], axis=1)
    for l in range(DEPTH):
        h = h + 0.5 * swiglu_ffn(rms_norm(h, ffn1_norm[l]), ffn1_w_gu[l], ffn1_w_down[l])
        h = h + token_mixing(rms_norm(h, mix_norm[l]), w_in[l], b_forget[l], b_gate[l],
                             fox_q_norm[l], fox_k_norm[l], mla_cq_norm[l], mla_w_uq[l],
                             mla_ckv_norm[l], mla_w_ukv[l], mla_q_norm[l], mla_k_norm[l],
                             w_branch_fox[l], w_branch_mla[l], w_out[l])
        h = h + 0.5 * swiglu_ffn(rms_norm(h, ffn2_norm[l]), ffn2_w_gu[l], ffn2_w_down[l])
    return h[:, N_META:]


_drawn_inputs = setup_inputs


def setup_inputs(seed=0):
    import zlib

    import numpy as np

    out = dict(_drawn_inputs(seed))
    spreads = {}
    factors = {'b_forget': 41.56,
     'b_gate': 6.36,
     'fox_q_norm': 3.04,
     'fox_k_norm': 3.045,
     'mla_cq_norm': 8.0,
     'mla_ckv_norm': 5.295,
     'mla_q_norm': 8.0,
     'mla_k_norm': 8.0,
     'ffn2_norm': 4.301}
    for name, (base, spread) in spreads.items():
        noise = np.random.default_rng([zlib.crc32(name.encode()), seed]).standard_normal(out[name].shape)
        drawn = base * np.exp(spread * noise) if base else spread * noise
        out[name] = __import__('jax').numpy.asarray(drawn.astype(out[name].dtype))
    for name, factor in factors.items():
        out[name] = (out[name] * factor).astype(out[name].dtype)
    return out
```

```python
from contextlib import ExitStack

import numpy as np

import concourse.bass as bass
from concourse import mybir

F32 = mybir.dt.float32
F32R = mybir.dt.float32r
ACT = mybir.ActivationFunctionType
ALU = mybir.AluOpType
AX_X = mybir.AxisListType.X

P = 128
D = 1024
KD = D // P
META = 16
SEQ = 1024
T = META + SEQ
QT = SEQ // P
DFF = 2816
FT = DFF // P
HEADS = 8
PAIRS = HEADS // 2
FOX_D = 64
NOPE, ROPE = 64, 32
MLA_D = NOPE + ROPE
VD = 64
CQ, CKV = 256, 128
EPS = 1e-6
NEG = -1.0e30
KEYS = 9 * P

ALL_TOKENS = [(0, 348), (348, 346), (694, 346)]
REAL_TOKENS = [(META, 512), (META + 512, 512)]


def mm3(nc, out, w_hi, w_lo, x_hi, x_lo, first, last):
    nc.tensor.matmul(out, w_hi, x_hi, start=first, stop=False)
    nc.tensor.matmul(out, w_lo, x_hi, start=False, stop=False)
    return nc.tensor.matmul(out, w_hi, x_lo, start=False, stop=last)


def load_phase(nc, g):
    with ExitStack() as s:
        sb = lambda n, sh, dt=F32: s.enter_context(nc.sbuf_tensor("ld_" + n, sh, dt))
        sem = lambda n: g.semaphore("ld_" + n)
        xin = sb("xin", [P, 3, D])
        metain = sb("metain", [META, D])
        tp = [s.enter_context(nc.psum_tensor(f"ld_tp{i}", [P, 4, P], F32)) for i in range(4)]
        x_in = [sem(f"x_in{i}") for i in range(3)]
        meta_in, transposed, copied, consts_in = sem("meta_in"), sem("transposed"), sem("copied"), sem("consts_in")
        block = s.enter_context(nc.Block())

        @block.sync
        def _(sp):
            sp.dma_start(g.ident[:, :], g.dram["ident"]).then_inc(consts_in, 16)
            sp.dma_start(metain[:, :], g.dram["meta"]).then_inc(meta_in, 16)
            for t in range(QT):
                if t >= 3:
                    sp.wait_ge(transposed, 2 * (t - 2))
                sp.dma_start(xin[:, t % 3, :], g.dram["x"][t * P:(t + 1) * P, :]).then_inc(x_in[t % 3], 16)
            sp.dma_start(g.gains[:, :], g.dram["gains"]).then_inc(consts_in, 16)
            sp.dma_start(g.ones[:, :], g.dram["ones"]).then_inc(consts_in, 16)
            sp.wait_ge(consts_in, 48)

        @block.tensor
        def _(pe):
            pe.wait_ge(consts_in, 16)
            for t in range(QT):
                pe.wait_ge(x_in[t % 3], 16 * (t // 3 + 1))
                for half in range(2):
                    n = 2 * t + half
                    if n >= 4:
                        pe.wait_ge(copied, n - 3)
                    for k in range(4):
                        kk = 4 * half + k
                        last = nc.tensor.transpose(tp[n % 4][:, k, :], xin[:, t % 3, kk * P:(kk + 1) * P],
                                                   g.ident[:, :])
                    last.then_inc(transposed, 1)
            pe.wait_ge(meta_in, 16)
            for half in range(2):
                n = 2 * QT + half
                pe.wait_ge(copied, n - 3)
                for k in range(4):
                    kk = 4 * half + k
                    last = nc.tensor.transpose(tp[n % 4][:, k, 0:META], metain[:, kk * P:(kk + 1) * P],
                                               g.ident[0:META, 0:META])
                last.then_inc(transposed, 1)

        @block.vector
        def _(dve):
            for t in range(QT):
                for half in range(2):
                    n = 2 * t + half
                    dve.wait_ge(transposed, n + 1)
                    nc.vector.tensor_copy(g.h[:, 4 * half:4 * half + 4, META + t * P:META + (t + 1) * P],
                                          tp[n % 4][:, :, :]).then_inc(copied, 1)
            for half in range(2):
                n = 2 * QT + half
                dve.wait_ge(transposed, n + 1)
                nc.vector.tensor_copy(g.h[:, 4 * half:4 * half + 4, 0:META],
                                      tp[n % 4][:, :, 0:META]).then_inc(copied, 1)


def norm_phase(nc, g, tag, gain_col, chunks):
    lo_t, hi_t = chunks[0][0], chunks[-1][0] + chunks[-1][1]
    n_tok = hi_t - lo_t
    with ExitStack() as s:
        sb = lambda n, sh, dt=F32: s.enter_context(nc.sbuf_tensor(f"{tag}_{n}", sh, dt))
        sem = lambda n: g.semaphore(f"{tag}_{n}")
        sq = sb("sq", [P, 2, T])
        rstd = sb("rstd", [P, T])
        u32 = sb("u32", [P, 4, 512])
        sums = [s.enter_context(nc.psum_tensor(f"{tag}_sums{i}", [P, 512], F32)) for i in range(len(chunks))]
        squared, summed, rooted, inverted = sem("squared"), sem("summed"), sem("rooted"), sem("inverted")
        u_done, hi_done, lo_done = sem("u_done"), sem("hi_done"), sem("lo_done")
        block = s.enter_context(nc.Block())
        units = [(c, k) for c in range(len(chunks)) for k in range(KD)]

        @block.scalar
        def _(act):
            for k in range(KD):
                if k >= 2:
                    act.wait_ge(summed, k - 1)
                nc.scalar.activation(sq[:, k % 2, 0:n_tok], g.h[:, k, lo_t:hi_t], ACT.Square).then_inc(squared, 1)
            act.wait_ge(summed, KD)
            for c, (t0, n) in enumerate(chunks):
                nc.scalar.activation(rstd[:, t0:t0 + n], sums[c][:, 0:n], ACT.Sqrt, scale=1.0 / D,
                                     bias=g.gains[:, g.EPS_COL:g.EPS_COL + 1]).then_inc(rooted, 1)
            for i, (c, k) in enumerate(units):
                t0, n = chunks[c]
                act.wait_ge(u_done, i + 1)
                nc.scalar.copy(g.u_hi[:, k, t0:t0 + n], u32[:, i % 4, 0:n]).then_inc(hi_done, 1)

        @block.tensor
        def _(pe):
            for k in range(KD):
                pe.wait_ge(squared, k + 1)
                for c, (t0, n) in enumerate(chunks):
                    last = nc.tensor.matmul(sums[c][:, 0:n], g.ones[:, :], sq[:, k % 2, t0 - lo_t:t0 - lo_t + n],
                                            start=(k == 0), stop=(k == KD - 1))
                last.then_inc(summed, 1)

        @block.vector
        def _(dve):
            for c, (t0, n) in enumerate(chunks):
                dve.wait_ge(rooted, c + 1)
                nc.vector.reciprocal(rstd[:, t0:t0 + n], rstd[:, t0:t0 + n]).then_inc(inverted, 1)
            for i, (c, k) in enumerate(units):
                t0, n = chunks[c]
                dve.wait_ge(inverted, c + 1)
                if i >= 4:
                    dve.wait_ge(lo_done, i - 3)
                nc.vector.scalar_tensor_tensor(u32[:, i % 4, 0:n], g.h[:, k, t0:t0 + n],
                                               g.gains[:, gain_col + k:gain_col + k + 1], rstd[:, t0:t0 + n],
                                               ALU.mult, ALU.mult).then_inc(u_done, 1)

        @block.gpsimd
        def _(pool):
            for i, (c, k) in enumerate(units):
                t0, n = chunks[c]
                pool.wait_ge(hi_done, i + 1)
                nc.gpsimd.tensor_tensor(g.u_lo[:, k, t0:t0 + n], u32[:, i % 4, 0:n],
                                        g.u_hi[:, k, t0:t0 + n].bitcast(F32), ALU.subtract).then_inc(lo_done, 1)


def ffn_phase(nc, g, tag, d_blocks, chunks):
    groups = FT // 2
    C = len(chunks)
    U = 2 * C
    V = KD * C
    n_blocks = 3 * FT
    with ExitStack() as s:
        sb = lambda n, sh, dt=F32: s.enter_context(nc.sbuf_tensor(f"{tag}_{n}", sh, dt))
        sem = lambda n: g.semaphore(f"{tag}_{n}")
        raw = sb("raw", [P, 3, D])
        w_hi = sb("w_hi", [P, 6, D], F32R)
        w_lo = sb("w_lo", [P, 6, D], F32R)
        hid_hi = sb("hid_hi", [P, 2, 2, T], F32R)
        hid_lo = sb("hid_lo", [P, 2, 2, T], F32R)
        silu = sb("silu", [P, 2, 512])
        h32 = sb("h32", [P, 512])
        bank = [s.enter_context(nc.psum_tensor(f"{tag}_bank{i}", [P, 512], F32)) for i in range(8)]
        raw_in = [sem(f"raw_in{i}") for i in range(3)]
        whi_done, wlo_done = sem("whi_done"), sem("wlo_done")
        gate_ready, up_ready, silu_done, h32_done = sem("gate_ready"), sem("up_ready"), sem("silu_done"), sem("h32_done")
        hid_hi_done, hid_done = sem("hid_hi_done"), sem("hid_done")
        down_ready, down_added = sem("down_ready"), sem("down_added")
        block = s.enter_context(nc.Block())

        @block.sync
        def _(sp):
            for n in range(3):
                sp.dma_start(raw[:, n, :], d_blocks[n]).then_inc(raw_in[n], 16)
            with sp.Fori(1, n_blocks // 3) as r:
                for n in range(3):
                    sp.wait_ge(wlo_done, 3 * r + (n - 2))
                    sp.dma_start(raw[:, n, :], d_blocks[3 * r + n]).then_inc(raw_in[n], 16)

        def gu_block(i, j):
            return j if isinstance(i, int) and i == 0 else 6 * i + (j - 2)

        def d_block(i, j):
            last = isinstance(i, int) and i == groups - 1
            return 6 * i + (j + 4 if last else j + 8)

        @block.scalar
        def _(act):
            def split_hi(n_rem, n, slot, times):
                act.wait_ge(raw_in[n_rem], 16 * times)
                nc.scalar.copy(w_hi[:, slot, :], raw[:, n_rem, :]).then_inc(whi_done, 1)

            def split_gu(i, f):
                act.wait_ge(up_ready, U * i + (C * (f + 1) - U))
                for j in (2 * f, 2 * f + 1):
                    split_hi((j - 2) % 3, None, j, 2 * i + ((j - 2) // 3 + 1))

            def split_d(i):
                if not (isinstance(i, int) and i == 0):
                    act.wait_ge(down_ready, V * i)
                last = isinstance(i, int) and i == groups - 1
                for j in range(2):
                    m = j + (4 if last else 8)
                    split_hi(m % 3, None, 4 + j, 2 * i + (m // 3 + 1))

            def group(i, more, parity_first=False):
                for f in range(2):
                    for c, (t0, n) in enumerate(chunks):
                        u = C * f + c
                        act.wait_ge(gate_ready, U * i + (u + 1))
                        if not (parity_first and u < 2):
                            act.wait_ge(h32_done, U * i + (u - 1))
                        nc.scalar.activation(silu[:, u % 2, 0:n], bank[2 * (u % 2)][:, 0:n],
                                             ACT.Silu).then_inc(silu_done, 1)
                    if more:
                        split_gu(i + 1, f)

            for j in range(4):
                split_hi(j % 3, j, j, j // 3 + 1)
            group(0, True, parity_first=True)
            split_d(0)
            group(1, True)
            with act.Fori(2, groups - 1) as i:
                split_d(i - 1)
                group(i, True)
            split_d(groups - 2)
            group(groups - 1, False)
            split_d(groups - 1)

        @block.gpsimd
        def _(pool):
            def split_lo(n, slot, raw_slot):
                pool.wait_ge(whi_done, n + 1)
                nc.gpsimd.tensor_tensor(w_lo[:, slot, :], raw[:, raw_slot, :], w_hi[:, slot, :].bitcast(F32),
                                        ALU.subtract).then_inc(wlo_done, 1)
            for n in range(4):
                split_lo(n, n, n % 3)
            with pool.Fori(1, groups) as i:
                for j in range(6):
                    split_lo(6 * i + (j - 2), j, (j - 2) % 3)
            for j in range(2):
                split_lo(n_blocks - 2 + j, 4 + j, (n_blocks - 2 + j) % 3)

        @block.tensor
        def _(pe):
            def gate_up(i, first=False):
                for f in range(2):
                    for c, (t0, n) in enumerate(chunks):
                        u = C * f + c
                        for which, ready, freed in ((0, gate_ready, silu_done), (1, up_ready, h32_done)):
                            slot = 2 * f + which
                            if c == 0:
                                pe.wait_ge(wlo_done, gu_block(i, slot) + 1)
                            if not (first and u < 2):
                                pe.wait_ge(freed, U * i + (u - 1))
                            out = bank[2 * (u % 2) + which]
                            for k in range(KD):
                                last = mm3(nc, out[:, 0:n], w_hi[:, slot, k * P:(k + 1) * P],
                                           w_lo[:, slot, k * P:(k + 1) * P], g.u_hi[:, k, t0:t0 + n],
                                           g.u_lo[:, k, t0:t0 + n], k == 0, k == KD - 1)
                            last.then_inc(ready, 1)

            def down(i, parity, first=False):
                pe.wait_ge(hid_done, U * i + U)
                pe.wait_ge(wlo_done, d_block(i, 1) + 1)
                for d in range(KD):
                    for c, (t0, n) in enumerate(chunks):
                        v = C * d + c
                        if not (first and v < 4):
                            pe.wait_ge(down_added, V * i + (v - 3))
                        for f in range(2):
                            last = mm3(nc, bank[4 + v % 4][:, 0:n], w_hi[:, 4 + f, d * P:(d + 1) * P],
                                       w_lo[:, 4 + f, d * P:(d + 1) * P], hid_hi[:, parity, f, t0:t0 + n],
                                       hid_lo[:, parity, f, t0:t0 + n], f == 0, f == 1)
                        last.then_inc(down_ready, 1)

            gate_up(0, first=True)
            gate_up(1)
            down(0, 0, first=True)
            with pe.Fori(2, groups - 1, 2) as i:
                gate_up(i)
                down(i - 1, 1)
                gate_up(i + 1)
                down(i, 0)
            gate_up(groups - 1)
            down(groups - 2, 1)
            down(groups - 1, 0)

        @block.vector
        def _(dve):
            def hidden(i, parity, first=False, reuse=True):
                if reuse:
                    dve.wait_ge(down_ready, V * (i - 1))
                for f in range(2):
                    for c, (t0, n) in enumerate(chunks):
                        u = C * f + c
                        dve.wait_ge(silu_done, U * i + (u + 1))
                        dve.wait_ge(up_ready, U * i + (u + 1))
                        if not (first and u == 0):
                            dve.wait_ge(hid_done, U * i + u)
                        nc.vector.tensor_tensor(h32[:, 0:n], silu[:, u % 2, 0:n], bank[2 * (u % 2) + 1][:, 0:n],
                                                ALU.mult).then_inc(h32_done, 1)
                        dve.wait_ge(h32_done, U * i + (u + 1))
                        nc.vector.tensor_copy(hid_hi[:, parity, f, t0:t0 + n], h32[:, 0:n]).then_inc(hid_hi_done, 1)
                        dve.wait_ge(hid_hi_done, U * i + (u + 1))
                        nc.vector.tensor_tensor(hid_lo[:, parity, f, t0:t0 + n], h32[:, 0:n],
                                                hid_hi[:, parity, f, t0:t0 + n].bitcast(F32),
                                                ALU.subtract).then_inc(hid_done, 1)

            def add_down(i, first=False):
                for d in range(KD):
                    for c, (t0, n) in enumerate(chunks):
                        v = C * d + c
                        dve.wait_ge(down_ready, V * i + (v + 1))
                        if not first:
                            dve.wait_ge(down_added, V * i + (v + 1 - V))
                        nc.vector.scalar_tensor_tensor(g.h[:, d, t0:t0 + n], bank[4 + v % 4][:, 0:n], 0.5,
                                                       g.h[:, d, t0:t0 + n], ALU.mult, ALU.add).then_inc(down_added, 1)

            hidden(0, 0, first=True, reuse=False)
            hidden(1, 1, reuse=False)
            add_down(0, first=True)
            with dve.Fori(2, groups - 1, 2) as i:
                hidden(i, 0)
                add_down(i - 1)
                hidden(i + 1, 1)
                add_down(i)
            hidden(groups - 1, 0)
            add_down(groups - 2)
            add_down(groups - 1)


def wait(eng, sem, p, per_pair, more):
    if isinstance(p, int):
        if per_pair * p + more > 0:
            eng.wait_ge(sem, per_pair * p + more)
    else:
        eng.wait_ge(sem, per_pair * p + more)


def over_pairs(eng, body):
    body(0)
    with eng.Fori(1, PAIRS - 1) as p:
        body(p)
    body(PAIRS - 1, last=True)


QK_TOKENS = [(0, 384), (384, 384), (768, 272)]
QK_TILES = [(0, 128, 256), (0, 128, 256), (0, 128, 144)]
LO_DVE = 4


def lo_counts(units_done):
    return units_done - units_done // LO_DVE, units_done // LO_DVE


ST_UNITS = []
for _c, (_q0, _n) in enumerate(REAL_TOKENS):
    for _kt in range(9):
        _a = max(_q0, P * _kt)
        if _a < _q0 + _n:
            ST_UNITS.append((_c, _kt, min(P * _kt, T - P), _a, _q0 + _n - _a))
NW = len(ST_UNITS)
LAST_OF = [max(w for w in range(NW) if ST_UNITS[w][0] == c) for c in range(2)]

MAX_UNITS = []
for _i in range(QT):
    _end = META + P * (_i + 1)
    _cuts = [0] + [x for x in (400, 912) if x < _end] + [_end]
    for _j in range(len(_cuts) - 1):
        MAX_UNITS.append((_i, _j, _cuts[_j], _cuts[_j + 1] - _cuts[_j]))
NM = len(MAX_UNITS)


def forget_phase(nc, g):
    with ExitStack() as s:
        sb = lambda n, sh, dt=F32: s.enter_context(nc.sbuf_tensor("fg_" + n, sh, dt))
        sem = lambda n: g.semaphore("fg_" + n)
        raw = sb("raw", [P, D])
        w_hi, w_lo = sb("w_hi", [P, D], F32R), sb("w_lo", [P, D], F32R)
        cf = sb("cf", [P, 2 * P + META])
        out = sb("out", [P, T])
        mag, lse, zmin = sb("mag", [HEADS, T]), sb("lse", [HEADS, T]), sb("zmin", [HEADS, T])
        one, cum = sb("one", [HEADS, T]), sb("cum", [HEADS, T])
        c_hi, c_lo = sb("c_hi", [HEADS, T], F32R), sb("c_lo", [HEADS, T], F32R)
        acc = [s.enter_context(nc.psum_tensor(f"fg_acc{i}", [P, 512], F32)) for i in range(3)]
        h_out, w_in, const_in, spilled = sem("h_out"), sem("w_in"), sem("const_in"), sem("spilled")
        const_done, whi, wlo, ready, copied = sem("const_done"), sem("whi"), sem("wlo"), sem("ready"), sem("copied")
        step_a, step_v = sem("step_a"), sem("step_v")
        block = s.enter_context(nc.Block())

        @block.sync
        def _(sp):
            sp.dma_start(raw[:, :], g.dram["misc"][0]).then_inc(w_in, 16)
            sp.dma_start(cf[:, :], g.dram["masks"][:, 0:2 * P + META]).then_inc(const_in, 16)
            sp.dma_start(g.head_sum[:, :], g.dram["masks"][:, 2 * P + META:3 * P + META]).then_inc(const_in, 16)
            sp.dma_start(g.rot[:, :], g.dram["masks"][:, 3 * P + META:4 * P + META]).then_inc(const_in, 16)
            sp.dma_start(g.dram["hsave"], g.h[:, :, :]).then_inc(h_out, 16)
            sp.wait_ge(copied, 3)
            sp.dma_start(g.dram["krope"], out[NOPE:MLA_D, :]).then_inc(spilled, 16)
            sp.wait_ge(step_v, 6)
            sp.dma_start(g.dram["cum"][0], c_hi[:, :].bitcast(F32)).then_inc(spilled, 16)
            sp.dma_start(g.dram["cum"][1], c_lo[:, :].bitcast(F32)).then_inc(spilled, 16)
            sp.wait_ge(spilled, 48)
            sp.wait_ge(h_out, 16)

        @block.scalar
        def _(act):
            act.wait_ge(w_in, 16)
            nc.scalar.copy(w_hi[:, :], raw[:, :]).then_inc(whi, 1)
            act.wait_ge(const_in, 48)
            nc.scalar.copy(g.ident_r[:, :], g.ident[:, :]).then_inc(const_done, 1)
            nc.scalar.copy(g.masks[:, :], cf[:, :]).then_inc(const_done, 1)
            act.wait_ge(copied, 3)
            bias = g.gains[0:HEADS, g.BF_COL:g.BF_COL + 1]
            nc.scalar.activation(mag[:, :], out[0:HEADS, :], ACT.Abs, bias=bias).then_inc(step_a, 1)
            act.wait_ge(step_a, 1)
            nc.scalar.activation(mag[:, :], mag[:, :], ACT.Exp, scale=-1.0).then_inc(step_a, 1)
            act.wait_ge(step_a, 2)
            nc.scalar.activation(lse[:, :], mag[:, :], ACT.Ln, bias=g.ones[0:HEADS, 0:1]).then_inc(step_a, 1)

        @block.gpsimd
        def _(pool):
            pool.wait_ge(whi, 1)
            nc.gpsimd.tensor_tensor(w_lo[:, :], raw[:, :], w_hi[:, :].bitcast(F32), ALU.subtract).then_inc(wlo, 1)

        @block.tensor
        def _(pe):
            pe.wait_ge(wlo, 1)
            for c, (t0, n) in enumerate(ALL_TOKENS):
                for k in range(KD):
                    last = mm3(nc, acc[c][:, 0:n], w_hi[:, k * P:(k + 1) * P], w_lo[:, k * P:(k + 1) * P],
                               g.u_hi[:, k, t0:t0 + n], g.u_lo[:, k, t0:t0 + n], k == 0, k == KD - 1)
                last.then_inc(ready, 1)

        @block.vector
        def _(dve):
            nc.vector.memset(one[:, :], 1.0).then_inc(step_v, 1)
            for c, (t0, n) in enumerate(ALL_TOKENS):
                dve.wait_ge(ready, c + 1)
                nc.vector.tensor_copy(out[:, t0:t0 + n], acc[c][:, 0:n]).then_inc(copied, 1)
            dve.wait_ge(copied, 3)
            nc.vector.tensor_scalar(zmin[:, :], out[0:HEADS, :], g.gains[0:HEADS, g.BF_COL:g.BF_COL + 1], 0.0,
                                    ALU.add, ALU.min).then_inc(step_v, 1)
            dve.wait_ge(step_v, 2)
            dve.wait_ge(step_a, 3)
            nc.vector.tensor_tensor(zmin[:, :], lse[:, :], zmin[:, :], ALU.subtract).then_inc(step_v, 1)
            dve.wait_ge(step_v, 3)
            nc.vector.tensor_tensor_scan(cum[:, :], one[:, :], zmin[:, :], 0.0, ALU.mult, ALU.add).then_inc(step_v, 1)
            dve.wait_ge(step_v, 4)
            nc.vector.tensor_copy(c_hi[:, :], cum[:, :]).then_inc(step_v, 1)
            dve.wait_ge(step_v, 5)
            nc.vector.tensor_tensor(c_lo[:, :], cum[:, :], c_hi[:, :].bitcast(F32), ALU.subtract).then_inc(step_v, 1)


def latent_phase(nc, g):
    with ExitStack() as s:
        sb = lambda n, sh, dt=F32: s.enter_context(nc.sbuf_tensor("lt_" + n, sh, dt))
        sem = lambda n: g.semaphore("lt_" + n)
        raw = sb("raw", [P, 3, D])
        w_hi, w_lo = sb("w_hi", [P, 3, D], F32R), sb("w_lo", [P, 3, D], F32R)
        sq = sb("sq", [P, 2, 348])
        rs = sb("rs", [P, 2, 348])
        kr = sb("kr", [P, T])
        t1 = sb("t1", [P, 348])
        bank = [s.enter_context(nc.psum_tensor(f"lt_bank{i}", [P, 512], F32)) for i in range(6)]
        w_in = [sem(f"w_in{i}") for i in range(3)]
        const_in, whi, wlo = sem("const_in"), sem("whi"), sem("wlo")
        ready, squared, summed, logged, rooted, normed = (sem("ready"), sem("squared"), sem("summed"),
                                                          sem("logged"), sem("rooted"), sem("normed"))
        ksq_done = sem("ksq_done")
        kr_gained, kr_turned, kr_steps = sem("kr_gained"), sem("kr_turned"), sem("kr_steps")
        block = s.enter_context(nc.Block())
        C = ALL_TOKENS

        @block.sync
        def _(sp):
            for j in range(3):
                sp.dma_start(raw[:, j, :], g.dram["misc"][1 + j]).then_inc(w_in[j], 16)
            sp.dma_start(kr[NOPE:MLA_D, :], g.dram["krope"]).then_inc(const_in, 16)
            sp.dma_start(g.cos[NOPE:MLA_D, :], g.dram["cos"]).then_inc(const_in, 16)
            sp.dma_start(g.sin[NOPE:MLA_D, :], g.dram["sin"]).then_inc(const_in, 16)
            sp.wait_ge(const_in, 48)

        @block.gpsimd
        def _(pool):
            for j in range(3):
                pool.wait_ge(whi, j + 1)
                nc.gpsimd.tensor_tensor(w_lo[:, j, :], raw[:, j, :], w_hi[:, j, :].bitcast(F32),
                                        ALU.subtract).then_inc(wlo, 1)

        @block.tensor
        def _(pe):
            pe.wait_ge(kr_gained, 1)
            for c, (t0, n) in enumerate(C):
                nc.tensor.matmul(bank[c][0:MLA_D, 0:n], g.rot[NOPE:MLA_D, 0:MLA_D], kr[NOPE:MLA_D, t0:t0 + n],
                                 start=True, stop=True).then_inc(kr_turned, 1)
            for c, (t0, n) in enumerate(C):
                for j in range(3):
                    pe.wait_ge(wlo, j + 1)
                    if c == 0:
                        pe.wait_ge(kr_steps, 3 * (j + 1))
                    else:
                        pe.wait_ge(normed, 3 * (c - 1) + j + 1)
                    for k in range(KD):
                        last = mm3(nc, bank[j][:, 0:n], w_hi[:, j, k * P:(k + 1) * P],
                                   w_lo[:, j, k * P:(k + 1) * P], g.u_hi[:, k, t0:t0 + n],
                                   g.u_lo[:, k, t0:t0 + n], k == 0, k == KD - 1)
                    last.then_inc(ready, 1)
                for j in range(3):
                    pe.wait_ge(squared, 3 * c + j + 1)
                    if c and j < 2:
                        pe.wait_ge(logged, 2 * c - 1 + j)
                    dst = bank[3 if j == 0 else 4]
                    nc.tensor.matmul(dst[:, 0:n], g.ones[:, :], sq[:, (3 * c + j) % 2, 0:n], start=(j != 2),
                                     stop=(j != 1)).then_inc(summed, 1)

        @block.scalar
        def _(act):
            for j in range(3):
                act.wait_ge(w_in[j], 16)
                nc.scalar.copy(w_hi[:, j, :], raw[:, j, :]).then_inc(whi, 1)
            act.wait_ge(const_in, 48)
            nc.scalar.activation(g.ksq[NOPE:MLA_D, :], kr[NOPE:MLA_D, :], ACT.Square).then_inc(ksq_done, 1)
            for c, (t0, n) in enumerate(C):
                for j in range(3):
                    act.wait_ge(ready, 3 * c + j + 1)
                    if 3 * c + j >= 2:
                        act.wait_ge(summed, 3 * c + j - 1)
                    nc.scalar.activation(sq[:, (3 * c + j) % 2, 0:n], bank[j][:, 0:n], ACT.Square).then_inc(squared, 1)
                for r in range(2):
                    act.wait_ge(summed, 3 * c + (1 if r == 0 else 3))
                    if c:
                        act.wait_ge(normed, 3 * (c - 1) + (1 if r == 0 else 3))
                    nc.scalar.activation(rs[:, r, 0:n], bank[3 + r][:, 0:n], ACT.Ln,
                                         scale=1.0 / (CKV if r == 0 else CQ),
                                         bias=g.gains[:, g.EPS_COL:g.EPS_COL + 1]).then_inc(logged, 1)
                    act.wait_ge(logged, 2 * c + r + 1)
                    nc.scalar.activation(rs[:, r, 0:n], rs[:, r, 0:n], ACT.Exp, scale=-0.5).then_inc(rooted, 1)

        @block.vector
        def _(dve):
            dve.wait_ge(const_in, 48)
            dve.wait_ge(ksq_done, 1)
            gk = g.gains[NOPE:MLA_D, g.MK_COL:g.MK_COL + 1]
            nc.vector.tensor_scalar(kr[NOPE:MLA_D, :], kr[NOPE:MLA_D, :], gk, None, ALU.mult).then_inc(kr_gained, 1)
            dve.wait_ge(kr_gained, 1)
            for c, (t0, n) in enumerate(C):
                r = slice(NOPE, MLA_D)
                nc.vector.tensor_tensor(g.krope[r, t0:t0 + n], kr[r, t0:t0 + n], g.cos[r, t0:t0 + n],
                                        ALU.mult).then_inc(kr_steps, 1)
                dve.wait_ge(kr_turned, c + 1)
                nc.vector.tensor_tensor(t1[r, 0:n], bank[c][r, 0:n], g.sin[r, t0:t0 + n], ALU.mult).then_inc(kr_steps, 1)
                dve.wait_ge(kr_steps, 3 * c + 2)
                nc.vector.tensor_tensor(g.krope[r, t0:t0 + n], g.krope[r, t0:t0 + n], t1[r, 0:n],
                                        ALU.add).then_inc(kr_steps, 1)
                dve.wait_ge(kr_steps, 3 * c + 3)
            for c, (t0, n) in enumerate(C):
                for j in range(3):
                    dve.wait_ge(rooted, 2 * c + (1 if j == 0 else 2))
                    dst = g.ckv[:, t0:t0 + n] if j == 0 else g.cq[:, j - 1, t0:t0 + n]
                    nc.vector.scalar_tensor_tensor(dst, bank[j][:, 0:n],
                                                   g.gains[:, g.CN_COL + j:g.CN_COL + j + 1],
                                                   rs[:, 0 if j == 0 else 1, 0:n], ALU.mult, ALU.mult).then_inc(normed, 1)


def attention_phase(nc, g, kind, o_out):
    fox = kind == "fox"
    DK = FOX_D if fox else MLA_D
    CR = 2 if fox else 0
    KMAX, KALL = DK + CR, DK + CR + 2
    NU = 6 if fox else 12
    with ExitStack() as s:
        sb = lambda n, sh, dt=F32: s.enter_context(nc.sbuf_tensor(f"{kind}_{n}", sh, dt))
        sem = lambda n: g.semaphore(f"{kind}_{n}")
        q_hi = [sb(f"q_hi{i}", [KALL, T], F32R) for i in range(2)]
        q_lo = [sb(f"q_lo{i}", [DK, T], F32R) for i in range(2)]
        k_hi = [sb(f"k_hi{i}", [KALL, T], F32R) for i in range(2)]
        k_lo = [sb(f"k_lo{i}", [DK, T], F32R) for i in range(2)]
        v_hi, v_lo = sb("v_hi", [P, 9, 3 * VD], F32R), sb("v_lo", [P, 9, 3 * VD], F32R)
        p32 = sb("p32", [P, 2, 512])
        p_hi, p_lo = sb("p_hi", [P, 3, 512], F32R), sb("p_lo", [P, 3, 512], F32R)
        rs = sb("rs", [P, 2, 384])
        x32 = sb("x32", [P, 2, 384])
        rden = sb("rden", [P, 512])
        NH = 2 if fox else 1
        ms, r0, nt = sb("ms", [P, 2, 3 * NH]), sb("r0", [P, 2, 3 * NH]), sb("nt", [P, 2, 3 * NH])
        threes = sb("threes", [P, 3 * NH])
        mpart, nm = sb("mpart", [P, QT, 3]), sb("nm", [P, P])
        m_hi, m_lo = sb("m_hi", [QT, P], F32R), sb("m_lo", [QT, P], F32R)
        if fox:
            r_wide = sb("r_wide", [P, 2, 3 * NH, FOX_D])
            raw = sb("raw", [P, 3, D])
            w_hi, w_lo = sb("w_hi", [P, 3, D], F32R), sb("w_lo", [P, 3, D], F32R)
        else:
            w_pair = sb("w_pair", [P, 2 * 2 * MLA_D + 2 * P])
        bank = [s.enter_context(nc.psum_tensor(f"{kind}_bank{i}", [P, 512], F32)) for i in range(8)]
        PROJ, SUM, BC, TURN = (bank[0], bank[1], bank[4], bank[5]), bank[2], bank[6:8], bank[3]
        VB, MAXB, MT = (bank[3], bank[7]), bank[0:2], bank[3]
        ST, OB = (bank[2], bank[4], bank[5]), bank[6:8]
        V_BANK = [t % 2 for t in range(8)] + [1]

        ones_set = sem("ones_set")
        raw_in = [sem(f"raw_in{i}") for i in range(3)]
        whi_done, wlo_done = sem("whi_done"), sem("wlo_done")
        cum_in, m_in = sem("cum_in"), sem("m_in")
        proj_ready, squared, sum_ready, ms_done, logged, rooted, newton = (
            sem("proj_ready"), sem("squared"), sem("sum_ready"), sem("ms_done"), sem("logged"), sem("rooted"),
            sem("newton"))
        bc_ready, rs_done = sem("bc_ready"), sem("rs_done")
        x_done, x_turned, rope_steps, xhi_done, qk_done = (sem("x_done"), sem("x_turned"), sem("rope_steps"),
                                                           sem("xhi_done"), sem("qk_done"))
        v_ready, vhi_done, v_done = sem("v_ready"), sem("vhi_done"), sem("v_done")
        max_ready, max_read, nm_done, mt_ready, mhi_done, m_done = (sem("max_ready"), sem("max_read"),
                                                                    sem("nm_done"), sem("mt_ready"),
                                                                    sem("mhi_done"), sem("m_done"))
        st_ready, exp_done, phi_done, plo_pool, plo_dve, pv_done = (sem("st_ready"), sem("exp_done"),
                                                                    sem("phi_done"), sem("plo_pool"),
                                                                    sem("plo_dve"), sem("pv_done"))
        ln_done, rden_done, o_done = sem("ln_done"), sem("rden_done"), sem("o_done")
        block = s.enter_context(nc.Block())
        PW, PM = 2 * NW, 2 * NM
        LO_P, LO_V = lo_counts(PW)

        def wait_split(eng, p, units_done):
            by_pool, by_dve = lo_counts(units_done) if units_done > 0 else (0, 0)
            wait(eng, plo_pool, p, LO_P, by_pool)
            wait(eng, plo_dve, p, LO_V, by_dve)

        W_HI_AT, W_LO_AT = [2, 5, 8, 11, 14, 17], [4, 7, 10, 13, 16, 19]
        if fox:
            units = [(which == 0, None, c) for which in range(2) for c in range(3)]
        else:
            units = [(which == 0, h, c) for h in range(2) for which in range(2) for c in range(3)]
        finish_after = {}
        for h in range(2):
            for c in range(2):
                finish_after.setdefault(min(NW * h + LAST_OF[c] + 4, PW - 1), []).append((h, c))

        @block.sync
        def _(sp):
            sp.wait_ge(ones_set, 1)

            def weights(p):
                if fox:
                    for j in range(3):
                        wait(sp, wlo_done, p, 6, 2 * j - 4)
                        sp.dma_start(raw[:, j, :], g.dram["fox"][3 * p + j]).then_inc(raw_in[j], 16)
                else:
                    wait(sp, v_ready, p, 9, 0)
                    sp.dma_start(w_pair[:, :], g.dram["mla"][p]).then_inc(raw_in[0], 16)

            def pair(p, last=False):
                if fox:
                    for h in range(2):
                        wait(sp, pv_done, p, PW, 0)
                        sp.dma_start(k_hi[h][DK:DK + 2, :].bitcast(F32),
                                     g.dram["cum"][:, 2 * p + h, :]).then_inc(cum_in, 16)
                if not last:
                    weights(p + 1)
                for h in range(2):
                    wait(sp, m_done, p, 2, h + 1)
                    for src, r in ((m_hi, KMAX), (m_lo, KMAX + 1)):
                        sp.dma_start(q_hi[h][r:r + 1, META:T].bitcast(F32).rearrange("o (a b) -> o a b", a=QT),
                                     src[:, :].bitcast(F32)).then_inc(m_in, 16)
            weights(0)
            over_pairs(sp, pair)

        @block.gpsimd
        def _(pool):
            pool.wait_ge(ones_set, 1)

            def pair(p, last=False):
                for u in range(NU):
                    r, m, t = r0[:, u % 2, :], ms[:, u % 2, :], nt[:, u % 2, :]
                    wait(pool, rooted, p, NU, u + 1)
                    nc.gpsimd.tensor_tensor(t, m, r, ALU.mult).then_inc(newton, 1)
                    wait(pool, newton, p, 4 * NU, 4 * u + 1)
                    nc.gpsimd.tensor_tensor(t, t, r, ALU.mult).then_inc(newton, 1)
                    wait(pool, newton, p, 4 * NU, 4 * u + 2)
                    nc.gpsimd.tensor_tensor(t, threes[:, :], t, ALU.subtract).then_inc(newton, 1)
                    wait(pool, newton, p, 4 * NU, 4 * u + 3)
                    if fox:
                        wait(pool, bc_ready, p, NU, u - 1)
                        wide = [P, 3 * NH, FOX_D]
                        nc.gpsimd.tensor_tensor(r_wide[:, u % 2], r.unsqueeze(2).broadcast_to(wide),
                                                t.unsqueeze(2).broadcast_to(wide), ALU.mult).then_inc(newton, 1)
                    else:
                        nc.gpsimd.tensor_tensor(r, r, t, ALU.mult).then_inc(newton, 1)
                for w in range(PW):
                    if w % LO_DVE == LO_DVE - 1:
                        continue
                    n = ST_UNITS[w % NW][4]
                    wait(pool, phi_done, p, PW, w + 1)
                    nc.gpsimd.tensor_tensor(p_lo[:, w % 3, 0:n], p32[:, w % 2, 0:n], p_hi[:, w % 3, 0:n].bitcast(F32),
                                            ALU.subtract).then_inc(plo_pool, 1)
            over_pairs(pool, pair)

        @block.scalar
        def _(act):
            def weights_hi(p, i):
                j, x = i // 2, slice(512 * (i % 2), 512 * (i % 2) + 512)
                act.wait_ge(raw_in[j], 16 * (p + 1))
                wait(act, proj_ready, p, NU, 0)
                wait(act, v_ready, p, 9, 0)
                nc.scalar.copy(w_hi[:, j, x], raw[:, j, x]).then_inc(whi_done, 1)

            def pair(p, last=False):
                for s_ in range(NU + 2):
                    u = s_
                    if u < NU:
                        is_q, h, c = units[u]
                        t0, n = QK_TOKENS[c]
                        src = PROJ[u % 4]
                        wait(act, proj_ready, p, NU, u + 1)
                        wait(act, sum_ready, p, NU, u - 1)
                        if u < 2:
                            wait_split(act, p, 0)
                        if fox or is_q:
                            R = P if fox else DK
                            nc.scalar.activation(p32[0:R, u % 2, 0:n], src[0:R, 0:n], ACT.Square).then_inc(squared, 1)
                        else:
                            nc.scalar.activation(g.ksq[0:NOPE, t0:t0 + n], src[0:NOPE, 0:n],
                                                 ACT.Square).then_inc(squared, 1)
                    u = s_ - 1
                    if 0 <= u < NU:
                        wait(act, ms_done, p, NU, u + 1)
                        wait(act, bc_ready, p, NU, u - 1)
                        nc.scalar.activation(r0[:, u % 2, :], ms[:, u % 2, :], ACT.Ln).then_inc(logged, 1)
                        wait(act, logged, p, NU, u + 1)
                        nc.scalar.activation(r0[:, u % 2, :], r0[:, u % 2, :], ACT.Exp, scale=-0.5).then_inc(rooted, 1)
                    u = s_ - 2
                    if u >= 0:
                        n, R = QK_TOKENS[units[u][2]][1], (P if fox else DK)
                        wait(act, bc_ready, p, NU, u + 1)
                        wait(act, x_done, p, NU, u - 1)
                        nc.scalar.copy(rs[0:R, u % 2, 0:n], BC[u % 2][0:R, 0:n]).then_inc(rs_done, 1)
                for t in range(9):
                    src = VB[V_BANK[t]][:, 0:P].rearrange("p (a b) -> p a b", a=2)
                    hi = v_hi[:, t, :].rearrange("p (a b) -> p a b", a=3)[:, 0:3:2, :]
                    wait(act, v_ready, p, 9, t + 1)
                    nc.scalar.copy(hi, src).then_inc(vhi_done, 1)

                for w in range(PW):
                    n = ST_UNITS[w % NW][4]
                    wait(act, st_ready, p, PW, w + 1)
                    wait_split(act, p, w - 1)
                    nc.scalar.activation(p32[:, w % 2, 0:n], ST[w % 3][:, 0:n], ACT.Exp).then_inc(exp_done, 1)
                    for h, c in finish_after.get(w, ()):
                        rows, ones_rows = (slice(0, VD), slice(VD, P))[::1 if h == 0 else -1]
                        f = 2 * h + c
                        wait(act, pv_done, p, PW, NW * h + LAST_OF[c] + 1)
                        wait(act, o_done, p, 4, f)
                        nc.scalar.activation(rden[rows, :], OB[c][ones_rows, :], ACT.Ln).then_inc(ln_done, 1)
                        wait(act, ln_done, p, 4, f + 1)
                        nc.scalar.activation(rden[rows, :], rden[rows, :], ACT.Exp, scale=-1.0).then_inc(rden_done, 1)
                    if fox and not last and w in W_HI_AT:
                        weights_hi(p + 1, W_HI_AT.index(w))
            act.preload_act_table_set("natural_log_exp_and_others")
            act.wait_ge(ones_set, 1)
            if fox:
                for i in range(6):
                    weights_hi(0, i)
            over_pairs(act, pair)

        @block.tensor
        def _(pe):
            pe.wait_ge(ones_set, 1)

            def pair(p, last=False):
                def products(u):
                    is_q, h, c = units[u]
                    t0, n = QK_TOKENS[c]
                    out = PROJ[u % 4]
                    if u < 2:
                        wait(pe, max_read, p, PM, 0)
                    elif u < 4:
                        wait(pe, exp_done, p, PW, 0)
                    else:
                        wait(pe, x_done, p, NU, u - 3)
                    if fox:
                        j = 0 if is_q else 1
                        if c == 0:
                            wait(pe, wlo_done, p, 6, 2 * j + 2)
                        for k in range(KD):
                            last = mm3(nc, out[:, 0:n], w_hi[:, j, k * P:(k + 1) * P], w_lo[:, j, k * P:(k + 1) * P],
                                       g.u_hi[:, k, t0:t0 + n], g.u_lo[:, k, t0:t0 + n], k == 0, k == KD - 1)
                    elif is_q:
                        pe.wait_ge(raw_in[0], 16 * (p + 1))
                        for k in range(2):
                            col = (2 * h + k) * MLA_D
                            last = nc.tensor.matmul(out[0:MLA_D, 0:n], w_pair[:, col:col + MLA_D],
                                                    g.cq[:, k, t0:t0 + n], start=(k == 0), stop=(k == 1))
                    else:
                        col = 4 * MLA_D + NOPE * h
                        last = nc.tensor.matmul(out[0:NOPE, 0:n], w_pair[:, col:col + NOPE], g.ckv[:, t0:t0 + n],
                                                start=True, stop=True)
                    last.then_inc(proj_ready, 1)

                def sums(u):
                    is_q, h, c = units[u]
                    t0, n = QK_TOKENS[c]
                    wait(pe, squared, p, NU, u + 1)
                    wait(pe, ms_done, p, NU, u)
                    if u == 0:
                        wait(pe, exp_done, p, PW, 0)
                    R = P if fox else DK
                    src = p32[0:R, u % 2, 0:n] if fox or is_q else g.ksq[0:R, t0:t0 + n]
                    per_head = g.head_sum[:, 0:P:FOX_D] if fox else g.ones[0:R, 0:1]
                    for i, off in enumerate(QK_TILES[c]):
                        last = nc.tensor.matmul(SUM[:, NH * i:NH * i + NH], src[:, off:off + P], per_head,
                                                start=True, stop=True)
                    last.then_inc(sum_ready, 1)

                def broadcast(u):
                    c = units[u][2]
                    wait(pe, newton, p, 4 * NU, 4 * u + 4)
                    if u < 2:
                        wait(pe, o_done, p, 4, 0)
                    else:
                        wait(pe, rs_done, p, NU, u - 1)
                    R = P if fox else DK
                    for i, off in enumerate(QK_TILES[c]):
                        if fox:
                            r = r_wide[:, u % 2, NH * i:NH * i + NH, :].rearrange("p a b -> p (a b)")
                        else:
                            r = r0[:, u % 2, i:i + 1].broadcast_to([P, R])
                        last = nc.tensor.matmul(BC[u % 2][0:R, off:off + P], r, g.ident[:, :], start=True, stop=True)
                    last.then_inc(bc_ready, 1)

                def turn(u):
                    t0, n = QK_TOKENS[units[u][2]]
                    q_count = sum(1 for x in units[:u + 1] if x[0])
                    wait(pe, x_done, p, NU, u + 1)
                    wait(pe, rope_steps, p, 18, 3 * (q_count - 1))
                    wait(pe, m_done, p, 2, 0)
                    nc.tensor.matmul(TURN[0:DK, 0:n], g.rot[NOPE:DK, 0:DK], x32[NOPE:DK, u % 2, 0:n],
                                     start=True, stop=True).then_inc(x_turned, 1)

                def values(t):
                    tok = min(P * t, T - P)
                    out = VB[V_BANK[t]]
                    wait(pe, v_done, p, 9, t if t == 8 else t - 1)
                    if t < 2:
                        wait(pe, o_done, p, 4, 0)
                        wait(pe, m_done, p, 2, 0)
                    if fox:
                        if t == 0:
                            wait(pe, wlo_done, p, 6, 6)
                        for k in range(KD):
                            last = mm3(nc, out[:, 0:P], g.u_hi[:, k, tok:tok + P], g.u_lo[:, k, tok:tok + P],
                                       w_hi[:, 2, k * P:(k + 1) * P], w_lo[:, 2, k * P:(k + 1) * P], k == 0, k == KD - 1)
                    else:
                        if t == 0:
                            wait(pe, rope_steps, p, 18, 18)
                        last = nc.tensor.matmul(out[:, 0:P], g.ckv[:, tok:tok + P],
                                                w_pair[:, 4 * MLA_D + P:4 * MLA_D + 2 * P], start=True, stop=True)
                    last.then_inc(v_ready, 1)

                def maxima(h, x):
                    i, part, k0, n = MAX_UNITS[x]
                    y = NM * h + x
                    out = MAXB[y % 2]
                    if y == 0:
                        wait(pe, qk_done, p, NU, NU)
                        if fox:
                            pe.wait_ge(cum_in, 32 * (p + 1))
                    wait(pe, max_read, p, PM, y - 1)
                    q0 = META + P * i
                    diagonal = k0 + n == q0 + P
                    last = nc.tensor.matmul(out[:, 0:n], q_hi[h][0:KMAX, q0:q0 + P], k_hi[h][0:KMAX, k0:k0 + n],
                                            start=True, stop=not diagonal)
                    if diagonal:
                        last = nc.tensor.matmul(out[:, n - P:n], g.ident_r[:, :], g.masks[:, P:2 * P],
                                                start=False, stop=True)
                    last.then_inc(max_ready, 1)

                def turn_maxima(h):
                    wait(pe, nm_done, p, 2, h + 1)
                    wait(pe, v_done, p, 9, 7)
                    wait(pe, m_done, p, 2, h)
                    nc.tensor.transpose(MT[:, 0:P], nm[:, :], g.ident[:, :]).then_inc(mt_ready, 1)

                def scores(w):
                    h, (c, kt, k0, q0, n) = w // NW, ST_UNITS[w % NW]
                    out = ST[w % 3]
                    wait(pe, exp_done, p, PW, w - 2 if w >= 3 else 0)
                    if w % NW == 0:
                        pe.wait_ge(m_in, 64 * p + 32 * (h + 1))
                    kh, kl = k_hi[h][:, k0:k0 + P], k_lo[h][:, k0:k0 + P]
                    nc.tensor.matmul(out[:, 0:n], kh[0:KALL], q_hi[h][0:KALL, q0:q0 + n], start=True, stop=False)
                    nc.tensor.matmul(out[:, 0:n], kl[0:DK], q_hi[h][0:DK, q0:q0 + n], start=False, stop=False)
                    d0, d1 = max(q0, P * kt), min(q0 + n, P * kt + P)
                    diagonal = d0 < d1
                    last = nc.tensor.matmul(out[:, 0:n], kh[0:DK], q_lo[h][0:DK, q0:q0 + n], start=False,
                                            stop=not diagonal)
                    if diagonal:
                        m0 = 2 * P if kt == 8 else d0 - P * kt
                        last = nc.tensor.matmul(out[:, d0 - q0:d1 - q0], g.ident_r[:, :],
                                                g.masks[:, m0:m0 + d1 - d0], start=False, stop=True)
                    last.then_inc(st_ready, 1)

                def weigh(w):
                    h, (c, kt, k0, q0, n) = w // NW, ST_UNITS[w % NW]
                    cq0 = REAL_TOKENS[c][0]
                    out = OB[c][:, q0 - cq0:q0 - cq0 + n]
                    wait_split(pe, p, w + 1)
                    if kt == 0:
                        wait(pe, o_done, p, 4, 2 * h + c - 1)
                        if w == 0:
                            wait(pe, v_done, p, 9, 9)
                    cols = slice(VD * h, VD * h + P)
                    last_of = w % NW == LAST_OF[c]
                    nc.tensor.matmul(out, v_hi[:, kt, cols], p_hi[:, w % 3, 0:n], start=(kt == 0), stop=False)
                    nc.tensor.matmul(out, v_lo[:, kt, cols], p_hi[:, w % 3, 0:n], start=False, stop=False)
                    nc.tensor.matmul(out, v_hi[:, kt, cols], p_lo[:, w % 3, 0:n], start=False,
                                     stop=last_of).then_inc(pv_done, 1)

                for step in range(NU + 3):
                    if step < NU:
                        products(step)
                    if 1 <= step <= NU:
                        sums(step - 1)
                    if 2 <= step <= NU + 1:
                        broadcast(step - 2)
                    if step >= 3 and not fox and units[step - 3][0]:
                        turn(step - 3)
                for t in range(7):
                    values(t)
                    maxima(0, 2 * t)
                    maxima(0, 2 * t + 1)
                values(7)
                turn_maxima(0)
                values(8)
                for w in range(PW):
                    scores(w)
                    if w < NM // 2:
                        maxima(1, 2 * w)
                        maxima(1, 2 * w + 1)
                    if w == 9:
                        turn_maxima(1)
                    if w >= 3:
                        weigh(w - 3)
                for w in range(PW - 3, PW):
                    weigh(w)
            over_pairs(pe, pair)

        @block.vector
        def _(dve):
            for h in range(2):
                nc.vector.memset(q_hi[h][DK:KALL, :].bitcast(F32), 1.0)
                nc.vector.memset(k_hi[h][DK:KALL, :].bitcast(F32), 1.0)
            nc.vector.memset(v_lo[:, :, VD:2 * VD].bitcast(F32), 0.0)
            nc.vector.memset(nm[:, :], 0.0)
            nc.vector.memset(threes[:, :], 3.0)
            nc.vector.memset(mpart[:, :, :], NEG)
            nc.vector.memset(v_hi[:, :, VD:2 * VD].bitcast(F32), 1.0).then_inc(ones_set, 1)
            dve.wait_ge(ones_set, 1)

            def weights_lo(p, i):
                j, x = i // 2, slice(512 * (i % 2), 512 * (i % 2) + 512)
                wait(dve, whi_done, p, 6, i + 1)
                nc.vector.tensor_tensor(w_lo[:, j, x], raw[:, j, x], w_hi[:, j, x].bitcast(F32),
                                        ALU.subtract).then_inc(wlo_done, 1)

            def pair(p, last=False):
                def mean_squares(u):
                    is_q = units[u][0]
                    wait(dve, sum_ready, p, NU, u + 1)
                    wait(dve, newton, p, 4 * NU, 4 * u - 4)
                    nc.vector.tensor_scalar(ms[:, u % 2, :], SUM[:, 0:3 * NH], 4.0 if is_q else 4.0 / DK,
                                            4 * DK * EPS if is_q else 4 * EPS, ALU.mult, ALU.add).then_inc(ms_done, 1)

                def qk(u):
                    is_q, h, c = units[u]
                    t0, n = QK_TOKENS[c]
                    hi, lo = (q_hi, q_lo) if is_q else (k_hi, k_lo)
                    src = PROJ[u % 4]
                    wait(dve, rs_done, p, NU, u + 1)
                    wait(dve, pv_done, p, PW, 0)
                    if fox:
                        col = g.FQ_COL if is_q else g.FK_COL
                        for j in range(2):
                            r = slice(FOX_D * j, FOX_D * (j + 1))
                            if j == 0:
                                wait(dve, qk_done, p, NU, u)
                            last = nc.vector.scalar_tensor_tensor(x32[0:FOX_D, j, 0:n], src[r, 0:n],
                                                                  g.gains[r, col:col + 1], rs[r, u % 2, 0:n],
                                                                  ALU.mult, ALU.mult)
                        last.then_inc(x_done, 1)
                        wait(dve, x_done, p, NU, u + 1)
                        for j in range(2):
                            last = nc.vector.tensor_copy(hi[j][0:FOX_D, t0:t0 + n], x32[0:FOX_D, j, 0:n])
                        last.then_inc(xhi_done, 1)
                        wait(dve, xhi_done, p, NU, u + 1)
                        for j in range(2):
                            last = nc.vector.tensor_tensor(lo[j][0:FOX_D, t0:t0 + n], x32[0:FOX_D, j, 0:n],
                                                           hi[j][0:FOX_D, t0:t0 + n].bitcast(F32), ALU.subtract)
                        last.then_inc(qk_done, 1)
                        return
                    x = x32[:, u % 2, 0:n]
                    rope = slice(NOPE, MLA_D)
                    wait(dve, qk_done, p, NU, u - 1)
                    if is_q:
                        nc.vector.scalar_tensor_tensor(x[0:DK], src[0:DK, 0:n], g.gains[0:DK, g.MQ_COL:g.MQ_COL + 1],
                                                       rs[0:DK, u % 2, 0:n], ALU.mult, ALU.mult).then_inc(x_done, 1)
                    else:
                        nc.vector.tensor_tensor(x[rope], g.krope[rope, t0:t0 + n], rs[rope, u % 2, 0:n], ALU.mult)
                        nc.vector.scalar_tensor_tensor(x[0:NOPE], src[0:NOPE, 0:n],
                                                       g.gains[0:NOPE, g.MK_COL:g.MK_COL + 1],
                                                       rs[0:NOPE, u % 2, 0:n], ALU.mult, ALU.mult).then_inc(x_done, 1)

                def split(u):
                    is_q, h, c = units[u]
                    t0, n = QK_TOKENS[c]
                    hi, lo = (q_hi, q_lo) if is_q else (k_hi, k_lo)
                    x = x32[:, u % 2, 0:n]
                    rope = slice(NOPE, MLA_D)
                    if is_q:
                        q_count = sum(1 for y in units[:u + 1] if y[0])
                        wait(dve, x_turned, p, 6, q_count)
                        wait(dve, x_done, p, NU, u + 1)
                        nc.vector.tensor_tensor(x[rope], x[rope], g.cos[rope, t0:t0 + n],
                                                ALU.mult).then_inc(rope_steps, 1)
                        nc.vector.tensor_tensor(rden[rope, 0:n], TURN[rope, 0:n], g.sin[rope, t0:t0 + n],
                                                ALU.mult).then_inc(rope_steps, 1)
                        wait(dve, rope_steps, p, 18, 3 * q_count - 1)
                        nc.vector.tensor_tensor(x[rope], x[rope], rden[rope, 0:n], ALU.add).then_inc(rope_steps, 1)
                        wait(dve, rope_steps, p, 18, 3 * q_count)
                    else:
                        wait(dve, x_done, p, NU, u + 1)
                    nc.vector.tensor_copy(hi[h][0:DK, t0:t0 + n], x[0:DK]).then_inc(xhi_done, 1)
                    wait(dve, xhi_done, p, NU, u + 1)
                    nc.vector.tensor_tensor(lo[h][0:DK, t0:t0 + n], x[0:DK], hi[h][0:DK, t0:t0 + n].bitcast(F32),
                                            ALU.subtract).then_inc(qk_done, 1)

                def values(t):
                    src = VB[V_BANK[t]][:, 0:P].rearrange("p (a b) -> p a b", a=2)
                    hi = v_hi[:, t, :].rearrange("p (a b) -> p a b", a=3)[:, 0:3:2, :]
                    lo = v_lo[:, t, :].rearrange("p (a b) -> p a b", a=3)[:, 0:3:2, :]
                    wait(dve, vhi_done, p, 9, t + 1)
                    nc.vector.tensor_tensor(lo, src, hi.bitcast(F32), ALU.subtract).then_inc(v_done, 1)

                def maxima(h, x):
                    i, part, k0, n = MAX_UNITS[x]
                    wait(dve, max_ready, p, PM, NM * h + x + 1)
                    if x == 0:
                        wait(dve, nm_done, p, 2, h)
                    nc.vector.tensor_reduce(mpart[:, i, part:part + 1], MAXB[(NM * h + x) % 2][:, 0:n], AX_X,
                                            ALU.max).then_inc(max_read, 1)

                def join_maxima(h):
                    wait(dve, max_read, p, PM, NM * (h + 1))
                    wait(dve, mt_ready, p, 2, h)
                    nc.vector.tensor_reduce(nm[:, 0:QT], mpart[:, :, :], AX_X, ALU.max, negate=True).then_inc(nm_done, 1)

                def split_maxima(h):
                    wait(dve, mt_ready, p, 2, h + 1)
                    wait(dve, m_in, p, 64, 32 * h)
                    nc.vector.tensor_copy(m_hi[:, :], MT[0:QT, 0:P]).then_inc(mhi_done, 1)
                    wait(dve, mhi_done, p, 2, h + 1)
                    nc.vector.tensor_tensor(m_lo[:, :], MT[0:QT, 0:P], m_hi[:, :].bitcast(F32),
                                            ALU.subtract).then_inc(m_done, 1)

                for step in range(NU + 3):
                    if 1 <= step <= NU:
                        mean_squares(step - 1)
                    if 2 <= step <= NU + 1:
                        qk(step - 2)
                    if step >= 3 and not fox:
                        split(step - 3)
                for t in range(7):
                    values(t)
                    maxima(0, 2 * t)
                    maxima(0, 2 * t + 1)
                join_maxima(0)
                values(7)
                split_maxima(0)
                values(8)
                for w in range(PW):
                    n = ST_UNITS[w % NW][4]
                    if w < NM // 2:
                        maxima(1, 2 * w)
                        maxima(1, 2 * w + 1)
                    if w == NM // 2:
                        join_maxima(1)
                    wait(dve, exp_done, p, PW, w + 1)
                    wait(dve, pv_done, p, PW, w - 2 if w >= 3 else 0)
                    nc.vector.tensor_copy(p_hi[:, w % 3, 0:n], p32[:, w % 2, 0:n]).then_inc(phi_done, 1)
                    if w % LO_DVE == LO_DVE - 1:
                        wait(dve, phi_done, p, PW, w + 1)
                        nc.vector.tensor_tensor(p_lo[:, w % 3, 0:n], p32[:, w % 2, 0:n],
                                                p_hi[:, w % 3, 0:n].bitcast(F32), ALU.subtract).then_inc(plo_dve, 1)
                    if w == 9:
                        split_maxima(1)
                    for h, c in finish_after.get(w, ()):
                        rows = slice(VD * h, VD * h + VD)
                        q0 = REAL_TOKENS[c][0] - META
                        wait(dve, rden_done, p, 4, 2 * h + c + 1)
                        nc.vector.tensor_tensor(o_out[rows, p, q0:q0 + 512], OB[c][rows, :], rden[rows, :],
                                                ALU.mult).then_inc(o_done, 1)
                    if fox and not last and w in W_LO_AT:
                        weights_lo(p + 1, W_LO_AT.index(w))
            if fox:
                for i in range(6):
                    weights_lo(0, i)
            over_pairs(dve, pair)


def gate_phase(nc, g):
    with ExitStack() as s:
        sb = lambda n, sh, dt=F32: s.enter_context(nc.sbuf_tensor("gt_" + n, sh, dt))
        sem = lambda n: g.semaphore("gt_" + n)
        raw = sb("raw", [P, 3, D])
        w_hi, w_lo = sb("w_hi", [P, 3, D], F32R), sb("w_lo", [P, 3, D], F32R)
        o_hi, o_lo = sb("o_hi", [P, KD, SEQ], F32R), sb("o_lo", [P, KD, SEQ], F32R)
        sg = sb("sg", [P, 3, 512])
        bank = [s.enter_context(nc.psum_tensor(f"gt_bank{i}", [P, 512], F32)) for i in range(8)]
        raw_in = [sem(f"raw_in{i}") for i in range(3)]
        whi_done, wlo_done, ohi_done, olo_done = sem("whi_done"), sem("wlo_done"), sem("ohi_done"), sem("olo_done")
        ready, opened, shut, mult_done = sem("ready"), sem("opened"), sem("shut"), sem("mult_done")
        uhi_done, ulo_done = sem("uhi_done"), sem("ulo_done")
        block = s.enter_context(nc.Block())
        o_tile = lambda t: (g.o_fox if t < PAIRS else g.o_mla)[:, t % PAIRS, :]
        UNITS = [("gf", 0), ("gf", 1), ("gm", 0), ("bf", 0), ("bm", 0), ("gm", 1), ("bf", 1), ("bm", 1)]

        def over_tiles(eng, body):
            body(0)
            with eng.Fori(1, KD) as m:
                body(m)

        @block.sync
        def _(sp):
            def tile(m):
                for j in range(3):
                    wait(sp, wlo_done, m, 3, j - 2)
                    sp.dma_start(raw[:, j, :], g.dram["gate"][3 * m + j]).then_inc(raw_in[j], 16)
            over_tiles(sp, tile)

        @block.gpsimd
        def _(pool):
            def split_lo(m, j):
                wait(pool, whi_done, m, 3, j + 1)
                nc.gpsimd.tensor_tensor(w_lo[:, j, :], raw[:, j, :], w_hi[:, j, :].bitcast(F32),
                                        ALU.subtract).then_inc(wlo_done, 1)
            for j in range(2):
                split_lo(0, j)
            for t in range(0, KD, 2):
                pool.wait_ge(ohi_done, t + 1)
                nc.gpsimd.tensor_tensor(o_lo[:, t, :], o_tile(t), o_hi[:, t, :].bitcast(F32),
                                        ALU.subtract).then_inc(olo_done, 1)
            split_lo(0, 2)
            with pool.Fori(1, KD) as m:
                for j in range(3):
                    split_lo(m, j)

        @block.scalar
        def _(act):
            def split_hi(m, j, used):
                act.wait_ge(raw_in[j], 16 * (m + 1))
                wait(act, ready, m, 8, used - 8)
                nc.scalar.copy(w_hi[:, j, :], raw[:, j, :]).then_inc(whi_done, 1)

            def sigmoid(m, which, c, slot, unit):
                wait(act, ready, m, 8, unit + 1)
                wait(act, shut, m, 4, {0: -2 + 0, 1: 0, 2: 0, 5: 2}[unit])
                bias = g.gains[:, bass.ds(m + (g.BG_COL + KD * which), 1)]
                nc.scalar.activation(sg[:, slot, :], bank[unit][:, :], ACT.Sigmoid, bias=bias).then_inc(opened, 1)

            def tile(m, more=True):
                if not (isinstance(m, int) and m == 0):
                    split_hi(m, 2, 8)
                sigmoid(m, 0, 0, 0, 0)
                sigmoid(m, 0, 1, 1, 1)
                if more:
                    split_hi(m + 1, 0, 2)
                sigmoid(m, 1, 0, 2, 2)
                sigmoid(m, 1, 1, 2, 5)
                if more:
                    split_hi(m + 1, 1, 6)

            split_hi(0, 0, 0)
            split_hi(0, 1, 0)
            for t in range(KD):
                nc.scalar.copy(o_hi[:, t, :], o_tile(t)).then_inc(ohi_done, 1)
            split_hi(0, 2, 0)
            for m in range(KD):
                tile(m, more=m < KD - 1)
            for t in range(KD):
                act.wait_ge(ready, 8 * KD)
                act.wait_ge(shut, 4 * KD)
                nc.scalar.copy(g.u_hi[:, t, META:T], o_tile(t)).then_inc(uhi_done, 1)

        @block.tensor
        def _(pe):
            def tile(m):
                for u, (kind, c) in enumerate(UNITS):
                    t0 = REAL_TOKENS[c][0]
                    out = bank[u]
                    if kind[0] == "g":
                        wait(pe, opened, m, 4, {0: -3, 1: -2, 2: -1, 5: 0}[u])
                        j = 0 if kind == "gf" else 1
                        if c == 0:
                            wait(pe, wlo_done, m, 3, j + 1)
                        for k in range(KD):
                            last = mm3(nc, out[:, :], w_hi[:, j, k * P:(k + 1) * P], w_lo[:, j, k * P:(k + 1) * P],
                                       g.u_hi[:, k, t0:t0 + 512], g.u_lo[:, k, t0:t0 + 512], k == 0, k == KD - 1)
                    else:
                        wait(pe, shut, m, 4, {3: -3, 4: -2, 6: -1, 7: 0}[u])
                        if u == 3:
                            wait(pe, wlo_done, m, 3, 3)
                            pe.wait_ge(olo_done, KD)
                        first = 0 if kind == "bf" else PAIRS
                        for k in range(first, first + PAIRS):
                            x = slice(512 * c, 512 * c + 512)
                            last = mm3(nc, out[:, :], w_hi[:, 2, k * P:(k + 1) * P], w_lo[:, 2, k * P:(k + 1) * P],
                                       o_hi[:, k, x], o_lo[:, k, x], k == first, k == first + PAIRS - 1)
                    last.then_inc(ready, 1)
            over_tiles(pe, tile)

        @block.vector
        def _(dve):
            def tile(m, dst, m_dst):
                for c in range(2):
                    base = (3, 6)[c]
                    for which in range(2):
                        slot = c if which == 0 else 2
                        wait(dve, ready, m, 8, base + which + 1)
                        wait(dve, opened, m, 4, {(0, 0): 1, (0, 1): 3, (1, 0): 2, (1, 1): 4}[(c, which)])
                        ins = nc.vector.tensor_tensor(sg[:, slot, :], bank[base + which][:, :], sg[:, slot, :], ALU.mult)
                        if which == 0:
                            ins.then_inc(shut, 1)
                        else:
                            ins.then_inc(mult_done, 1)
                    wait(dve, mult_done, m, 2, c + 1)
                    wait(dve, shut, m, 4, 2 * c + 1)
                    nc.vector.tensor_tensor(dst[:, m_dst, 512 * c:512 * c + 512], sg[:, c, :], sg[:, 2, :],
                                            ALU.add).then_inc(shut, 1)

            for t in range(1, KD, 2):
                dve.wait_ge(ohi_done, t + 1)
                nc.vector.tensor_tensor(o_lo[:, t, :], o_tile(t), o_hi[:, t, :].bitcast(F32),
                                        ALU.subtract).then_inc(olo_done, 1)
            dve.wait_ge(olo_done, KD)
            tile(0, g.o_fox, 0)
            with dve.Fori(1, PAIRS) as m:
                tile(m, g.o_fox, m)
            with dve.Fori(PAIRS, KD) as m:
                tile(m, g.o_mla, m - PAIRS)
            for t in range(KD):
                dve.wait_ge(uhi_done, t + 1)
                nc.vector.tensor_tensor(g.u_lo[:, t, META:T], o_tile(t), g.u_hi[:, t, META:T].bitcast(F32),
                                        ALU.subtract).then_inc(ulo_done, 1)


def out_proj_phase(nc, g):
    with ExitStack() as s:
        sb = lambda n, sh, dt=F32: s.enter_context(nc.sbuf_tensor("op_" + n, sh, dt))
        sem = lambda n: g.semaphore("op_" + n)
        raw = sb("raw", [P, 3, D])
        w_hi, w_lo = sb("w_hi", [P, 3, D], F32R), sb("w_lo", [P, 3, D], F32R)
        bank = [s.enter_context(nc.psum_tensor(f"op_bank{i}", [P, 512], F32)) for i in range(4)]
        raw_in = [sem(f"raw_in{i}") for i in range(3)]
        h_in = [sem(f"h_in{i}") for i in range(KD)]
        whi_done, wlo_done, ready, added = sem("whi_done"), sem("wlo_done"), sem("ready"), sem("added")
        block = s.enter_context(nc.Block())

        @block.sync
        def _(sp):
            for m in range(KD):
                if m >= 3:
                    sp.wait_ge(wlo_done, m - 2)
                sp.dma_start(raw[:, m % 3, :], g.dram["wout"][m]).then_inc(raw_in[m % 3], 16)
                sp.dma_start(g.h[:, m, :], g.dram["hsave"][:, m, :]).then_inc(h_in[m], 16)

        @block.scalar
        def _(act):
            for m in range(KD):
                act.wait_ge(raw_in[m % 3], 16 * (m // 3 + 1))
                if m >= 3:
                    act.wait_ge(ready, 2 * (m - 2))
                nc.scalar.copy(w_hi[:, m % 3, :], raw[:, m % 3, :]).then_inc(whi_done, 1)

        @block.gpsimd
        def _(pool):
            for m in range(KD):
                pool.wait_ge(whi_done, m + 1)
                nc.gpsimd.tensor_tensor(w_lo[:, m % 3, :], raw[:, m % 3, :], w_hi[:, m % 3, :].bitcast(F32),
                                        ALU.subtract).then_inc(wlo_done, 1)

        @block.tensor
        def _(pe):
            for m in range(KD):
                pe.wait_ge(wlo_done, m + 1)
                for c, (t0, n) in enumerate(REAL_TOKENS):
                    u = 2 * m + c
                    if u >= 4:
                        pe.wait_ge(added, u - 3)
                    for k in range(KD):
                        last = mm3(nc, bank[u % 4][:, :], w_hi[:, m % 3, k * P:(k + 1) * P],
                                   w_lo[:, m % 3, k * P:(k + 1) * P], g.u_hi[:, k, t0:t0 + n],
                                   g.u_lo[:, k, t0:t0 + n], k == 0, k == KD - 1)
                    last.then_inc(ready, 1)

        @block.vector
        def _(dve):
            for m in range(KD):
                dve.wait_ge(h_in[m], 16)
                for c, (t0, n) in enumerate(REAL_TOKENS):
                    u = 2 * m + c
                    dve.wait_ge(ready, u + 1)
                    nc.vector.tensor_tensor(g.h[:, m, t0:t0 + n], g.h[:, m, t0:t0 + n], bank[u % 4][:, :],
                                            ALU.add).then_inc(added, 1)


def store_phase(nc, g):
    with ExitStack() as s:
        sem = lambda n: g.semaphore("st_" + n)
        rows = s.enter_context(nc.sbuf_tensor("st_rows", [P, 3, D], F32))
        tp = [s.enter_context(nc.psum_tensor(f"st_tp{i}", [P, 4, P], F32)) for i in range(4)]
        transposed, copied = sem("transposed"), sem("copied")
        stored = [sem(f"stored{i}") for i in range(3)]
        block = s.enter_context(nc.Block())

        @block.tensor
        def _(pe):
            for t in range(QT):
                for half in range(2):
                    n = 2 * t + half
                    if n >= 4:
                        pe.wait_ge(copied, n - 3)
                    for k in range(4):
                        last = nc.tensor.transpose(tp[n % 4][:, k, :],
                                                   g.h[:, 4 * half + k, META + t * P:META + (t + 1) * P], g.ident[:, :])
                    last.then_inc(transposed, 1)

        @block.vector
        def _(dve):
            for t in range(QT):
                for half in range(2):
                    n = 2 * t + half
                    dve.wait_ge(transposed, n + 1)
                    if t >= 3:
                        dve.wait_ge(stored[t % 3], 16 * (t // 3))
                    nc.vector.tensor_copy(rows[:, t % 3, 512 * half:512 * half + 512],
                                          tp[n % 4][:, :, :].rearrange("p a b -> p (a b)")).then_inc(copied, 1)

        @block.sync
        def _(sp):
            for t in range(QT):
                sp.wait_ge(copied, 2 * (t + 1))
                sp.dma_start(g.dram["out"][t * P:(t + 1) * P, :], rows[:, t % 3, :]).then_inc(stored[t % 3], 16)
            for i in range(3):
                sp.wait_ge(stored[i], 16 * len(range(i, QT, 3)))


class Shared:
    FFN1_GAIN, MIX_GAIN, FFN2_GAIN = 0, KD, 2 * KD
    EPS_COL, EPSQ_COL, BF_COL = 3 * KD, 3 * KD + 1, 3 * KD + 3
    FQ_COL, FK_COL, MQ_COL, MK_COL, CN_COL, BG_COL = [3 * KD + x for x in (4, 5, 6, 7, 8, 11)]

    def __init__(self):
        self.dram = {}


def build(nc, g):
    with ExitStack() as s:
        first_half = []

        def of_first_half(name):
            first_half.append(nc.alloc_semaphore(name))
            return first_half[-1]
        g.semaphore = of_first_half
        sb = lambda n, sh, dt=F32: s.enter_context(nc.sbuf_tensor(n, sh, dt))
        g.ident = sb("ident", [P, P])
        g.ones = sb("ones", [P, P])
        g.gains = sb("gains", [P, g.dram["gains"].shape[1]])
        g.u_hi = sb("u_hi", [P, KD, T], F32R)
        g.u_lo = sb("u_lo", [P, KD, T], F32R)
        with ExitStack() as mix:
            mb = lambda n, sh, dt=F32: mix.enter_context(nc.sbuf_tensor(n, sh, dt))
            g.ident_r = mb("ident_r", [P, P], F32R)
            g.masks = mb("masks", [P, 2 * P + META], F32R)
            g.head_sum = mb("head_sum", [P, P])
            g.rot = mb("rot", [P, P])
            with nc.sbuf_tensor("h_in", [P, KD, T], F32) as h:
                g.h = h
                load_phase(nc, g)
                norm_phase(nc, g, "n1", g.FFN1_GAIN, ALL_TOKENS)
                ffn_phase(nc, g, "f1", g.dram["ffn1"], ALL_TOKENS)
                norm_phase(nc, g, "n2", g.MIX_GAIN, ALL_TOKENS)
                forget_phase(nc, g)
            g.o_fox = mb("o_fox", [P, PAIRS, SEQ])
            attention_phase(nc, g, "fox", g.o_fox)
            nc.clear_and_free_semaphores(first_half)
            nc.all_engine_barrier()
            g.semaphore = lambda name: s.enter_context(nc.semaphore(name))
            g.o_mla = mb("o_mla", [P, PAIRS, SEQ])
            with ExitStack() as lat:
                lb = lambda n, sh, dt=F32: lat.enter_context(nc.sbuf_tensor(n, sh, dt))
                g.cq, g.ckv = lb("cq", [P, 2, T]), lb("ckv", [P, T])
                g.krope, g.ksq = lb("krope", [P, T]), lb("ksq", [P, T])
                g.cos, g.sin = lb("cos", [P, T]), lb("sin", [P, T])
                latent_phase(nc, g)
                attention_phase(nc, g, "mla", g.o_mla)
            gate_phase(nc, g)
        with nc.sbuf_tensor("h_out", [P, KD, T], F32) as h:
            g.h = h
            out_proj_phase(nc, g)
            norm_phase(nc, g, "n3", g.FFN2_GAIN, REAL_TOKENS)
            ffn_phase(nc, g, "f2", g.dram["ffn2"], REAL_TOKENS)
            store_phase(nc, g)


def _k_blocks(w):
    n = w.shape[1] // P
    return w.reshape(KD, P, n, P).transpose(2, 1, 0, 3).reshape(n, P, D)


def _ffn_blocks(w_gu, w_down):
    gate, up = _k_blocks(w_gu[:, :DFF]), _k_blocks(w_gu[:, DFF:])
    down = w_down.reshape(FT, P, D)
    gu = lambda i: [gate[2 * i], up[2 * i], gate[2 * i + 1], up[2 * i + 1]]
    dn = lambda i: [down[2 * i], down[2 * i + 1]]
    order = gu(0)
    for i in range(1, FT // 2):
        order += gu(i) + dn(i - 1)
    return np.stack(order + dn(FT // 2 - 1))


def _columns(v):
    return v.reshape(-1, P).T


def layout(i):
    a = {n: np.asarray(v) for n, v in i.items()}
    out = {"x": a["x"][0], "meta": a["meta_tokens"]}
    out["ffn1"] = _ffn_blocks(a["ffn1_w_gu"][0], a["ffn1_w_down"][0])
    out["ident"] = np.eye(P, dtype=np.float32)
    out["ones"] = np.ones((P, P), np.float32)
    w_in = a["w_in"][0]
    cuts = np.cumsum([FOX_D * HEADS] * 3 + [HEADS, CQ, CKV, ROPE, 2 * D])
    fq, fk, fv, fl, cq, ckv, kr, gates = np.split(w_in, cuts[:-1], axis=1)
    out["fox"] = np.stack([_k_blocks(w)[p] for p in range(PAIRS) for w in (fq, fk, fv)])
    shared = np.zeros((D, P), np.float32)
    shared[:, 0:HEADS] = fl
    shared[:, NOPE:MLA_D] = kr
    out["misc"] = np.concatenate([_k_blocks(shared), _k_blocks(ckv), _k_blocks(cq)])
    uq = a["mla_w_uq"][0].reshape(2, P, PAIRS, 2, MLA_D).transpose(2, 1, 3, 0, 4).reshape(PAIRS, P, 4 * MLA_D)
    ukv = a["mla_w_ukv"][0].reshape(P, PAIRS, 2, 2, NOPE).transpose(1, 0, 3, 2, 4).reshape(PAIRS, P, 4 * NOPE)
    out["mla"] = np.concatenate([uq, ukv], axis=2)
    branch = np.concatenate([a["w_branch_fox"][0], a["w_branch_mla"][0]])
    gate_blocks, branch_blocks = _k_blocks(gates), _k_blocks(branch)
    out["gate"] = np.stack([w for m in range(KD) for w in (gate_blocks[m], gate_blocks[KD + m], branch_blocks[m])])
    out["wout"] = _k_blocks(a["w_out"][0])
    out["ffn2"] = _ffn_blocks(a["ffn2_w_gu"][0], a["ffn2_w_down"][0])

    r, c = np.arange(P)[:, None], np.arange(P)[None, :]
    masks = np.zeros((P, 4 * P + META), np.float32)
    masks[:, 0:P] = np.where(r > c, NEG, 0)
    masks[:, P:2 * P] = np.where(c > r, NEG, 0)
    last = r - (P - META)
    masks[:, 2 * P:2 * P + META] = np.where((last < 0) | (last > c[:, :META]), NEG, 0)
    masks[:, 2 * P + META:3 * P + META] = (r // FOX_D == c // FOX_D)
    half = ROPE // 2
    for i in range(half):
        masks[NOPE + half + i, 3 * P + META + NOPE + i] = -1.0
        masks[NOPE + i, 3 * P + META + NOPE + half + i] = 1.0
    out["masks"] = masks
    freq = np.float32(10000.0) ** (-np.arange(0, ROPE, 2, dtype=np.float32) / np.float32(ROPE))
    angle = np.arange(T, dtype=np.float32)[None, :] * np.tile(freq, 2)[:, None]
    out["cos"], out["sin"] = np.cos(angle), np.sin(angle)

    def column(v):
        full = np.zeros((P, 1), np.float32)
        full[:len(v), 0] = v
        return full

    const = lambda x: np.full((P, 1), x, np.float32)
    out["gains"] = np.concatenate([
        _columns(a["ffn1_norm"][0]), _columns(a["mix_norm"][0]), _columns(a["ffn2_norm"][0]),
        const(EPS), const(FOX_D * EPS), const(MLA_D * EPS), column(a["b_forget"][0]),
        column(np.tile(a["fox_q_norm"][0], 2)), column(np.tile(a["fox_k_norm"][0], 2)),
        column(a["mla_q_norm"][0]), column(a["mla_k_norm"][0]),
        _columns(a["mla_ckv_norm"][0]), _columns(a["mla_cq_norm"][0]), _columns(a["b_gate"][0])], axis=1)
    return {n: np.ascontiguousarray(v, dtype=np.float32) for n, v in out.items()}


def kernel(**inputs):
    import concourse.bacc as bacc
    from concourse.bass_utils import run_bass_kernel_spmd
    arrays = layout(inputs)
    nc = bacc.Bacc("TRN2", target_bir_lowering=False, num_devices=1)
    g = Shared()
    for name, a in arrays.items():
        g.dram[name] = nc.dram_tensor(f"in_{name}", a.shape, mybir.dt.from_np(a.dtype), kind="ExternalInput").ap()
    for name, shape in (("hsave", (P, KD, T)), ("krope", (ROPE, T)), ("cum", (2, HEADS, T))):
        g.dram[name] = nc.dram_tensor(f"kept_{name}", shape, F32, kind="Internal").ap()
    g.dram["out"] = nc.dram_tensor("out", (SEQ, D), F32, kind="ExternalOutput").ap()
    build(nc, g)
    r = run_bass_kernel_spmd(nc, [{f"in_{n}": v for n, v in arrays.items()}], core_ids=[0])
    return np.asarray(r.results[0]["out"]).reshape(1, SEQ, D)
```

```python
from contextlib import ExitStack

import numpy as np

import concourse.bass as bass
from concourse import mybir

F32 = mybir.dt.float32
F32R = mybir.dt.float32r
ACT = mybir.ActivationFunctionType
ALU = mybir.AluOpType
AX_X = mybir.AxisListType.X

P = 128
D = 1024
KD = D // P
META = 16
SEQ = 1024
T = META + SEQ
QT = SEQ // P
DFF = 2816
FT = DFF // P
HEADS = 8
PAIRS = HEADS // 2
FOX_D = 64
NOPE, ROPE = 64, 32
MLA_D = NOPE + ROPE
VD = 64
CQ, CKV = 256, 128
EPS = 1e-6
NEG = -1.0e30
KEYS = 9 * P

ALL_TOKENS = [(0, 348), (348, 346), (694, 346)]
REAL_TOKENS = [(META, 512), (META + 512, 512)]


def mm3(nc, out, w_hi, w_lo, x_hi, x_lo, first, last):
    nc.tensor.matmul(out, w_hi, x_hi, start=first, stop=False)
    nc.tensor.matmul(out, w_lo, x_hi, start=False, stop=False)
    return nc.tensor.matmul(out, w_hi, x_lo, start=False, stop=last)


def load_phase(nc, g):
    with ExitStack() as s:
        sb = lambda n, sh, dt=F32: s.enter_context(nc.sbuf_tensor("ld_" + n, sh, dt))
        sem = lambda n: g.semaphore("ld_" + n)
        xin = sb("xin", [P, 3, D])
        metain = sb("metain", [META, D])
        tp = [s.enter_context(nc.psum_tensor(f"ld_tp{i}", [P, 4, P], F32)) for i in range(4)]
        x_in = [sem(f"x_in{i}") for i in range(3)]
        meta_in, transposed, copied, consts_in = sem("meta_in"), sem("transposed"), sem("copied"), sem("consts_in")
        block = s.enter_context(nc.Block())

        @block.sync
        def _(sp):
            sp.dma_start(g.ident[:, :], g.dram["ident"]).then_inc(consts_in, 16)
            sp.dma_start(metain[:, :], g.dram["meta"]).then_inc(meta_in, 16)
            for t in range(QT):
                if t >= 3:
                    sp.wait_ge(transposed, 2 * (t - 2))
                sp.dma_start(xin[:, t % 3, :], g.dram["x"][t * P:(t + 1) * P, :]).then_inc(x_in[t % 3], 16)
            sp.dma_start(g.gains[:, :], g.dram["gains"]).then_inc(consts_in, 16)
            sp.dma_start(g.ones[:, :], g.dram["ones"]).then_inc(consts_in, 16)
            sp.wait_ge(consts_in, 48)

        @block.tensor
        def _(pe):
            pe.wait_ge(consts_in, 16)
            for t in range(QT):
                pe.wait_ge(x_in[t % 3], 16 * (t // 3 + 1))
                for half in range(2):
                    n = 2 * t + half
                    if n >= 4:
                        pe.wait_ge(copied, n - 3)
                    for k in range(4):
                        kk = 4 * half + k
                        last = nc.tensor.transpose(tp[n % 4][:, k, :], xin[:, t % 3, kk * P:(kk + 1) * P],
                                                   g.ident[:, :])
                    last.then_inc(transposed, 1)
            pe.wait_ge(meta_in, 16)
            for half in range(2):
                n = 2 * QT + half
                pe.wait_ge(copied, n - 3)
                for k in range(4):
                    kk = 4 * half + k
                    last = nc.tensor.transpose(tp[n % 4][:, k, 0:META], metain[:, kk * P:(kk + 1) * P],
                                               g.ident[0:META, 0:META])
                last.then_inc(transposed, 1)

        @block.vector
        def _(dve):
            for t in range(QT):
                for half in range(2):
                    n = 2 * t + half
                    dve.wait_ge(transposed, n + 1)
                    nc.vector.tensor_copy(g.h[:, 4 * half:4 * half + 4, META + t * P:META + (t + 1) * P],
                                          tp[n % 4][:, :, :]).then_inc(copied, 1)
            for half in range(2):
                n = 2 * QT + half
                dve.wait_ge(transposed, n + 1)
                nc.vector.tensor_copy(g.h[:, 4 * half:4 * half + 4, 0:META],
                                      tp[n % 4][:, :, 0:META]).then_inc(copied, 1)


def norm_phase(nc, g, tag, gain_col, chunks):
    lo_t, hi_t = chunks[0][0], chunks[-1][0] + chunks[-1][1]
    n_tok = hi_t - lo_t
    with ExitStack() as s:
        sb = lambda n, sh, dt=F32: s.enter_context(nc.sbuf_tensor(f"{tag}_{n}", sh, dt))
        sem = lambda n: g.semaphore(f"{tag}_{n}")
        sq = sb("sq", [P, 2, T])
        rstd = sb("rstd", [P, T])
        u32 = sb("u32", [P, 4, 512])
        sums = [s.enter_context(nc.psum_tensor(f"{tag}_sums{i}", [P, 512], F32)) for i in range(len(chunks))]
        squared, summed, rooted, inverted = sem("squared"), sem("summed"), sem("rooted"), sem("inverted")
        u_done, hi_done, lo_done = sem("u_done"), sem("hi_done"), sem("lo_done")
        block = s.enter_context(nc.Block())
        units = [(c, k) for c in range(len(chunks)) for k in range(KD)]

        @block.scalar
        def _(act):
            for k in range(KD):
                if k >= 2:
                    act.wait_ge(summed, k - 1)
                nc.scalar.activation(sq[:, k % 2, 0:n_tok], g.h[:, k, lo_t:hi_t], ACT.Square).then_inc(squared, 1)
            act.wait_ge(summed, KD)
            for c, (t0, n) in enumerate(chunks):
                nc.scalar.activation(rstd[:, t0:t0 + n], sums[c][:, 0:n], ACT.Sqrt, scale=1.0 / D,
                                     bias=g.gains[:, g.EPS_COL:g.EPS_COL + 1]).then_inc(rooted, 1)
            for i, (c, k) in enumerate(units):
                t0, n = chunks[c]
                act.wait_ge(u_done, i + 1)
                nc.scalar.copy(g.u_hi[:, k, t0:t0 + n], u32[:, i % 4, 0:n]).then_inc(hi_done, 1)

        @block.tensor
        def _(pe):
            for k in range(KD):
                pe.wait_ge(squared, k + 1)
                for c, (t0, n) in enumerate(chunks):
                    last = nc.tensor.matmul(sums[c][:, 0:n], g.ones[:, :], sq[:, k % 2, t0 - lo_t:t0 - lo_t + n],
                                            start=(k == 0), stop=(k == KD - 1))
                last.then_inc(summed, 1)

        @block.vector
        def _(dve):
            for c, (t0, n) in enumerate(chunks):
                dve.wait_ge(rooted, c + 1)
                nc.vector.reciprocal(rstd[:, t0:t0 + n], rstd[:, t0:t0 + n]).then_inc(inverted, 1)
            for i, (c, k) in enumerate(units):
                t0, n = chunks[c]
                dve.wait_ge(inverted, c + 1)
                if i >= 4:
                    dve.wait_ge(lo_done, i - 3)
                nc.vector.scalar_tensor_tensor(u32[:, i % 4, 0:n], g.h[:, k, t0:t0 + n],
                                               g.gains[:, gain_col + k:gain_col + k + 1], rstd[:, t0:t0 + n],
                                               ALU.mult, ALU.mult).then_inc(u_done, 1)

        @block.gpsimd
        def _(pool):
            for i, (c, k) in enumerate(units):
                t0, n = chunks[c]
                pool.wait_ge(hi_done, i + 1)
                nc.gpsimd.tensor_tensor(g.u_lo[:, k, t0:t0 + n], u32[:, i % 4, 0:n],
                                        g.u_hi[:, k, t0:t0 + n].bitcast(F32), ALU.subtract).then_inc(lo_done, 1)


def ffn_phase(nc, g, tag, d_blocks, chunks):
    groups = FT // 2
    C = len(chunks)
    U = 2 * C
    V = KD * C
    n_blocks = 3 * FT
    with ExitStack() as s:
        sb = lambda n, sh, dt=F32: s.enter_context(nc.sbuf_tensor(f"{tag}_{n}", sh, dt))
        sem = lambda n: g.semaphore(f"{tag}_{n}")
        raw = sb("raw", [P, 3, D])
        w_hi = sb("w_hi", [P, 6, D], F32R)
        w_lo = sb("w_lo", [P, 6, D], F32R)
        hid_hi = sb("hid_hi", [P, 2, 2, T], F32R)
        hid_lo = sb("hid_lo", [P, 2, 2, T], F32R)
        silu = sb("silu", [P, 2, 512])
        h32 = sb("h32", [P, 512])
        bank = [s.enter_context(nc.psum_tensor(f"{tag}_bank{i}", [P, 512], F32)) for i in range(8)]
        raw_in = [sem(f"raw_in{i}") for i in range(3)]
        whi_done, wlo_done = sem("whi_done"), sem("wlo_done")
        gate_ready, up_ready, silu_done, h32_done = sem("gate_ready"), sem("up_ready"), sem("silu_done"), sem("h32_done")
        hid_hi_done, hid_done = sem("hid_hi_done"), sem("hid_done")
        down_ready, down_added = sem("down_ready"), sem("down_added")
        block = s.enter_context(nc.Block())

        @block.sync
        def _(sp):
            for n in range(3):
                sp.dma_start(raw[:, n, :], d_blocks[n]).then_inc(raw_in[n], 16)
            with sp.Fori(1, n_blocks // 3) as r:
                for n in range(3):
                    sp.wait_ge(wlo_done, 3 * r + (n - 2))
                    sp.dma_start(raw[:, n, :], d_blocks[3 * r + n]).then_inc(raw_in[n], 16)

        def gu_block(i, j):
            return j if isinstance(i, int) and i == 0 else 6 * i + (j - 2)

        def d_block(i, j):
            last = isinstance(i, int) and i == groups - 1
            return 6 * i + (j + 4 if last else j + 8)

        @block.scalar
        def _(act):
            def split_hi(n_rem, n, slot, times):
                act.wait_ge(raw_in[n_rem], 16 * times)
                nc.scalar.copy(w_hi[:, slot, :], raw[:, n_rem, :]).then_inc(whi_done, 1)

            def split_gu(i, f):
                act.wait_ge(up_ready, U * i + (C * (f + 1) - U))
                for j in (2 * f, 2 * f + 1):
                    split_hi((j - 2) % 3, None, j, 2 * i + ((j - 2) // 3 + 1))

            def split_d(i):
                if not (isinstance(i, int) and i == 0):
                    act.wait_ge(down_ready, V * i)
                last = isinstance(i, int) and i == groups - 1
                for j in range(2):
                    m = j + (4 if last else 8)
                    split_hi(m % 3, None, 4 + j, 2 * i + (m // 3 + 1))

            def group(i, more, parity_first=False):
                for f in range(2):
                    for c, (t0, n) in enumerate(chunks):
                        u = C * f + c
                        act.wait_ge(gate_ready, U * i + (u + 1))
                        if not (parity_first and u < 2):
                            act.wait_ge(h32_done, U * i + (u - 1))
                        nc.scalar.activation(silu[:, u % 2, 0:n], bank[2 * (u % 2)][:, 0:n],
                                             ACT.Silu).then_inc(silu_done, 1)
                    if more:
                        split_gu(i + 1, f)

            for j in range(4):
                split_hi(j % 3, j, j, j // 3 + 1)
            group(0, True, parity_first=True)
            split_d(0)
            group(1, True)
            with act.Fori(2, groups - 1) as i:
                split_d(i - 1)
                group(i, True)
            split_d(groups - 2)
            group(groups - 1, False)
            split_d(groups - 1)

        @block.gpsimd
        def _(pool):
            def split_lo(n, slot, raw_slot):
                pool.wait_ge(whi_done, n + 1)
                nc.gpsimd.tensor_tensor(w_lo[:, slot, :], raw[:, raw_slot, :], w_hi[:, slot, :].bitcast(F32),
                                        ALU.subtract).then_inc(wlo_done, 1)
            for n in range(4):
                split_lo(n, n, n % 3)
            with pool.Fori(1, groups) as i:
                for j in range(6):
                    split_lo(6 * i + (j - 2), j, (j - 2) % 3)
            for j in range(2):
                split_lo(n_blocks - 2 + j, 4 + j, (n_blocks - 2 + j) % 3)

        @block.tensor
        def _(pe):
            def gate_up(i, first=False):
                for f in range(2):
                    for c, (t0, n) in enumerate(chunks):
                        u = C * f + c
                        for which, ready, freed in ((0, gate_ready, silu_done), (1, up_ready, h32_done)):
                            slot = 2 * f + which
                            if c == 0:
                                pe.wait_ge(wlo_done, gu_block(i, slot) + 1)
                            if not (first and u < 2):
                                pe.wait_ge(freed, U * i + (u - 1))
                            out = bank[2 * (u % 2) + which]
                            for k in range(KD):
                                last = mm3(nc, out[:, 0:n], w_hi[:, slot, k * P:(k + 1) * P],
                                           w_lo[:, slot, k * P:(k + 1) * P], g.u_hi[:, k, t0:t0 + n],
                                           g.u_lo[:, k, t0:t0 + n], k == 0, k == KD - 1)
                            last.then_inc(ready, 1)

            def down(i, parity, first=False):
                pe.wait_ge(hid_done, U * i + U)
                pe.wait_ge(wlo_done, d_block(i, 1) + 1)
                for d in range(KD):
                    for c, (t0, n) in enumerate(chunks):
                        v = C * d + c
                        if not (first and v < 4):
                            pe.wait_ge(down_added, V * i + (v - 3))
                        for f in range(2):
                            last = mm3(nc, bank[4 + v % 4][:, 0:n], w_hi[:, 4 + f, d * P:(d + 1) * P],
                                       w_lo[:, 4 + f, d * P:(d + 1) * P], hid_hi[:, parity, f, t0:t0 + n],
                                       hid_lo[:, parity, f, t0:t0 + n], f == 0, f == 1)
                        last.then_inc(down_ready, 1)

            gate_up(0, first=True)
            gate_up(1)
            down(0, 0, first=True)
            with pe.Fori(2, groups - 1, 2) as i:
                gate_up(i)
                down(i - 1, 1)
                gate_up(i + 1)
                down(i, 0)
            gate_up(groups - 1)
            down(groups - 2, 1)
            down(groups - 1, 0)

        @block.vector
        def _(dve):
            def hidden(i, parity, first=False, reuse=True):
                if reuse:
                    dve.wait_ge(down_ready, V * (i - 1))
                for f in range(2):
                    for c, (t0, n) in enumerate(chunks):
                        u = C * f + c
                        dve.wait_ge(silu_done, U * i + (u + 1))
                        dve.wait_ge(up_ready, U * i + (u + 1))
                        if not (first and u == 0):
                            dve.wait_ge(hid_done, U * i + u)
                        nc.vector.tensor_tensor(h32[:, 0:n], silu[:, u % 2, 0:n], bank[2 * (u % 2) + 1][:, 0:n],
                                                ALU.mult).then_inc(h32_done, 1)
                        dve.wait_ge(h32_done, U * i + (u + 1))
                        nc.vector.tensor_copy(hid_hi[:, parity, f, t0:t0 + n], h32[:, 0:n]).then_inc(hid_hi_done, 1)
                        dve.wait_ge(hid_hi_done, U * i + (u + 1))
                        nc.vector.tensor_tensor(hid_lo[:, parity, f, t0:t0 + n], h32[:, 0:n],
                                                hid_hi[:, parity, f, t0:t0 + n].bitcast(F32),
                                                ALU.subtract).then_inc(hid_done, 1)

            def add_down(i, first=False):
                for d in range(KD):
                    for c, (t0, n) in enumerate(chunks):
                        v = C * d + c
                        dve.wait_ge(down_ready, V * i + (v + 1))
                        if not first:
                            dve.wait_ge(down_added, V * i + (v + 1 - V))
                        nc.vector.scalar_tensor_tensor(g.h[:, d, t0:t0 + n], bank[4 + v % 4][:, 0:n], 0.5,
                                                       g.h[:, d, t0:t0 + n], ALU.mult, ALU.add).then_inc(down_added, 1)

            hidden(0, 0, first=True, reuse=False)
            hidden(1, 1, reuse=False)
            add_down(0, first=True)
            with dve.Fori(2, groups - 1, 2) as i:
                hidden(i, 0)
                add_down(i - 1)
                hidden(i + 1, 1)
                add_down(i)
            hidden(groups - 1, 0)
            add_down(groups - 2)
            add_down(groups - 1)


def wait(eng, sem, p, per_pair, more):
    if isinstance(p, int):
        if per_pair * p + more > 0:
            eng.wait_ge(sem, per_pair * p + more)
    else:
        eng.wait_ge(sem, per_pair * p + more)


def over_pairs(eng, body):
    body(0)
    with eng.Fori(1, PAIRS - 1) as p:
        body(p)
    body(PAIRS - 1, last=True)


QK_TOKENS = [(0, 384), (384, 384), (768, 272)]
QK_TILES = [(0, 128, 256), (0, 128, 256), (0, 128, 144)]
LO_DVE = 4


def lo_counts(units_done):
    return units_done - units_done // LO_DVE, units_done // LO_DVE


ST_UNITS = []
for _c, (_q0, _n) in enumerate(REAL_TOKENS):
    for _kt in range(9):
        _a = max(_q0, P * _kt)
        if _a < _q0 + _n:
            ST_UNITS.append((_c, _kt, min(P * _kt, T - P), _a, _q0 + _n - _a))
NW = len(ST_UNITS)
LAST_OF = [max(w for w in range(NW) if ST_UNITS[w][0] == c) for c in range(2)]

MAX_UNITS = []
for _i in range(QT):
    _end = META + P * (_i + 1)
    _cuts = [0] + [x for x in (400, 912) if x < _end] + [_end]
    for _j in range(len(_cuts) - 1):
        MAX_UNITS.append((_i, _j, _cuts[_j], _cuts[_j + 1] - _cuts[_j]))
NM = len(MAX_UNITS)
SHORT = sum(1 for _u in MAX_UNITS if META + P * (_u[0] + 1) <= QK_TOKENS[2][0])


def forget_phase(nc, g):
    with ExitStack() as s:
        sb = lambda n, sh, dt=F32: s.enter_context(nc.sbuf_tensor("fg_" + n, sh, dt))
        sem = lambda n: g.semaphore("fg_" + n)
        raw = sb("raw", [P, D])
        w_hi, w_lo = sb("w_hi", [P, D], F32R), sb("w_lo", [P, D], F32R)
        cf = sb("cf", [P, 2 * P + META])
        out = sb("out", [P, T])
        mag, lse, zmin = sb("mag", [HEADS, T]), sb("lse", [HEADS, T]), sb("zmin", [HEADS, T])
        one, cum = sb("one", [HEADS, T]), sb("cum", [HEADS, T])
        c_hi, c_lo = sb("c_hi", [HEADS, T], F32R), sb("c_lo", [HEADS, T], F32R)
        acc = [s.enter_context(nc.psum_tensor(f"fg_acc{i}", [P, 512], F32)) for i in range(3)]
        h_out, w_in, const_in, spilled = sem("h_out"), sem("w_in"), sem("const_in"), sem("spilled")
        const_done, whi, wlo, ready, copied = sem("const_done"), sem("whi"), sem("wlo"), sem("ready"), sem("copied")
        step_a, step_v = sem("step_a"), sem("step_v")
        block = s.enter_context(nc.Block())

        @block.sync
        def _(sp):
            sp.dma_start(raw[:, :], g.dram["misc"][0]).then_inc(w_in, 16)
            sp.dma_start(cf[:, :], g.dram["masks"][:, 0:2 * P + META]).then_inc(const_in, 16)
            sp.dma_start(g.head_sum[:, :], g.dram["masks"][:, 2 * P + META:3 * P + META]).then_inc(const_in, 16)
            sp.dma_start(g.rot[:, :], g.dram["masks"][:, 3 * P + META:4 * P + META]).then_inc(const_in, 16)
            sp.dma_start(g.dram["hsave"], g.h[:, :, :]).then_inc(h_out, 16)
            sp.wait_ge(copied, 3)
            sp.dma_start(g.dram["krope"], out[NOPE:MLA_D, :]).then_inc(spilled, 16)
            sp.wait_ge(step_v, 6)
            sp.dma_start(g.dram["cum"][0], c_hi[:, :].bitcast(F32)).then_inc(spilled, 16)
            sp.dma_start(g.dram["cum"][1], c_lo[:, :].bitcast(F32)).then_inc(spilled, 16)
            sp.wait_ge(spilled, 48)
            sp.wait_ge(h_out, 16)

        @block.scalar
        def _(act):
            act.wait_ge(w_in, 16)
            nc.scalar.copy(w_hi[:, :], raw[:, :]).then_inc(whi, 1)
            act.wait_ge(const_in, 48)
            nc.scalar.copy(g.ident_r[:, :], g.ident[:, :]).then_inc(const_done, 1)
            nc.scalar.copy(g.masks[:, :], cf[:, :]).then_inc(const_done, 1)
            act.wait_ge(copied, 3)
            bias = g.gains[0:HEADS, g.BF_COL:g.BF_COL + 1]
            nc.scalar.activation(mag[:, :], out[0:HEADS, :], ACT.Abs, bias=bias).then_inc(step_a, 1)
            act.wait_ge(step_a, 1)
            nc.scalar.activation(mag[:, :], mag[:, :], ACT.Exp, scale=-1.0).then_inc(step_a, 1)
            act.wait_ge(step_a, 2)
            nc.scalar.activation(lse[:, :], mag[:, :], ACT.Ln, bias=g.ones[0:HEADS, 0:1]).then_inc(step_a, 1)

        @block.gpsimd
        def _(pool):
            pool.wait_ge(whi, 1)
            nc.gpsimd.tensor_tensor(w_lo[:, :], raw[:, :], w_hi[:, :].bitcast(F32), ALU.subtract).then_inc(wlo, 1)

        @block.tensor
        def _(pe):
            pe.wait_ge(wlo, 1)
            for c, (t0, n) in enumerate(ALL_TOKENS):
                for k in range(KD):
                    last = mm3(nc, acc[c][:, 0:n], w_hi[:, k * P:(k + 1) * P], w_lo[:, k * P:(k + 1) * P],
                               g.u_hi[:, k, t0:t0 + n], g.u_lo[:, k, t0:t0 + n], k == 0, k == KD - 1)
                last.then_inc(ready, 1)

        @block.vector
        def _(dve):
            nc.vector.memset(one[:, :], 1.0).then_inc(step_v, 1)
            for c, (t0, n) in enumerate(ALL_TOKENS):
                dve.wait_ge(ready, c + 1)
                nc.vector.tensor_copy(out[:, t0:t0 + n], acc[c][:, 0:n]).then_inc(copied, 1)
            dve.wait_ge(copied, 3)
            nc.vector.tensor_scalar(zmin[:, :], out[0:HEADS, :], g.gains[0:HEADS, g.BF_COL:g.BF_COL + 1], 0.0,
                                    ALU.add, ALU.min).then_inc(step_v, 1)
            dve.wait_ge(step_v, 2)
            dve.wait_ge(step_a, 3)
            nc.vector.tensor_tensor(zmin[:, :], lse[:, :], zmin[:, :], ALU.subtract).then_inc(step_v, 1)
            dve.wait_ge(step_v, 3)
            nc.vector.tensor_tensor_scan(cum[:, :], one[:, :], zmin[:, :], 0.0, ALU.mult, ALU.add).then_inc(step_v, 1)
            dve.wait_ge(step_v, 4)
            nc.vector.tensor_copy(c_hi[:, :], cum[:, :]).then_inc(step_v, 1)
            dve.wait_ge(step_v, 5)
            nc.vector.tensor_tensor(c_lo[:, :], cum[:, :], c_hi[:, :].bitcast(F32), ALU.subtract).then_inc(step_v, 1)


def latent_phase(nc, g):
    with ExitStack() as s:
        sb = lambda n, sh, dt=F32: s.enter_context(nc.sbuf_tensor("lt_" + n, sh, dt))
        sem = lambda n: g.semaphore("lt_" + n)
        raw = sb("raw", [P, 3, D])
        w_hi, w_lo = sb("w_hi", [P, 3, D], F32R), sb("w_lo", [P, 3, D], F32R)
        sq = sb("sq", [P, 2, 348])
        rs = sb("rs", [P, 2, 348])
        kr = sb("kr", [P, T])
        t1 = sb("t1", [P, 348])
        bank = [s.enter_context(nc.psum_tensor(f"lt_bank{i}", [P, 512], F32)) for i in range(6)]
        w_in = [sem(f"w_in{i}") for i in range(3)]
        const_in, whi, wlo = sem("const_in"), sem("whi"), sem("wlo")
        ready, squared, summed, logged, rooted, normed = (sem("ready"), sem("squared"), sem("summed"),
                                                          sem("logged"), sem("rooted"), sem("normed"))
        ksq_done = sem("ksq_done")
        kr_gained, kr_turned, kr_steps = sem("kr_gained"), sem("kr_turned"), sem("kr_steps")
        block = s.enter_context(nc.Block())
        C = ALL_TOKENS

        @block.sync
        def _(sp):
            for j in range(3):
                sp.dma_start(raw[:, j, :], g.dram["misc"][1 + j]).then_inc(w_in[j], 16)
            sp.dma_start(kr[NOPE:MLA_D, :], g.dram["krope"]).then_inc(const_in, 16)
            sp.dma_start(g.cos[NOPE:MLA_D, :], g.dram["cos"]).then_inc(const_in, 16)
            sp.dma_start(g.sin[NOPE:MLA_D, :], g.dram["sin"]).then_inc(const_in, 16)
            sp.wait_ge(const_in, 48)

        @block.gpsimd
        def _(pool):
            for j in range(3):
                pool.wait_ge(whi, j + 1)
                nc.gpsimd.tensor_tensor(w_lo[:, j, :], raw[:, j, :], w_hi[:, j, :].bitcast(F32),
                                        ALU.subtract).then_inc(wlo, 1)

        @block.tensor
        def _(pe):
            pe.wait_ge(kr_gained, 1)
            for c, (t0, n) in enumerate(C):
                nc.tensor.matmul(bank[c][0:MLA_D, 0:n], g.rot[NOPE:MLA_D, 0:MLA_D], kr[NOPE:MLA_D, t0:t0 + n],
                                 start=True, stop=True).then_inc(kr_turned, 1)
            for c, (t0, n) in enumerate(C):
                for j in range(3):
                    pe.wait_ge(wlo, j + 1)
                    if c == 0:
                        pe.wait_ge(kr_steps, 3 * (j + 1))
                    else:
                        pe.wait_ge(normed, 3 * (c - 1) + j + 1)
                    for k in range(KD):
                        last = mm3(nc, bank[j][:, 0:n], w_hi[:, j, k * P:(k + 1) * P],
                                   w_lo[:, j, k * P:(k + 1) * P], g.u_hi[:, k, t0:t0 + n],
                                   g.u_lo[:, k, t0:t0 + n], k == 0, k == KD - 1)
                    last.then_inc(ready, 1)
                for j in range(3):
                    pe.wait_ge(squared, 3 * c + j + 1)
                    if c and j < 2:
                        pe.wait_ge(logged, 2 * c - 1 + j)
                    dst = bank[3 if j == 0 else 4]
                    nc.tensor.matmul(dst[:, 0:n], g.ones[:, :], sq[:, (3 * c + j) % 2, 0:n], start=(j != 2),
                                     stop=(j != 1)).then_inc(summed, 1)

        @block.scalar
        def _(act):
            for j in range(3):
                act.wait_ge(w_in[j], 16)
                nc.scalar.copy(w_hi[:, j, :], raw[:, j, :]).then_inc(whi, 1)
            act.wait_ge(const_in, 48)
            nc.scalar.activation(g.ksq[NOPE:MLA_D, :], kr[NOPE:MLA_D, :], ACT.Square).then_inc(ksq_done, 1)
            for c, (t0, n) in enumerate(C):
                for j in range(3):
                    act.wait_ge(ready, 3 * c + j + 1)
                    if 3 * c + j >= 2:
                        act.wait_ge(summed, 3 * c + j - 1)
                    nc.scalar.activation(sq[:, (3 * c + j) % 2, 0:n], bank[j][:, 0:n], ACT.Square).then_inc(squared, 1)
                for r in range(2):
                    act.wait_ge(summed, 3 * c + (1 if r == 0 else 3))
                    if c:
                        act.wait_ge(normed, 3 * (c - 1) + (1 if r == 0 else 3))
                    nc.scalar.activation(rs[:, r, 0:n], bank[3 + r][:, 0:n], ACT.Ln,
                                         scale=1.0 / (CKV if r == 0 else CQ),
                                         bias=g.gains[:, g.EPS_COL:g.EPS_COL + 1]).then_inc(logged, 1)
                    act.wait_ge(logged, 2 * c + r + 1)
                    nc.scalar.activation(rs[:, r, 0:n], rs[:, r, 0:n], ACT.Exp, scale=-0.5).then_inc(rooted, 1)

        @block.vector
        def _(dve):
            dve.wait_ge(const_in, 48)
            dve.wait_ge(ksq_done, 1)
            gk = g.gains[NOPE:MLA_D, g.MK_COL:g.MK_COL + 1]
            nc.vector.tensor_scalar(kr[NOPE:MLA_D, :], kr[NOPE:MLA_D, :], gk, None, ALU.mult).then_inc(kr_gained, 1)
            dve.wait_ge(kr_gained, 1)
            for c, (t0, n) in enumerate(C):
                r = slice(NOPE, MLA_D)
                nc.vector.tensor_tensor(g.krope[r, t0:t0 + n], kr[r, t0:t0 + n], g.cos[r, t0:t0 + n],
                                        ALU.mult).then_inc(kr_steps, 1)
                dve.wait_ge(kr_turned, c + 1)
                nc.vector.tensor_tensor(t1[r, 0:n], bank[c][r, 0:n], g.sin[r, t0:t0 + n], ALU.mult).then_inc(kr_steps, 1)
                dve.wait_ge(kr_steps, 3 * c + 2)
                nc.vector.tensor_tensor(g.krope[r, t0:t0 + n], g.krope[r, t0:t0 + n], t1[r, 0:n],
                                        ALU.add).then_inc(kr_steps, 1)
                dve.wait_ge(kr_steps, 3 * c + 3)
            for c, (t0, n) in enumerate(C):
                for j in range(3):
                    dve.wait_ge(rooted, 2 * c + (1 if j == 0 else 2))
                    dst = g.ckv[:, t0:t0 + n] if j == 0 else g.cq[:, j - 1, t0:t0 + n]
                    nc.vector.scalar_tensor_tensor(dst, bank[j][:, 0:n],
                                                   g.gains[:, g.CN_COL + j:g.CN_COL + j + 1],
                                                   rs[:, 0 if j == 0 else 1, 0:n], ALU.mult, ALU.mult).then_inc(normed, 1)


def attention_phase(nc, g, kind, o_out):
    fox = kind == "fox"
    DK = FOX_D if fox else MLA_D
    CR = 2 if fox else 0
    KMAX, KALL = DK + CR, DK + CR + 2
    NU = 6 if fox else 12
    with ExitStack() as s:
        sb = lambda n, sh, dt=F32: s.enter_context(nc.sbuf_tensor(f"{kind}_{n}", sh, dt))
        sem = lambda n: g.semaphore(f"{kind}_{n}")
        q_hi = [sb(f"q_hi{i}", [KALL, T], F32R) for i in range(2)]
        q_lo = [sb(f"q_lo{i}", [DK, T], F32R) for i in range(2)]
        k_hi = [sb(f"k_hi{i}", [KALL, T], F32R) for i in range(2)]
        k_lo = [sb(f"k_lo{i}", [DK, T], F32R) for i in range(2)]
        v_hi, v_lo = sb("v_hi", [P, 9, 3 * VD], F32R), sb("v_lo", [P, 9, 3 * VD], F32R)
        p32 = sb("p32", [P, 2, 512])
        p_hi, p_lo = sb("p_hi", [P, 3, 512], F32R), sb("p_lo", [P, 3, 512], F32R)
        rs = sb("rs", [P, 2, 384])
        x32 = sb("x32", [P, 2, 384])
        rden = sb("rden", [P, 512])
        NH = 2 if fox else 1
        ms, r0, nt = sb("ms", [P, 2, 3 * NH]), sb("r0", [P, 2, 3 * NH]), sb("nt", [P, 2, 3 * NH])
        threes = sb("threes", [P, 3 * NH])
        mpart, nm = sb("mpart", [P, QT, 3]), sb("nm", [P, P])
        m_hi, m_lo = sb("m_hi", [QT, P], F32R), sb("m_lo", [QT, P], F32R)
        if fox:
            vt = sb("vt", [P, T])
            r_wide = sb("r_wide", [P, 2, 3 * NH, FOX_D])
            raw = sb("raw", [P, 3, D])
            w_hi, w_lo = sb("w_hi", [P, 3, D], F32R), sb("w_lo", [P, 3, D], F32R)
        else:
            w_pair = sb("w_pair", [P, 2 * 2 * MLA_D + 2 * P])
        bank = [s.enter_context(nc.psum_tensor(f"{kind}_bank{i}", [P, 512], F32)) for i in range(8)]
        PROJ, SUM, BC, TURN = (bank[0], bank[1], bank[4], bank[5]), bank[2], bank[6:8], bank[3]
        VB, MAXB, MT = bank[6:8], (bank[3], bank[0]), bank[1]
        ST, OB = (bank[2], bank[4], bank[5]), bank[6:8]

        ones_set = sem("ones_set")
        raw_in = [sem(f"raw_in{i}") for i in range(3)]
        whi_done, wlo_done = sem("whi_done"), sem("wlo_done")
        cum_in, m_in = sem("cum_in"), sem("m_in")
        proj_ready, squared, sum_ready, ms_done, logged, rooted, newton = (
            sem("proj_ready"), sem("squared"), sem("sum_ready"), sem("ms_done"), sem("logged"), sem("rooted"),
            sem("newton"))
        bc_ready, rs_done = sem("bc_ready"), sem("rs_done")
        x_done, x_turned, rope_steps, xhi_done, qk_done = (sem("x_done"), sem("x_turned"), sem("rope_steps"),
                                                           sem("xhi_done"), sem("qk_done"))
        vt_done, v_ready, vhi_done, v_done = sem("vt_done"), sem("v_ready"), sem("vhi_done"), sem("v_done")
        max_ready, max_read, nm_done, mt_ready, mhi_done, m_done = (sem("max_ready"), sem("max_read"),
                                                                    sem("nm_done"), sem("mt_ready"),
                                                                    sem("mhi_done"), sem("m_done"))
        st_ready, exp_done, phi_done, plo_pool, plo_dve, pv_done = (sem("st_ready"), sem("exp_done"),
                                                                    sem("phi_done"), sem("plo_pool"),
                                                                    sem("plo_dve"), sem("pv_done"))
        ln_done, rden_done, o_done = sem("ln_done"), sem("rden_done"), sem("o_done")
        block = s.enter_context(nc.Block())
        PW, PM = 2 * NW, 2 * NM
        LO_P, LO_V = lo_counts(PW)

        def wait_split(eng, p, units_done):
            by_pool, by_dve = lo_counts(units_done) if units_done > 0 else (0, 0)
            wait(eng, plo_pool, p, LO_P, by_pool)
            wait(eng, plo_dve, p, LO_V, by_dve)

        W_HI_AT, W_LO_AT = [2, 5, 8, 11, 14, 17], [4, 7, 10, 13, 16, 19]
        if fox:
            units = [(is_q, None, c) for c in range(3) for is_q in (True, False)]
        else:
            units = [(is_q, h, c) for h in range(2) for c in range(3) for is_q in (True, False)]
        NPROJ = NU + 3 if fox else NU
        EARLY = 6
        finish_after = {}
        for h in range(2):
            for c in range(2):
                finish_after.setdefault(min(NW * h + LAST_OF[c] + 4, PW - 1), []).append((h, c))

        V_PROJ = (bank[4], bank[5], bank[4])

        def v_columns(v, b):
            return v[:, 3 * b:3 * b + 3, :].rearrange("p t (a b) -> p t a b", a=3)[:, :, 0:3:2, :]

        def v_turned(b):
            return VB[b % 2][:, 0:3 * P].rearrange("p (t a b) -> p t a b", t=3, a=2)

        @block.sync
        def _(sp):
            sp.wait_ge(ones_set, 1)

            def weights(p):
                if fox:
                    for j in range(3):
                        wait(sp, wlo_done, p, 6, 2 * j - 4)
                        sp.dma_start(raw[:, j, :], g.dram["fox"][3 * p + j]).then_inc(raw_in[j], 16)
                else:
                    wait(sp, v_ready, p, 3, 0)
                    sp.dma_start(w_pair[:, :], g.dram["mla"][p]).then_inc(raw_in[0], 16)

            def pair(p, last=False):
                if fox:
                    for h in range(2):
                        wait(sp, pv_done, p, PW, 0)
                        sp.dma_start(k_hi[h][DK:DK + 2, :].bitcast(F32),
                                     g.dram["cum"][:, 2 * p + h, :]).then_inc(cum_in, 16)
                if not last:
                    weights(p + 1)
                for h in range(2):
                    wait(sp, m_done, p, 2, h + 1)
                    for src, r in ((m_hi, KMAX), (m_lo, KMAX + 1)):
                        sp.dma_start(q_hi[h][r:r + 1, META:T].bitcast(F32).rearrange("o (a b) -> o a b", a=QT),
                                     src[:, :].bitcast(F32)).then_inc(m_in, 16)
            weights(0)
            over_pairs(sp, pair)

        @block.gpsimd
        def _(pool):
            pool.wait_ge(ones_set, 1)

            def pair(p, last=False):
                for u in range(NU):
                    r, m, t = r0[:, u % 2, :], ms[:, u % 2, :], nt[:, u % 2, :]
                    wait(pool, rooted, p, NU, u + 1)
                    nc.gpsimd.tensor_tensor(t, m, r, ALU.mult).then_inc(newton, 1)
                    wait(pool, newton, p, 4 * NU, 4 * u + 1)
                    nc.gpsimd.tensor_tensor(t, t, r, ALU.mult).then_inc(newton, 1)
                    wait(pool, newton, p, 4 * NU, 4 * u + 2)
                    nc.gpsimd.tensor_tensor(t, threes[:, :], t, ALU.subtract).then_inc(newton, 1)
                    wait(pool, newton, p, 4 * NU, 4 * u + 3)
                    if fox:
                        wait(pool, bc_ready, p, NU, u - 1)
                        wide = [P, 3 * NH, FOX_D]
                        nc.gpsimd.tensor_tensor(r_wide[:, u % 2], r.unsqueeze(2).broadcast_to(wide),
                                                t.unsqueeze(2).broadcast_to(wide), ALU.mult).then_inc(newton, 1)
                    else:
                        nc.gpsimd.tensor_tensor(r, r, t, ALU.mult).then_inc(newton, 1)
                for w in range(PW):
                    if w % LO_DVE == LO_DVE - 1:
                        continue
                    n = ST_UNITS[w % NW][4]
                    wait(pool, phi_done, p, PW, w + 1)
                    nc.gpsimd.tensor_tensor(p_lo[:, w % 3, 0:n], p32[:, w % 2, 0:n], p_hi[:, w % 3, 0:n].bitcast(F32),
                                            ALU.subtract).then_inc(plo_pool, 1)
            over_pairs(pool, pair)

        @block.scalar
        def _(act):
            def weights_hi(p, i):
                j, x = i // 2, slice(512 * (i % 2), 512 * (i % 2) + 512)
                act.wait_ge(raw_in[j], 16 * (p + 1))
                wait(act, proj_ready, p, NPROJ, 0)
                nc.scalar.copy(w_hi[:, j, x], raw[:, j, x]).then_inc(whi_done, 1)

            def pair(p, last=False):
                def evacuate_v(c):
                    t0, n = QK_TOKENS[c]
                    wait(act, proj_ready, p, NPROJ, NU + c + 1)
                    wait(act, v_ready, p, 3, 0)
                    nc.scalar.copy(vt[:, t0:t0 + n], V_PROJ[c][:, 0:n]).then_inc(vt_done, 1)

                for s_ in range(NU + 2):
                    u = s_
                    if u < NU:
                        is_q, h, c = units[u]
                        t0, n = QK_TOKENS[c]
                        src = PROJ[u % 4]
                        wait(act, proj_ready, p, NPROJ, u + 1)
                        wait(act, sum_ready, p, NU, u - 1)
                        if u < 2:
                            wait_split(act, p, 0)
                        if fox or is_q:
                            R = P if fox else DK
                            nc.scalar.activation(p32[0:R, u % 2, 0:n], src[0:R, 0:n], ACT.Square).then_inc(squared, 1)
                        else:
                            nc.scalar.activation(g.ksq[0:NOPE, t0:t0 + n], src[0:NOPE, 0:n],
                                                 ACT.Square).then_inc(squared, 1)
                    u = s_ - 1
                    if 0 <= u < NU:
                        wait(act, ms_done, p, NU, u + 1)
                        wait(act, bc_ready, p, NU, u - 1)
                        nc.scalar.activation(r0[:, u % 2, :], ms[:, u % 2, :], ACT.Ln).then_inc(logged, 1)
                        wait(act, logged, p, NU, u + 1)
                        nc.scalar.activation(r0[:, u % 2, :], r0[:, u % 2, :], ACT.Exp, scale=-0.5).then_inc(rooted, 1)
                    u = s_ - 2
                    if u >= 0:
                        n, R = QK_TOKENS[units[u][2]][1], (P if fox else DK)
                        wait(act, bc_ready, p, NU, u + 1)
                        wait(act, x_done, p, NU, u - 1)
                        nc.scalar.copy(rs[0:R, u % 2, 0:n], BC[u % 2][0:R, 0:n]).then_inc(rs_done, 1)
                    if fox and s_ == NU:
                        evacuate_v(0)
                if fox:
                    evacuate_v(1)
                    evacuate_v(2)
                for b in range(3):
                    wait(act, v_ready, p, 3, b + 1)
                    nc.scalar.copy(v_columns(v_hi, b), v_turned(b)).then_inc(vhi_done, 1)

                for w in range(PW):
                    n = ST_UNITS[w % NW][4]
                    wait(act, st_ready, p, PW, w + 1)
                    wait_split(act, p, w - 1)
                    nc.scalar.activation(p32[:, w % 2, 0:n], ST[w % 3][:, 0:n], ACT.Exp).then_inc(exp_done, 1)
                    for h, c in finish_after.get(w, ()):
                        rows, ones_rows = (slice(0, VD), slice(VD, P))[::1 if h == 0 else -1]
                        f = 2 * h + c
                        wait(act, pv_done, p, PW, NW * h + LAST_OF[c] + 1)
                        wait(act, o_done, p, 4, f)
                        nc.scalar.activation(rden[rows, :], OB[c][ones_rows, :], ACT.Ln).then_inc(ln_done, 1)
                        wait(act, ln_done, p, 4, f + 1)
                        nc.scalar.activation(rden[rows, :], rden[rows, :], ACT.Exp, scale=-1.0).then_inc(rden_done, 1)
                    if fox and not last and w in W_HI_AT:
                        weights_hi(p + 1, W_HI_AT.index(w))
            act.preload_act_table_set("natural_log_exp_and_others")
            act.wait_ge(ones_set, 1)
            if fox:
                for i in range(6):
                    weights_hi(0, i)
            over_pairs(act, pair)

        @block.tensor
        def _(pe):
            pe.wait_ge(ones_set, 1)

            def pair(p, last=False):
                def products(u, between=None):
                    is_q, h, c = units[u] if u < NU else (None, None, u - NU)
                    t0, n = QK_TOKENS[c]
                    out = PROJ[u % 4] if u < NU else V_PROJ[c]
                    if u == 0:
                        wait(pe, max_read, p, PM, 0)
                    elif u == 1:
                        wait(pe, m_done, p, 2, 0)
                    elif u < 4:
                        wait(pe, exp_done, p, PW, 0)
                    elif u < NU + 2:
                        wait(pe, x_done, p, NU, u - 3)
                    else:
                        wait(pe, vt_done, p, 3, 1)
                    if fox:
                        j = 2 if u >= NU else 0 if is_q else 1
                        if c == 0:
                            wait(pe, wlo_done, p, 6, 2 * j + 2)
                        for k in range(KD):
                            last = mm3(nc, out[:, 0:n], w_hi[:, j, k * P:(k + 1) * P], w_lo[:, j, k * P:(k + 1) * P],
                                       g.u_hi[:, k, t0:t0 + n], g.u_lo[:, k, t0:t0 + n], k == 0, k == KD - 1)
                            if k == KD - 1:
                                last.then_inc(proj_ready, 1)
                            if between:
                                between(u - NU, k)
                        return
                    if is_q:
                        pe.wait_ge(raw_in[0], 16 * (p + 1))
                        for k in range(2):
                            col = (2 * h + k) * MLA_D
                            last = nc.tensor.matmul(out[0:MLA_D, 0:n], w_pair[:, col:col + MLA_D],
                                                    g.cq[:, k, t0:t0 + n], start=(k == 0), stop=(k == 1))
                    else:
                        col = 4 * MLA_D + NOPE * h
                        last = nc.tensor.matmul(out[0:NOPE, 0:n], w_pair[:, col:col + NOPE], g.ckv[:, t0:t0 + n],
                                                start=True, stop=True)
                    last.then_inc(proj_ready, 1)

                def sums(u):
                    is_q, h, c = units[u]
                    t0, n = QK_TOKENS[c]
                    wait(pe, squared, p, NU, u + 1)
                    wait(pe, ms_done, p, NU, u)
                    if u == 0:
                        wait(pe, exp_done, p, PW, 0)
                    R = P if fox else DK
                    src = p32[0:R, u % 2, 0:n] if fox or is_q else g.ksq[0:R, t0:t0 + n]
                    per_head = g.head_sum[:, 0:P:FOX_D] if fox else g.ones[0:R, 0:1]
                    for i, off in enumerate(QK_TILES[c]):
                        last = nc.tensor.matmul(SUM[:, NH * i:NH * i + NH], src[:, off:off + P], per_head,
                                                start=True, stop=True)
                    last.then_inc(sum_ready, 1)

                def broadcast(u):
                    c = units[u][2]
                    wait(pe, newton, p, 4 * NU, 4 * u + 4)
                    if u < 2:
                        wait(pe, o_done, p, 4, 0)
                    else:
                        wait(pe, rs_done, p, NU, u - 1)
                    R = P if fox else DK
                    for i, off in enumerate(QK_TILES[c]):
                        if fox:
                            r = r_wide[:, u % 2, NH * i:NH * i + NH, :].rearrange("p a b -> p (a b)")
                        else:
                            r = r0[:, u % 2, i:i + 1].broadcast_to([P, R])
                        last = nc.tensor.matmul(BC[u % 2][0:R, off:off + P], r, g.ident[:, :], start=True, stop=True)
                    last.then_inc(bc_ready, 1)

                def turn(u):
                    t0, n = QK_TOKENS[units[u][2]]
                    q_count = sum(1 for x in units[:u + 1] if x[0])
                    wait(pe, x_done, p, NU, u + 1)
                    wait(pe, rope_steps, p, 18, 3 * (q_count - 1))
                    nc.tensor.matmul(TURN[0:DK, 0:n], g.rot[NOPE:DK, 0:DK], x32[NOPE:DK, u % 2, 0:n],
                                     start=True, stop=True).then_inc(x_turned, 1)

                def values(b):
                    if b < 2:
                        wait(pe, rs_done, p, NU, NU)
                    else:
                        wait(pe, v_done, p, 3, b - 1)
                    if fox:
                        wait(pe, vt_done, p, 3, b + 1)
                    for i in range(3):
                        tok = min(P * (3 * b + i), T - P)
                        out = VB[b % 2][:, P * i:P * i + P]
                        if fox:
                            last = nc.tensor.transpose(out, vt[:, tok:tok + P], g.ident[:, :])
                        else:
                            last = nc.tensor.matmul(out, g.ckv[:, tok:tok + P],
                                                    w_pair[:, 4 * MLA_D + P:4 * MLA_D + 2 * P], start=True, stop=True)
                    last.then_inc(v_ready, 1)

                def maxima(h, x):
                    i, part, k0, n = MAX_UNITS[x]
                    y = NM * h + x
                    out = MAXB[y % 2]
                    if y == 0:
                        wait(pe, qk_done, p, NU, NU - 2 if fox else NU)
                        if fox:
                            wait(pe, x_done, p, NU, NU - 1)
                            pe.wait_ge(cum_in, 32 * (p + 1))
                    if fox and x == SHORT and h == 0:
                        wait(pe, qk_done, p, NU, NU)
                    wait(pe, max_read, p, PM, y - 1)
                    q0 = META + P * i
                    diagonal = k0 + n == q0 + P
                    last = nc.tensor.matmul(out[:, 0:n], q_hi[h][0:KMAX, q0:q0 + P], k_hi[h][0:KMAX, k0:k0 + n],
                                            start=True, stop=not diagonal)
                    if diagonal:
                        last = nc.tensor.matmul(out[:, n - P:n], g.ident_r[:, :], g.masks[:, P:2 * P],
                                                start=False, stop=True)
                    last.then_inc(max_ready, 1)

                def turn_maxima(h):
                    wait(pe, nm_done, p, 2, h + 1)
                    wait(pe, m_done, p, 2, h)
                    nc.tensor.transpose(MT[:, 0:P], nm[:, :], g.ident[:, :]).then_inc(mt_ready, 1)

                def scores(w):
                    h, (c, kt, k0, q0, n) = w // NW, ST_UNITS[w % NW]
                    out = ST[w % 3]
                    wait(pe, exp_done, p, PW, w - 2 if w >= 3 else 0)
                    if w % NW == 0:
                        pe.wait_ge(m_in, 64 * p + 32 * (h + 1))
                    kh, kl = k_hi[h][:, k0:k0 + P], k_lo[h][:, k0:k0 + P]
                    nc.tensor.matmul(out[:, 0:n], kh[0:KALL], q_hi[h][0:KALL, q0:q0 + n], start=True, stop=False)
                    nc.tensor.matmul(out[:, 0:n], kl[0:DK], q_hi[h][0:DK, q0:q0 + n], start=False, stop=False)
                    d0, d1 = max(q0, P * kt), min(q0 + n, P * kt + P)
                    diagonal = d0 < d1
                    last = nc.tensor.matmul(out[:, 0:n], kh[0:DK], q_lo[h][0:DK, q0:q0 + n], start=False,
                                            stop=not diagonal)
                    if diagonal:
                        m0 = 2 * P if kt == 8 else d0 - P * kt
                        last = nc.tensor.matmul(out[:, d0 - q0:d1 - q0], g.ident_r[:, :],
                                                g.masks[:, m0:m0 + d1 - d0], start=False, stop=True)
                    last.then_inc(st_ready, 1)

                def weigh(w):
                    h, (c, kt, k0, q0, n) = w // NW, ST_UNITS[w % NW]
                    cq0 = REAL_TOKENS[c][0]
                    out = OB[c][:, q0 - cq0:q0 - cq0 + n]
                    wait_split(pe, p, w + 1)
                    if kt == 0:
                        wait(pe, o_done, p, 4, 2 * h + c - 1)
                        if w == 0:
                            wait(pe, v_done, p, 3, 3)
                    cols = slice(VD * h, VD * h + P)
                    last_of = w % NW == LAST_OF[c]
                    nc.tensor.matmul(out, v_hi[:, kt, cols], p_hi[:, w % 3, 0:n], start=(kt == 0), stop=False)
                    nc.tensor.matmul(out, v_lo[:, kt, cols], p_hi[:, w % 3, 0:n], start=False, stop=False)
                    nc.tensor.matmul(out, v_hi[:, kt, cols], p_lo[:, w % 3, 0:n], start=False,
                                     stop=last_of).then_inc(pv_done, 1)

                def between(c, k):
                    if (c, k) == (0, 1):
                        broadcast(NU - 2)
                    elif (c, k) == (0, 2):
                        sums(NU - 1)
                    elif (c, k) == (1, 1):
                        broadcast(NU - 1)
                    x = {0: k - 6, 1: k + 2, 2: 8 + k}[c]
                    if c == 1 and x >= SHORT:
                        x = SHORT if k == KD - 1 else -1
                    if 0 <= x < NM:
                        maxima(0, x)

                for step in range(NU if fox else NU + 3):
                    if step < NU:
                        products(step)
                    if 1 <= step <= NU:
                        sums(step - 1)
                    if 2 <= step <= NU + 1:
                        broadcast(step - 2)
                    if step >= 3 and not fox and units[step - 3][0]:
                        turn(step - 3)
                if fox:
                    for c in range(3):
                        products(NU + c, between)
                    values(0)
                    values(1)
                else:
                    for x in range(NM):
                        if x % 7 == 0:
                            values(x // 7)
                        maxima(0, x)
                turn_maxima(0)
                values(2)
                for x in range(EARLY):
                    maxima(1, x)
                for w in range(PW):
                    scores(w)
                    if w < NM - EARLY:
                        maxima(1, EARLY + w)
                    if w == NM - EARLY + 1:
                        turn_maxima(1)
                    if w >= 3:
                        weigh(w - 3)
                for w in range(PW - 3, PW):
                    weigh(w)
            over_pairs(pe, pair)

        @block.vector
        def _(dve):
            for h in range(2):
                nc.vector.memset(q_hi[h][DK:KALL, :].bitcast(F32), 1.0)
                nc.vector.memset(k_hi[h][DK:KALL, :].bitcast(F32), 1.0)
            nc.vector.memset(v_lo[:, :, VD:2 * VD].bitcast(F32), 0.0)
            nc.vector.memset(nm[:, :], 0.0)
            nc.vector.memset(threes[:, :], 3.0)
            nc.vector.memset(mpart[:, :, :], NEG)
            nc.vector.memset(v_hi[:, :, VD:2 * VD].bitcast(F32), 1.0).then_inc(ones_set, 1)
            dve.wait_ge(ones_set, 1)

            def weights_lo(p, i):
                j, x = i // 2, slice(512 * (i % 2), 512 * (i % 2) + 512)
                wait(dve, whi_done, p, 6, i + 1)
                nc.vector.tensor_tensor(w_lo[:, j, x], raw[:, j, x], w_hi[:, j, x].bitcast(F32),
                                        ALU.subtract).then_inc(wlo_done, 1)

            def pair(p, last=False):
                def mean_squares(u):
                    is_q = units[u][0]
                    wait(dve, sum_ready, p, NU, u + 1)
                    wait(dve, newton, p, 4 * NU, 4 * u - 4)
                    nc.vector.tensor_scalar(ms[:, u % 2, :], SUM[:, 0:3 * NH], 4.0 if is_q else 4.0 / DK,
                                            4 * DK * EPS if is_q else 4 * EPS, ALU.mult, ALU.add).then_inc(ms_done, 1)

                def qk(u):
                    is_q, h, c = units[u]
                    t0, n = QK_TOKENS[c]
                    hi, lo = (q_hi, q_lo) if is_q else (k_hi, k_lo)
                    src = PROJ[u % 4]
                    wait(dve, rs_done, p, NU, u + 1)
                    wait(dve, pv_done, p, PW, 0)
                    if fox:
                        col = g.FQ_COL if is_q else g.FK_COL
                        for j in range(2):
                            r = slice(FOX_D * j, FOX_D * (j + 1))
                            if j == 0:
                                wait(dve, qk_done, p, NU, u)
                            last = nc.vector.scalar_tensor_tensor(x32[0:FOX_D, j, 0:n], src[r, 0:n],
                                                                  g.gains[r, col:col + 1], rs[r, u % 2, 0:n],
                                                                  ALU.mult, ALU.mult)
                        last.then_inc(x_done, 1)
                        wait(dve, x_done, p, NU, u + 1)
                        for j in range(2):
                            last = nc.vector.tensor_copy(hi[j][0:FOX_D, t0:t0 + n], x32[0:FOX_D, j, 0:n])
                        last.then_inc(xhi_done, 1)
                        wait(dve, xhi_done, p, NU, u + 1)
                        for j in range(2):
                            last = nc.vector.tensor_tensor(lo[j][0:FOX_D, t0:t0 + n], x32[0:FOX_D, j, 0:n],
                                                           hi[j][0:FOX_D, t0:t0 + n].bitcast(F32), ALU.subtract)
                        last.then_inc(qk_done, 1)
                        return
                    x = x32[:, u % 2, 0:n]
                    rope = slice(NOPE, MLA_D)
                    wait(dve, qk_done, p, NU, u - 1)
                    if is_q:
                        nc.vector.scalar_tensor_tensor(x[0:DK], src[0:DK, 0:n], g.gains[0:DK, g.MQ_COL:g.MQ_COL + 1],
                                                       rs[0:DK, u % 2, 0:n], ALU.mult, ALU.mult).then_inc(x_done, 1)
                    else:
                        nc.vector.tensor_tensor(x[rope], g.krope[rope, t0:t0 + n], rs[rope, u % 2, 0:n], ALU.mult)
                        nc.vector.scalar_tensor_tensor(x[0:NOPE], src[0:NOPE, 0:n],
                                                       g.gains[0:NOPE, g.MK_COL:g.MK_COL + 1],
                                                       rs[0:NOPE, u % 2, 0:n], ALU.mult, ALU.mult).then_inc(x_done, 1)

                def split(u):
                    is_q, h, c = units[u]
                    t0, n = QK_TOKENS[c]
                    hi, lo = (q_hi, q_lo) if is_q else (k_hi, k_lo)
                    x = x32[:, u % 2, 0:n]
                    rope = slice(NOPE, MLA_D)
                    if is_q:
                        q_count = sum(1 for y in units[:u + 1] if y[0])
                        wait(dve, x_turned, p, 6, q_count)
                        wait(dve, x_done, p, NU, u + 1)
                        nc.vector.tensor_tensor(x[rope], x[rope], g.cos[rope, t0:t0 + n],
                                                ALU.mult).then_inc(rope_steps, 1)
                        nc.vector.tensor_tensor(rden[rope, 0:n], TURN[rope, 0:n], g.sin[rope, t0:t0 + n],
                                                ALU.mult).then_inc(rope_steps, 1)
                        wait(dve, rope_steps, p, 18, 3 * q_count - 1)
                        nc.vector.tensor_tensor(x[rope], x[rope], rden[rope, 0:n], ALU.add).then_inc(rope_steps, 1)
                        wait(dve, rope_steps, p, 18, 3 * q_count)
                    else:
                        wait(dve, x_done, p, NU, u + 1)
                    nc.vector.tensor_copy(hi[h][0:DK, t0:t0 + n], x[0:DK]).then_inc(xhi_done, 1)
                    wait(dve, xhi_done, p, NU, u + 1)
                    nc.vector.tensor_tensor(lo[h][0:DK, t0:t0 + n], x[0:DK], hi[h][0:DK, t0:t0 + n].bitcast(F32),
                                            ALU.subtract).then_inc(qk_done, 1)

                def values(b):
                    wait(dve, vhi_done, p, 3, b + 1)
                    nc.vector.tensor_tensor(v_columns(v_lo, b), v_turned(b), v_columns(v_hi, b).bitcast(F32),
                                            ALU.subtract).then_inc(v_done, 1)

                def maxima(h, x):
                    i, part, k0, n = MAX_UNITS[x]
                    wait(dve, max_ready, p, PM, NM * h + x + 1)
                    if x == 0:
                        wait(dve, nm_done, p, 2, h)
                    nc.vector.tensor_reduce(mpart[:, i, part:part + 1], MAXB[(NM * h + x) % 2][:, 0:n], AX_X,
                                            ALU.max).then_inc(max_read, 1)

                def join_maxima(h):
                    wait(dve, max_read, p, PM, NM * (h + 1))
                    wait(dve, mt_ready, p, 2, h)
                    nc.vector.tensor_reduce(nm[:, 0:QT], mpart[:, :, :], AX_X, ALU.max, negate=True).then_inc(nm_done, 1)

                def split_maxima(h):
                    wait(dve, mt_ready, p, 2, h + 1)
                    wait(dve, m_in, p, 64, 32 * h)
                    nc.vector.tensor_copy(m_hi[:, :], MT[0:QT, 0:P]).then_inc(mhi_done, 1)
                    wait(dve, mhi_done, p, 2, h + 1)
                    nc.vector.tensor_tensor(m_lo[:, :], MT[0:QT, 0:P], m_hi[:, :].bitcast(F32),
                                            ALU.subtract).then_inc(m_done, 1)

                for step in range(1, NU + 3):
                    if step <= NU:
                        mean_squares(step - 1)
                    if fox and step == NU + 1:
                        for x in range(SHORT - 3):
                            maxima(0, x)
                    if 2 <= step <= NU + 1:
                        qk(step - 2)
                    if step >= 3 and not fox:
                        split(step - 3)
                for x in range(SHORT - 3 if fox else 0, NM):
                    if not fox and x % 7 == 0:
                        values(x // 7)
                    maxima(0, x)
                join_maxima(0)
                split_maxima(0)
                for b in range(0 if fox else 2, 3):
                    values(b)
                for x in range(EARLY):
                    maxima(1, x)
                for w in range(PW):
                    n = ST_UNITS[w % NW][4]
                    if w < NM - EARLY:
                        maxima(1, EARLY + w)
                    if w == NM - EARLY:
                        join_maxima(1)
                    wait(dve, exp_done, p, PW, w + 1)
                    wait(dve, pv_done, p, PW, w - 2 if w >= 3 else 0)
                    nc.vector.tensor_copy(p_hi[:, w % 3, 0:n], p32[:, w % 2, 0:n]).then_inc(phi_done, 1)
                    if w % LO_DVE == LO_DVE - 1:
                        wait(dve, phi_done, p, PW, w + 1)
                        nc.vector.tensor_tensor(p_lo[:, w % 3, 0:n], p32[:, w % 2, 0:n],
                                                p_hi[:, w % 3, 0:n].bitcast(F32), ALU.subtract).then_inc(plo_dve, 1)
                    if w == NM - EARLY + 1:
                        split_maxima(1)
                    for h, c in finish_after.get(w, ()):
                        rows = slice(VD * h, VD * h + VD)
                        q0 = REAL_TOKENS[c][0] - META
                        wait(dve, rden_done, p, 4, 2 * h + c + 1)
                        nc.vector.tensor_tensor(o_out[rows, p, q0:q0 + 512], OB[c][rows, :], rden[rows, :],
                                                ALU.mult).then_inc(o_done, 1)
                    if fox and not last and w in W_LO_AT:
                        weights_lo(p + 1, W_LO_AT.index(w))
            if fox:
                for i in range(6):
                    weights_lo(0, i)
            over_pairs(dve, pair)


def latent_attention_phase(nc, g):
    DK = MLA_D
    KALL = DK + 2
    NU = 6
    units = [(is_q, c) for c in range(3) for is_q in (True, False)]
    V_TILES = (range(0, 5), range(5, 9))
    MAXIMA_FROM = NU + 1
    TURN_STEP, V_STEP = NW - 2, NW - 1
    FINISH_0, FINISH_1 = 7, 2
    ROPE_ROWS = slice(NOPE, MLA_D)
    with ExitStack() as s:
        sb = lambda n, sh, dt=F32: s.enter_context(nc.sbuf_tensor(f"mla_{n}", sh, dt))
        sem = lambda n: g.semaphore(f"mla_{n}")
        q_hi = [sb(f"q_hi{i}", [KALL, T], F32R) for i in range(2)]
        q_lo = [sb(f"q_lo{i}", [DK, T], F32R) for i in range(2)]
        k_hi = [sb(f"k_hi{i}", [KALL, T], F32R) for i in range(2)]
        k_lo = [sb(f"k_lo{i}", [DK, T], F32R) for i in range(2)]
        v_hi, v_lo = sb("v_hi", [P, 9, 3 * VD], F32R), sb("v_lo", [P, 9, 3 * VD], F32R)
        p32 = sb("p32", [P, 2, 512])
        p_hi, p_lo = sb("p_hi", [P, 2, 512], F32R), sb("p_lo", [P, 2, 512], F32R)
        sq, rs = sb("sq", [P, 384]), sb("rs", [P, 384])
        x32, turned = sb("x32", [P, 2, 384]), sb("turned", [P, 384])
        rden = sb("rden", [P, 512])
        ms, r0, nt = sb("ms", [P, 2, 3]), sb("r0", [P, 2, 3]), sb("nt", [P, 2, 3])
        threes = sb("threes", [P, 3])
        mpart, nm = sb("mpart", [P, QT, 3]), sb("nm", [P, P])
        m_hi, m_lo = sb("m_hi", [QT, P], F32R), sb("m_lo", [QT, P], F32R)
        UK, UV = 2 * MLA_D, 2 * MLA_D + NOPE
        w_head = [sb(f"w_head{i}", [P, UV + VD]) for i in range(2)]
        bank = [s.enter_context(nc.psum_tensor(f"mla_bank{i}", [P, 512], F32)) for i in range(8)]
        ST, OB = bank[0:2], bank[2:4]
        PROJ, BC = bank[4:7], bank[7]
        SUM_AT = 400
        MAXB, MT, VB = (bank[4], bank[7]), bank[5], (bank[6], bank[7])

        ones_set = sem("ones_set")
        w_in = [sem(f"w_in{i}") for i in range(2)]
        m_in = sem("m_in")
        proj_ready, squared, sum_ready, ms_done, logged, rooted, newton = (
            sem("proj_ready"), sem("squared"), sem("sum_ready"), sem("ms_done"), sem("logged"), sem("rooted"),
            sem("newton"))
        bc_ready, rs_done = sem("bc_ready"), sem("rs_done")
        x_done, x_turned, rope_steps, xhi_done, qk_done = (sem("x_done"), sem("x_turned"), sem("rope_steps"),
                                                           sem("xhi_done"), sem("qk_done"))
        v_ready, vhi_done, v_done = sem("v_ready"), sem("vhi_done"), sem("v_done")
        max_ready, max_read, nm_done, mt_ready, mhi_done, m_done = (sem("max_ready"), sem("max_read"),
                                                                    sem("nm_done"), sem("mt_ready"),
                                                                    sem("mhi_done"), sem("m_done"))
        st_ready, exp_done, phi_done, plo_done, pv_done = (sem("st_ready"), sem("exp_done"), sem("phi_done"),
                                                           sem("plo_done"), sem("pv_done"))
        ln_done, rden_done, o_done = sem("ln_done"), sem("rden_done"), sem("o_done")
        block = s.enter_context(nc.Block())

        def upto(eng, sem, per_head, p, h, more):
            wait(eng, sem, p, 2 * per_head, per_head * h + more)

        def shifted(p, h, w):
            if w >= 2:
                return h, w - 2
            return None if isinstance(p, int) and p == 0 and h == 0 else (h - 1, w - 2 + NW)

        def maximum_of(w, place):
            x = 3 * (w - MAXIMA_FROM) + place
            return x if 0 <= x < NM else None

        def v_columns(v, h, b):
            t = V_TILES[b]
            return v[:, t[0]:t[-1] + 1, 2 * VD * (h % 2):2 * VD * (h % 2) + VD]

        def v_tiles(b):
            return VB[b][:, 0:VD * len(V_TILES[b])].rearrange("p (t a) -> p t a", a=VD)

        def split_of(h, u):
            return (q_hi if units[u][0] else k_hi)[h % 2], (q_lo if units[u][0] else k_lo)[h % 2]

        @block.sync
        def _(sp):
            sp.wait_ge(ones_set, 1)

            def weights(p, i):
                upto(sp, v_ready, 2, p, i - 2, 2)
                sp.dma_start(w_head[i][:, :], g.dram["mla"][2 * p + i]).then_inc(w_in[i], 16)

            def maxima_rows(p, h):
                upto(sp, m_done, 1, p, h, 1)
                for src, r in ((m_hi, DK), (m_lo, DK + 1)):
                    sp.dma_start(q_hi[h % 2][r:r + 1, META:T].bitcast(F32).rearrange("o (a b) -> o a b", a=QT),
                                 src[:, :].bitcast(F32)).then_inc(m_in, 16)

            def pair(p, last=False):
                if not last:
                    weights(p + 1, 0)
                maxima_rows(p, 1)
                if not last:
                    weights(p + 1, 1)
                    maxima_rows(p, 2)
            weights(0, 0)
            weights(0, 1)
            maxima_rows(0, 0)
            over_pairs(sp, pair)

        @block.gpsimd
        def _(pool):
            pool.wait_ge(ones_set, 1)

            def newton_step(p, h, u):
                r, m, t = r0[:, u % 2, :], ms[:, u % 2, :], nt[:, u % 2, :]
                upto(pool, rooted, NU, p, h, u + 1)
                nc.gpsimd.tensor_tensor(t, m, r, ALU.mult).then_inc(newton, 1)
                upto(pool, newton, 4 * NU, p, h, 4 * u + 1)
                nc.gpsimd.tensor_tensor(t, t, r, ALU.mult).then_inc(newton, 1)
                upto(pool, newton, 4 * NU, p, h, 4 * u + 2)
                nc.gpsimd.tensor_tensor(t, threes[:, :], t, ALU.subtract).then_inc(newton, 1)
                upto(pool, newton, 4 * NU, p, h, 4 * u + 3)
                nc.gpsimd.tensor_tensor(r, r, t, ALU.mult).then_inc(newton, 1)

            def head(p, h, more=True):
                for w in range(NW):
                    if more and w < NU:
                        newton_step(p, h + 1, w)
                    n = ST_UNITS[w][4]
                    upto(pool, phi_done, NW, p, h, w + 1)
                    nc.gpsimd.tensor_tensor(p_lo[:, w % 2, 0:n], p32[:, w % 2, 0:n],
                                            p_hi[:, w % 2, 0:n].bitcast(F32), ALU.subtract).then_inc(plo_done, 1)

            def pair(p, last=False):
                head(p, 0)
                head(p, 1, more=not last)
            for u in range(NU):
                newton_step(0, 0, u)
            over_pairs(pool, pair)

        @block.scalar
        def _(act):
            def early(p, h, w):
                u = w - 3
                if 0 <= u < NU:
                    t0, n = QK_TOKENS[units[u][1]]
                    if units[u][0]:
                        upto(act, rope_steps, 9, p, h, 3 * (u // 2) + 3)
                    else:
                        upto(act, x_done, NU, p, h, u + 1)
                    if u == 0:
                        upto(act, st_ready, NW, p, h - 1, 0)
                    nc.scalar.copy(split_of(h, u)[0][0:DK, t0:t0 + n], x32[0:DK, u % 2, 0:n]).then_inc(xhi_done, 1)
                if w < NU:
                    is_q, c = units[w]
                    t0, n = QK_TOKENS[c]
                    upto(act, proj_ready, NU, p, h, w + 1)
                    upto(act, sum_ready, NU, p, h, w - 1)
                    src = PROJ[w % 3]
                    if is_q:
                        nc.scalar.activation(sq[0:DK, 0:n], src[0:DK, 0:n], ACT.Square).then_inc(squared, 1)
                    else:
                        nc.scalar.activation(g.ksq[0:NOPE, t0:t0 + n], src[0:NOPE, 0:n],
                                             ACT.Square).then_inc(squared, 1)

            def late(p, h, w):
                if w < NU:
                    upto(act, ms_done, NU, p, h, w + 1)
                    upto(act, bc_ready, NU, p, h, w - 1)
                    nc.scalar.activation(r0[:, w % 2, :], ms[:, w % 2, :], ACT.Ln).then_inc(logged, 1)
                    upto(act, logged, NU, p, h, w + 1)
                    nc.scalar.activation(r0[:, w % 2, :], r0[:, w % 2, :], ACT.Exp, scale=-0.5).then_inc(rooted, 1)
                if 1 <= w <= NU:
                    u = w - 1
                    n = QK_TOKENS[units[u][1]][1]
                    upto(act, bc_ready, NU, p, h, u + 1)
                    upto(act, x_done, NU, p, h, u)
                    nc.scalar.copy(rs[0:DK, 0:n], BC[0:DK, 0:n]).then_inc(rs_done, 1)
                if w == V_STEP:
                    upto(act, pv_done, NW, p, h - 1, 0)
                    for b in range(2):
                        upto(act, v_ready, 2, p, h, b + 1)
                        nc.scalar.copy(v_columns(v_hi, h, b), v_tiles(b)).then_inc(vhi_done, 1)

            def exponential(p, h, w):
                n = ST_UNITS[w][4]
                upto(act, st_ready, NW, p, h, w + 1)
                upto(act, plo_done, NW, p, h, w - 1)
                nc.scalar.activation(p32[:, w % 2, 0:n], ST[w % 2][:, 0:n], ACT.Exp).then_inc(exp_done, 1)

            def finish(p, h, c):
                rows, ones_rows = (slice(0, VD), slice(VD, P))[::1 if h % 2 == 0 else -1]
                upto(act, pv_done, NW, p, h, LAST_OF[c] + 1)
                upto(act, o_done, 2, p, h, c)
                nc.scalar.activation(rden[rows, :], OB[c][ones_rows, :], ACT.Ln).then_inc(ln_done, 1)
                upto(act, ln_done, 2, p, h, c + 1)
                nc.scalar.activation(rden[rows, :], rden[rows, :], ACT.Exp, scale=-1.0).then_inc(rden_done, 1)

            def head(p, h, more=True):
                for w in range(NW):
                    if more:
                        early(p, h + 1, w)
                    exponential(p, h, w)
                    if more:
                        late(p, h + 1, w)
                    if w == FINISH_0:
                        finish(p, h, 0)
                    if w == FINISH_1 and shifted(p, h, 1):
                        finish(p, h - 1, 1)

            def pair(p, last=False):
                head(p, 0)
                head(p, 1, more=not last)
            act.wait_ge(ones_set, 1)
            for w in range(NW):
                early(0, 0, w)
                late(0, 0, w)
            over_pairs(act, pair)
            finish(PAIRS - 1, 1, 1)

        @block.tensor
        def _(pe):
            pe.wait_ge(ones_set, 1)

            def products(p, h, u):
                is_q, c = units[u]
                t0, n = QK_TOKENS[c]
                out, w = PROJ[u % 3], w_head[h % 2]
                if u == 0:
                    upto(pe, max_read, NM, p, h, 0)
                    pe.wait_ge(w_in[h % 2], 16 * (p + (h // 2 + 1)))
                elif u == 1:
                    upto(pe, m_done, 1, p, h, 0)
                elif u == 2:
                    upto(pe, v_done, 2, p, h, -1)
                elif units[u - 3][0]:
                    upto(pe, rope_steps, 9, p, h, 3 * ((u - 3) // 2) + 2)
                else:
                    upto(pe, x_done, NU, p, h, u - 2)
                if is_q:
                    for k in range(2):
                        last = nc.tensor.matmul(out[0:DK, 0:n], w[:, k * DK:(k + 1) * DK], g.cq[:, k, t0:t0 + n],
                                                start=(k == 0), stop=(k == 1))
                else:
                    last = nc.tensor.matmul(out[0:NOPE, 0:n], w[:, UK:UK + NOPE], g.ckv[:, t0:t0 + n],
                                            start=True, stop=True)
                last.then_inc(proj_ready, 1)

            def sums(p, h, u):
                is_q, c = units[u]
                t0, n = QK_TOKENS[c]
                upto(pe, squared, NU, p, h, u + 1)
                src = sq[0:DK, 0:n] if is_q else g.ksq[0:DK, t0:t0 + n]
                for i, off in enumerate(QK_TILES[c]):
                    last = nc.tensor.matmul(PROJ[u % 3][:, SUM_AT + i:SUM_AT + i + 1], src[:, off:off + P],
                                            g.ones[0:DK, 0:1], start=True, stop=True)
                last.then_inc(sum_ready, 1)

            def broadcast(p, h, u):
                upto(pe, newton, 4 * NU, p, h, 4 * u + 4)
                if u == 0:
                    upto(pe, v_done, 2, p, h, 0)
                else:
                    upto(pe, rs_done, NU, p, h, u)
                for i, off in enumerate(QK_TILES[units[u][1]]):
                    last = nc.tensor.matmul(BC[0:DK, off:off + P], r0[:, u % 2, i:i + 1].broadcast_to([P, DK]),
                                            g.ident[:, :], start=True, stop=True)
                last.then_inc(bc_ready, 1)

            def turn(p, h, u):
                n = QK_TOKENS[units[u][1]][1]
                upto(pe, x_done, NU, p, h, u + 1)
                nc.tensor.matmul(PROJ[u % 3][0:DK, 0:n], g.rot[NOPE:DK, 0:DK], x32[NOPE:DK, u % 2, 0:n],
                                 start=True, stop=True).then_inc(x_turned, 1)

            def values(p, h, b):
                if b == 0:
                    upto(pe, x_done, NU, p, h, NU)
                else:
                    upto(pe, max_read, NM, p, h, NM)
                for i, t in enumerate(V_TILES[b]):
                    tok = min(P * t, T - P)
                    last = nc.tensor.matmul(VB[b][:, VD * i:VD * i + VD], g.ckv[:, tok:tok + P],
                                            w_head[h % 2][:, UV:UV + VD], start=True, stop=True)
                last.then_inc(v_ready, 1)

            def maxima(p, h, w, place):
                x = maximum_of(w, place)
                if x is None:
                    return
                i, part, k0, n = MAX_UNITS[x]
                out = MAXB[x % 2]
                if x == 0:
                    upto(pe, qk_done, NU, p, h, NU - 2)
                elif x == 1:
                    upto(pe, rs_done, NU, p, h, NU)
                else:
                    upto(pe, max_read, NM, p, h, x - 1)
                if x == SHORT:
                    upto(pe, qk_done, NU, p, h, NU)
                q0 = META + P * i
                diagonal = k0 + n == q0 + P
                last = nc.tensor.matmul(out[:, 0:n], q_hi[h % 2][0:DK, q0:q0 + P], k_hi[h % 2][0:DK, k0:k0 + n],
                                        start=True, stop=not diagonal)
                if diagonal:
                    last = nc.tensor.matmul(out[:, n - P:n], g.ident_r[:, :], g.masks[:, P:2 * P],
                                            start=False, stop=True)
                last.then_inc(max_ready, 1)

            def turn_maxima(p, h):
                upto(pe, nm_done, 1, p, h, 1)
                nc.tensor.transpose(MT[:, 0:P], nm[:, :], g.ident[:, :]).then_inc(mt_ready, 1)

            def scores(p, h, w):
                c, kt, k0, q0, n = ST_UNITS[w]
                out = ST[w % 2]
                upto(pe, exp_done, NW, p, h, w - 1)
                if w == 0:
                    upto(pe, m_in, 32, p, h, 32)
                kh, kl = k_hi[h % 2][:, k0:k0 + P], k_lo[h % 2][:, k0:k0 + P]
                qh, ql = q_hi[h % 2], q_lo[h % 2]
                nc.tensor.matmul(out[:, 0:n], kh[0:KALL], qh[0:KALL, q0:q0 + n], start=True, stop=False)
                nc.tensor.matmul(out[:, 0:n], kl[0:DK], qh[0:DK, q0:q0 + n], start=False, stop=False)
                d0, d1 = max(q0, P * kt), min(q0 + n, P * kt + P)
                diagonal = d0 < d1
                last = nc.tensor.matmul(out[:, 0:n], kh[0:DK], ql[0:DK, q0:q0 + n], start=False, stop=not diagonal)
                if diagonal:
                    m0 = 2 * P if kt == 8 else d0 - P * kt
                    last = nc.tensor.matmul(out[:, d0 - q0:d1 - q0], g.ident_r[:, :],
                                            g.masks[:, m0:m0 + d1 - d0], start=False, stop=True)
                last.then_inc(st_ready, 1)

            def weigh(p, h, w):
                c, kt, k0, q0, n = ST_UNITS[w]
                cq0 = REAL_TOKENS[c][0]
                out = OB[c][:, q0 - cq0:q0 - cq0 + n]
                upto(pe, plo_done, NW, p, h, w + 1)
                if kt == 0:
                    upto(pe, o_done, 2, p, h, c - 1)
                    if c == 0:
                        upto(pe, v_done, 2, p, h, 2)
                cols = slice(VD * (h % 2), VD * (h % 2) + P)
                nc.tensor.matmul(out, v_hi[:, kt, cols], p_hi[:, w % 2, 0:n], start=(kt == 0), stop=False)
                nc.tensor.matmul(out, v_lo[:, kt, cols], p_hi[:, w % 2, 0:n], start=False, stop=False)
                nc.tensor.matmul(out, v_hi[:, kt, cols], p_lo[:, w % 2, 0:n], start=False,
                                 stop=w == LAST_OF[c]).then_inc(pv_done, 1)

            def prepare(p, h, w):
                if w < NU:
                    sums(p, h, w)
                if 0 <= w - 2 < NU and units[w - 2][0]:
                    turn(p, h, w - 2)
                if 1 <= w <= NU:
                    broadcast(p, h, w - 1)
                maxima(p, h, w, 2)
                if w == TURN_STEP:
                    turn_maxima(p, h)
                if w == V_STEP:
                    values(p, h, 0)
                    values(p, h, 1)

            def head(p, h, more=True):
                for w in range(NW):
                    if more and w < NU:
                        products(p, h + 1, w)
                    if more:
                        maxima(p, h + 1, w, 0)
                    scores(p, h, w)
                    if more:
                        maxima(p, h + 1, w, 1)
                    if shifted(p, h, w):
                        weigh(p, *shifted(p, h, w))
                    if more:
                        prepare(p, h + 1, w)

            def pair(p, last=False):
                head(p, 0)
                head(p, 1, more=not last)
            for w in range(NW):
                if w < NU:
                    products(0, 0, w)
                maxima(0, 0, w, 0)
                maxima(0, 0, w, 1)
                prepare(0, 0, w)
            over_pairs(pe, pair)
            for w in range(NW - 2, NW):
                weigh(PAIRS - 1, 1, w)

        @block.vector
        def _(dve):
            for h in range(2):
                nc.vector.memset(q_hi[h][DK:KALL, :].bitcast(F32), 1.0)
                nc.vector.memset(k_hi[h][DK:KALL, :].bitcast(F32), 1.0)
            nc.vector.memset(v_lo[:, :, VD:2 * VD].bitcast(F32), 0.0)
            nc.vector.memset(nm[:, :], 0.0)
            nc.vector.memset(threes[:, :], 3.0)
            nc.vector.memset(mpart[:, :, :], NEG)
            nc.vector.memset(v_hi[:, :, VD:2 * VD].bitcast(F32), 1.0).then_inc(ones_set, 1)
            dve.wait_ge(ones_set, 1)

            def mean_squares(p, h, u):
                is_q = units[u][0]
                upto(dve, sum_ready, NU, p, h, u + 1)
                upto(dve, newton, 4 * NU, p, h, 4 * u - 4)
                nc.vector.tensor_scalar(ms[:, u % 2, :], PROJ[u % 3][:, SUM_AT:SUM_AT + 3],
                                        4.0 if is_q else 4.0 / DK, 4 * DK * EPS if is_q else 4 * EPS,
                                        ALU.mult, ALU.add).then_inc(ms_done, 1)

            def scale(p, h, u):
                is_q, c = units[u]
                t0, n = QK_TOKENS[c]
                src, x = PROJ[u % 3], x32[:, u % 2, 0:n]
                upto(dve, rs_done, NU, p, h, u + 1)
                upto(dve, qk_done, NU, p, h, u - 1)
                if is_q:
                    nc.vector.scalar_tensor_tensor(x[0:DK], src[0:DK, 0:n], g.gains[0:DK, g.MQ_COL:g.MQ_COL + 1],
                                                   rs[0:DK, 0:n], ALU.mult, ALU.mult).then_inc(x_done, 1)
                else:
                    nc.vector.tensor_tensor(x[ROPE_ROWS], g.krope[ROPE_ROWS, t0:t0 + n], rs[ROPE_ROWS, 0:n], ALU.mult)
                    nc.vector.scalar_tensor_tensor(x[0:NOPE], src[0:NOPE, 0:n], g.gains[0:NOPE, g.MK_COL:g.MK_COL + 1],
                                                   rs[0:NOPE, 0:n], ALU.mult, ALU.mult).then_inc(x_done, 1)

            def rope(p, h, u):
                t0, n = QK_TOKENS[units[u][1]]
                x, q_count = x32[ROPE_ROWS, u % 2, 0:n], u // 2
                upto(dve, x_turned, 3, p, h, q_count + 1)
                nc.vector.tensor_tensor(x, x, g.cos[ROPE_ROWS, t0:t0 + n], ALU.mult).then_inc(rope_steps, 1)
                nc.vector.tensor_tensor(turned[ROPE_ROWS, 0:n], PROJ[u % 3][ROPE_ROWS, 0:n],
                                        g.sin[ROPE_ROWS, t0:t0 + n], ALU.mult).then_inc(rope_steps, 1)
                upto(dve, rope_steps, 9, p, h, 3 * q_count + 2)
                nc.vector.tensor_tensor(x, x, turned[ROPE_ROWS, 0:n], ALU.add).then_inc(rope_steps, 1)

            def split_lo(p, h, u):
                t0, n = QK_TOKENS[units[u][1]]
                hi, lo = split_of(h, u)
                upto(dve, xhi_done, NU, p, h, u + 1)
                nc.vector.tensor_tensor(lo[0:DK, t0:t0 + n], x32[0:DK, u % 2, 0:n],
                                        hi[0:DK, t0:t0 + n].bitcast(F32), ALU.subtract).then_inc(qk_done, 1)

            def maxima(p, h, w, place):
                x = maximum_of(w, place)
                if x is None:
                    return
                i, part, k0, n = MAX_UNITS[x]
                upto(dve, max_ready, NM, p, h, x + 1)
                nc.vector.tensor_reduce(mpart[:, i, part:part + 1], MAXB[x % 2][:, 0:n], AX_X,
                                        ALU.max).then_inc(max_read, 1)
                if x == NM - 1:
                    upto(dve, max_read, NM, p, h, NM)
                    upto(dve, mt_ready, 1, p, h, 0)
                    nc.vector.tensor_reduce(nm[:, 0:QT], mpart[:, :, :], AX_X, ALU.max,
                                            negate=True).then_inc(nm_done, 1)

            def prepare(p, h, w):
                if 0 <= w - 2 < NU and units[w - 2][0]:
                    rope(p, h, w - 2)
                if 0 <= w - 3 < NU:
                    split_lo(p, h, w - 3)
                if 1 <= w <= NU:
                    scale(p, h, w - 1)
                maxima(p, h, w, 2)
                if w == TURN_STEP:
                    upto(dve, mt_ready, 1, p, h, 1)
                    upto(dve, m_in, 32, p, h, 0)
                    nc.vector.tensor_copy(m_hi[:, :], MT[0:QT, 0:P]).then_inc(mhi_done, 1)
                    upto(dve, mhi_done, 1, p, h, 1)
                    nc.vector.tensor_tensor(m_lo[:, :], MT[0:QT, 0:P], m_hi[:, :].bitcast(F32),
                                            ALU.subtract).then_inc(m_done, 1)
                if w == V_STEP:
                    for b in range(2):
                        upto(dve, vhi_done, 2, p, h, b + 1)
                        nc.vector.tensor_tensor(v_columns(v_lo, h, b), v_tiles(b), v_columns(v_hi, h, b).bitcast(F32),
                                                ALU.subtract).then_inc(v_done, 1)

            def finish(p, h, c):
                rows = slice(VD * (h % 2), VD * (h % 2) + VD)
                q0 = REAL_TOKENS[c][0] - META
                upto(dve, rden_done, 2, p, h, c + 1)
                nc.vector.tensor_tensor(g.o_mla[rows, p if h >= 0 else p - 1, q0:q0 + 512], OB[c][rows, :],
                                        rden[rows, :], ALU.mult).then_inc(o_done, 1)

            def head(p, h, more=True):
                for w in range(NW):
                    n = ST_UNITS[w][4]
                    if more and w < NU:
                        mean_squares(p, h + 1, w)
                    if more:
                        maxima(p, h + 1, w, 0)
                        maxima(p, h + 1, w, 1)
                    upto(dve, exp_done, NW, p, h, w + 1)
                    upto(dve, pv_done, NW, p, h, w - 1)
                    nc.vector.tensor_copy(p_hi[:, w % 2, 0:n], p32[:, w % 2, 0:n]).then_inc(phi_done, 1)
                    if more:
                        prepare(p, h + 1, w)
                    if w == FINISH_0:
                        finish(p, h, 0)
                    if w == FINISH_1 and shifted(p, h, 1):
                        finish(p, h - 1, 1)

            def pair(p, last=False):
                head(p, 0)
                head(p, 1, more=not last)
            for w in range(NW):
                if w < NU:
                    mean_squares(0, 0, w)
                maxima(0, 0, w, 0)
                maxima(0, 0, w, 1)
                prepare(0, 0, w)
            over_pairs(dve, pair)
            finish(PAIRS - 1, 1, 1)


def gate_phase(nc, g):
    with ExitStack() as s:
        sb = lambda n, sh, dt=F32: s.enter_context(nc.sbuf_tensor("gt_" + n, sh, dt))
        sem = lambda n: g.semaphore("gt_" + n)
        raw = sb("raw", [P, 3, D])
        w_hi, w_lo = sb("w_hi", [P, 3, D], F32R), sb("w_lo", [P, 3, D], F32R)
        o_hi, o_lo = sb("o_hi", [P, KD, SEQ], F32R), sb("o_lo", [P, KD, SEQ], F32R)
        sg = sb("sg", [P, 3, 512])
        bank = [s.enter_context(nc.psum_tensor(f"gt_bank{i}", [P, 512], F32)) for i in range(8)]
        raw_in = [sem(f"raw_in{i}") for i in range(3)]
        whi_done, wlo_done, ohi_done, olo_done = sem("whi_done"), sem("wlo_done"), sem("ohi_done"), sem("olo_done")
        ready, opened, shut, mult_done = sem("ready"), sem("opened"), sem("shut"), sem("mult_done")
        uhi_done, ulo_done = sem("uhi_done"), sem("ulo_done")
        block = s.enter_context(nc.Block())
        o_tile = lambda t: (g.o_fox if t < PAIRS else g.o_mla)[:, t % PAIRS, :]
        UNITS = [("gf", 0), ("gf", 1), ("gm", 0), ("bf", 0), ("bm", 0), ("gm", 1), ("bf", 1), ("bm", 1)]

        def over_tiles(eng, body):
            body(0)
            with eng.Fori(1, KD) as m:
                body(m)

        @block.sync
        def _(sp):
            def tile(m):
                for j in range(3):
                    wait(sp, wlo_done, m, 3, j - 2)
                    sp.dma_start(raw[:, j, :], g.dram["gate"][3 * m + j]).then_inc(raw_in[j], 16)
            over_tiles(sp, tile)

        @block.gpsimd
        def _(pool):
            def split_lo(m, j):
                wait(pool, whi_done, m, 3, j + 1)
                nc.gpsimd.tensor_tensor(w_lo[:, j, :], raw[:, j, :], w_hi[:, j, :].bitcast(F32),
                                        ALU.subtract).then_inc(wlo_done, 1)
            for j in range(2):
                split_lo(0, j)
            for t in range(0, KD, 2):
                pool.wait_ge(ohi_done, t + 1)
                nc.gpsimd.tensor_tensor(o_lo[:, t, :], o_tile(t), o_hi[:, t, :].bitcast(F32),
                                        ALU.subtract).then_inc(olo_done, 1)
            split_lo(0, 2)
            with pool.Fori(1, KD) as m:
                for j in range(3):
                    split_lo(m, j)

        @block.scalar
        def _(act):
            def split_hi(m, j, used):
                act.wait_ge(raw_in[j], 16 * (m + 1))
                wait(act, ready, m, 8, used - 8)
                nc.scalar.copy(w_hi[:, j, :], raw[:, j, :]).then_inc(whi_done, 1)

            def sigmoid(m, which, c, slot, unit):
                wait(act, ready, m, 8, unit + 1)
                wait(act, shut, m, 4, {0: -2 + 0, 1: 0, 2: 0, 5: 2}[unit])
                bias = g.gains[:, bass.ds(m + (g.BG_COL + KD * which), 1)]
                nc.scalar.activation(sg[:, slot, :], bank[unit][:, :], ACT.Sigmoid, bias=bias).then_inc(opened, 1)

            def tile(m, more=True):
                if not (isinstance(m, int) and m == 0):
                    split_hi(m, 2, 8)
                sigmoid(m, 0, 0, 0, 0)
                sigmoid(m, 0, 1, 1, 1)
                if more:
                    split_hi(m + 1, 0, 2)
                sigmoid(m, 1, 0, 2, 2)
                sigmoid(m, 1, 1, 2, 5)
                if more:
                    split_hi(m + 1, 1, 6)

            split_hi(0, 0, 0)
            split_hi(0, 1, 0)
            for t in range(KD):
                nc.scalar.copy(o_hi[:, t, :], o_tile(t)).then_inc(ohi_done, 1)
            split_hi(0, 2, 0)
            for m in range(KD):
                tile(m, more=m < KD - 1)
            for t in range(KD):
                act.wait_ge(ready, 8 * KD)
                act.wait_ge(shut, 4 * KD)
                nc.scalar.copy(g.u_hi[:, t, META:T], o_tile(t)).then_inc(uhi_done, 1)

        @block.tensor
        def _(pe):
            def tile(m):
                for u, (kind, c) in enumerate(UNITS):
                    t0 = REAL_TOKENS[c][0]
                    out = bank[u]
                    if kind[0] == "g":
                        wait(pe, opened, m, 4, {0: -3, 1: -2, 2: -1, 5: 0}[u])
                        j = 0 if kind == "gf" else 1
                        if c == 0:
                            wait(pe, wlo_done, m, 3, j + 1)
                        for k in range(KD):
                            last = mm3(nc, out[:, :], w_hi[:, j, k * P:(k + 1) * P], w_lo[:, j, k * P:(k + 1) * P],
                                       g.u_hi[:, k, t0:t0 + 512], g.u_lo[:, k, t0:t0 + 512], k == 0, k == KD - 1)
                    else:
                        wait(pe, shut, m, 4, {3: -3, 4: -2, 6: -1, 7: 0}[u])
                        if u == 3:
                            wait(pe, wlo_done, m, 3, 3)
                            pe.wait_ge(olo_done, KD)
                        first = 0 if kind == "bf" else PAIRS
                        for k in range(first, first + PAIRS):
                            x = slice(512 * c, 512 * c + 512)
                            last = mm3(nc, out[:, :], w_hi[:, 2, k * P:(k + 1) * P], w_lo[:, 2, k * P:(k + 1) * P],
                                       o_hi[:, k, x], o_lo[:, k, x], k == first, k == first + PAIRS - 1)
                    last.then_inc(ready, 1)
            over_tiles(pe, tile)

        @block.vector
        def _(dve):
            def tile(m, dst, m_dst):
                for c in range(2):
                    base = (3, 6)[c]
                    for which in range(2):
                        slot = c if which == 0 else 2
                        wait(dve, ready, m, 8, base + which + 1)
                        wait(dve, opened, m, 4, {(0, 0): 1, (0, 1): 3, (1, 0): 2, (1, 1): 4}[(c, which)])
                        ins = nc.vector.tensor_tensor(sg[:, slot, :], bank[base + which][:, :], sg[:, slot, :], ALU.mult)
                        if which == 0:
                            ins.then_inc(shut, 1)
                        else:
                            ins.then_inc(mult_done, 1)
                    wait(dve, mult_done, m, 2, c + 1)
                    wait(dve, shut, m, 4, 2 * c + 1)
                    nc.vector.tensor_tensor(dst[:, m_dst, 512 * c:512 * c + 512], sg[:, c, :], sg[:, 2, :],
                                            ALU.add).then_inc(shut, 1)

            for t in range(1, KD, 2):
                dve.wait_ge(ohi_done, t + 1)
                nc.vector.tensor_tensor(o_lo[:, t, :], o_tile(t), o_hi[:, t, :].bitcast(F32),
                                        ALU.subtract).then_inc(olo_done, 1)
            dve.wait_ge(olo_done, KD)
            tile(0, g.o_fox, 0)
            with dve.Fori(1, PAIRS) as m:
                tile(m, g.o_fox, m)
            with dve.Fori(PAIRS, KD) as m:
                tile(m, g.o_mla, m - PAIRS)
            for t in range(KD):
                dve.wait_ge(uhi_done, t + 1)
                nc.vector.tensor_tensor(g.u_lo[:, t, META:T], o_tile(t), g.u_hi[:, t, META:T].bitcast(F32),
                                        ALU.subtract).then_inc(ulo_done, 1)


def out_proj_phase(nc, g):
    with ExitStack() as s:
        sb = lambda n, sh, dt=F32: s.enter_context(nc.sbuf_tensor("op_" + n, sh, dt))
        sem = lambda n: g.semaphore("op_" + n)
        raw = sb("raw", [P, 3, D])
        w_hi, w_lo = sb("w_hi", [P, 3, D], F32R), sb("w_lo", [P, 3, D], F32R)
        bank = [s.enter_context(nc.psum_tensor(f"op_bank{i}", [P, 512], F32)) for i in range(4)]
        raw_in = [sem(f"raw_in{i}") for i in range(3)]
        h_in = [sem(f"h_in{i}") for i in range(KD)]
        whi_done, wlo_done, ready, added = sem("whi_done"), sem("wlo_done"), sem("ready"), sem("added")
        block = s.enter_context(nc.Block())

        @block.sync
        def _(sp):
            for m in range(KD):
                if m >= 3:
                    sp.wait_ge(wlo_done, m - 2)
                sp.dma_start(raw[:, m % 3, :], g.dram["wout"][m]).then_inc(raw_in[m % 3], 16)
                sp.dma_start(g.h[:, m, :], g.dram["hsave"][:, m, :]).then_inc(h_in[m], 16)

        @block.scalar
        def _(act):
            for m in range(KD):
                act.wait_ge(raw_in[m % 3], 16 * (m // 3 + 1))
                if m >= 3:
                    act.wait_ge(ready, 2 * (m - 2))
                nc.scalar.copy(w_hi[:, m % 3, :], raw[:, m % 3, :]).then_inc(whi_done, 1)

        @block.gpsimd
        def _(pool):
            for m in range(KD):
                pool.wait_ge(whi_done, m + 1)
                nc.gpsimd.tensor_tensor(w_lo[:, m % 3, :], raw[:, m % 3, :], w_hi[:, m % 3, :].bitcast(F32),
                                        ALU.subtract).then_inc(wlo_done, 1)

        @block.tensor
        def _(pe):
            for m in range(KD):
                pe.wait_ge(wlo_done, m + 1)
                for c, (t0, n) in enumerate(REAL_TOKENS):
                    u = 2 * m + c
                    if u >= 4:
                        pe.wait_ge(added, u - 3)
                    for k in range(KD):
                        last = mm3(nc, bank[u % 4][:, :], w_hi[:, m % 3, k * P:(k + 1) * P],
                                   w_lo[:, m % 3, k * P:(k + 1) * P], g.u_hi[:, k, t0:t0 + n],
                                   g.u_lo[:, k, t0:t0 + n], k == 0, k == KD - 1)
                    last.then_inc(ready, 1)

        @block.vector
        def _(dve):
            for m in range(KD):
                dve.wait_ge(h_in[m], 16)
                for c, (t0, n) in enumerate(REAL_TOKENS):
                    u = 2 * m + c
                    dve.wait_ge(ready, u + 1)
                    nc.vector.tensor_tensor(g.h[:, m, t0:t0 + n], g.h[:, m, t0:t0 + n], bank[u % 4][:, :],
                                            ALU.add).then_inc(added, 1)


def store_phase(nc, g):
    with ExitStack() as s:
        sem = lambda n: g.semaphore("st_" + n)
        rows = s.enter_context(nc.sbuf_tensor("st_rows", [P, 3, D], F32))
        tp = [s.enter_context(nc.psum_tensor(f"st_tp{i}", [P, 4, P], F32)) for i in range(4)]
        transposed, copied = sem("transposed"), sem("copied")
        stored = [sem(f"stored{i}") for i in range(3)]
        block = s.enter_context(nc.Block())

        @block.tensor
        def _(pe):
            for t in range(QT):
                for half in range(2):
                    n = 2 * t + half
                    if n >= 4:
                        pe.wait_ge(copied, n - 3)
                    for k in range(4):
                        last = nc.tensor.transpose(tp[n % 4][:, k, :],
                                                   g.h[:, 4 * half + k, META + t * P:META + (t + 1) * P], g.ident[:, :])
                    last.then_inc(transposed, 1)

        @block.vector
        def _(dve):
            for t in range(QT):
                for half in range(2):
                    n = 2 * t + half
                    dve.wait_ge(transposed, n + 1)
                    if t >= 3:
                        dve.wait_ge(stored[t % 3], 16 * (t // 3))
                    nc.vector.tensor_copy(rows[:, t % 3, 512 * half:512 * half + 512],
                                          tp[n % 4][:, :, :].rearrange("p a b -> p (a b)")).then_inc(copied, 1)

        @block.sync
        def _(sp):
            for t in range(QT):
                sp.wait_ge(copied, 2 * (t + 1))
                sp.dma_start(g.dram["out"][t * P:(t + 1) * P, :], rows[:, t % 3, :]).then_inc(stored[t % 3], 16)
            for i in range(3):
                sp.wait_ge(stored[i], 16 * len(range(i, QT, 3)))


class Shared:
    FFN1_GAIN, MIX_GAIN, FFN2_GAIN = 0, KD, 2 * KD
    EPS_COL, EPSQ_COL, BF_COL = 3 * KD, 3 * KD + 1, 3 * KD + 3
    FQ_COL, FK_COL, MQ_COL, MK_COL, CN_COL, BG_COL = [3 * KD + x for x in (4, 5, 6, 7, 8, 11)]

    def __init__(self):
        self.dram = {}


def build(nc, g):
    with ExitStack() as s:
        first_half = []

        def of_first_half(name):
            first_half.append(nc.alloc_semaphore(name))
            return first_half[-1]
        g.semaphore = of_first_half
        sb = lambda n, sh, dt=F32: s.enter_context(nc.sbuf_tensor(n, sh, dt))
        g.ident = sb("ident", [P, P])
        g.ones = sb("ones", [P, P])
        g.gains = sb("gains", [P, g.dram["gains"].shape[1]])
        g.u_hi = sb("u_hi", [P, KD, T], F32R)
        g.u_lo = sb("u_lo", [P, KD, T], F32R)
        with ExitStack() as mix:
            mb = lambda n, sh, dt=F32: mix.enter_context(nc.sbuf_tensor(n, sh, dt))
            g.ident_r = mb("ident_r", [P, P], F32R)
            g.masks = mb("masks", [P, 2 * P + META], F32R)
            g.head_sum = mb("head_sum", [P, P])
            g.rot = mb("rot", [P, P])
            with nc.sbuf_tensor("h_in", [P, KD, T], F32) as h:
                g.h = h
                load_phase(nc, g)
                norm_phase(nc, g, "n1", g.FFN1_GAIN, ALL_TOKENS)
                ffn_phase(nc, g, "f1", g.dram["ffn1"], ALL_TOKENS)
                norm_phase(nc, g, "n2", g.MIX_GAIN, ALL_TOKENS)
                forget_phase(nc, g)
            g.o_fox = mb("o_fox", [P, PAIRS, SEQ])
            attention_phase(nc, g, "fox", g.o_fox)
            nc.clear_and_free_semaphores(first_half)
            nc.all_engine_barrier()
            g.semaphore = lambda name: s.enter_context(nc.semaphore(name))
            g.o_mla = mb("o_mla", [P, PAIRS, SEQ])
            with ExitStack() as lat:
                lb = lambda n, sh, dt=F32: lat.enter_context(nc.sbuf_tensor(n, sh, dt))
                g.cq, g.ckv = lb("cq", [P, 2, T]), lb("ckv", [P, T])
                g.krope, g.ksq = lb("krope", [P, T]), lb("ksq", [P, T])
                g.cos, g.sin = lb("cos", [P, T]), lb("sin", [P, T])
                latent_phase(nc, g)
                latent_attention_phase(nc, g)
            gate_phase(nc, g)
        with nc.sbuf_tensor("h_out", [P, KD, T], F32) as h:
            g.h = h
            out_proj_phase(nc, g)
            norm_phase(nc, g, "n3", g.FFN2_GAIN, REAL_TOKENS)
            ffn_phase(nc, g, "f2", g.dram["ffn2"], REAL_TOKENS)
            store_phase(nc, g)


def _k_blocks(w):
    n = w.shape[1] // P
    return w.reshape(KD, P, n, P).transpose(2, 1, 0, 3).reshape(n, P, D)


def _ffn_blocks(w_gu, w_down):
    gate, up = _k_blocks(w_gu[:, :DFF]), _k_blocks(w_gu[:, DFF:])
    down = w_down.reshape(FT, P, D)
    gu = lambda i: [gate[2 * i], up[2 * i], gate[2 * i + 1], up[2 * i + 1]]
    dn = lambda i: [down[2 * i], down[2 * i + 1]]
    order = gu(0)
    for i in range(1, FT // 2):
        order += gu(i) + dn(i - 1)
    return np.stack(order + dn(FT // 2 - 1))


def _columns(v):
    return v.reshape(-1, P).T


def layout(i):
    a = {n: np.asarray(v) for n, v in i.items()}
    out = {"x": a["x"][0], "meta": a["meta_tokens"]}
    out["ffn1"] = _ffn_blocks(a["ffn1_w_gu"][0], a["ffn1_w_down"][0])
    out["ident"] = np.eye(P, dtype=np.float32)
    out["ones"] = np.ones((P, P), np.float32)
    w_in = a["w_in"][0]
    cuts = np.cumsum([FOX_D * HEADS] * 3 + [HEADS, CQ, CKV, ROPE, 2 * D])
    fq, fk, fv, fl, cq, ckv, kr, gates = np.split(w_in, cuts[:-1], axis=1)
    out["fox"] = np.stack([_k_blocks(w)[p] for p in range(PAIRS) for w in (fq, fk, fv)])
    shared = np.zeros((D, P), np.float32)
    shared[:, 0:HEADS] = fl
    shared[:, NOPE:MLA_D] = kr
    out["misc"] = np.concatenate([_k_blocks(shared), _k_blocks(ckv), _k_blocks(cq)])
    uq = a["mla_w_uq"][0].reshape(2, P, HEADS, MLA_D).transpose(2, 1, 0, 3).reshape(HEADS, P, 2 * MLA_D)
    ukv = a["mla_w_ukv"][0].reshape(P, HEADS, 2 * NOPE).transpose(1, 0, 2)
    out["mla"] = np.concatenate([uq, ukv], axis=2)
    branch = np.concatenate([a["w_branch_fox"][0], a["w_branch_mla"][0]])
    gate_blocks, branch_blocks = _k_blocks(gates), _k_blocks(branch)
    out["gate"] = np.stack([w for m in range(KD) for w in (gate_blocks[m], gate_blocks[KD + m], branch_blocks[m])])
    out["wout"] = _k_blocks(a["w_out"][0])
    out["ffn2"] = _ffn_blocks(a["ffn2_w_gu"][0], a["ffn2_w_down"][0])

    r, c = np.arange(P)[:, None], np.arange(P)[None, :]
    masks = np.zeros((P, 4 * P + META), np.float32)
    masks[:, 0:P] = np.where(r > c, NEG, 0)
    masks[:, P:2 * P] = np.where(c > r, NEG, 0)
    last = r - (P - META)
    masks[:, 2 * P:2 * P + META] = np.where((last < 0) | (last > c[:, :META]), NEG, 0)
    masks[:, 2 * P + META:3 * P + META] = (r // FOX_D == c // FOX_D)
    half = ROPE // 2
    for i in range(half):
        masks[NOPE + half + i, 3 * P + META + NOPE + i] = -1.0
        masks[NOPE + i, 3 * P + META + NOPE + half + i] = 1.0
    out["masks"] = masks
    freq = np.float32(10000.0) ** (-np.arange(0, ROPE, 2, dtype=np.float32) / np.float32(ROPE))
    angle = np.arange(T, dtype=np.float32)[None, :] * np.tile(freq, 2)[:, None]
    out["cos"], out["sin"] = np.cos(angle), np.sin(angle)

    def column(v):
        full = np.zeros((P, 1), np.float32)
        full[:len(v), 0] = v
        return full

    const = lambda x: np.full((P, 1), x, np.float32)
    out["gains"] = np.concatenate([
        _columns(a["ffn1_norm"][0]), _columns(a["mix_norm"][0]), _columns(a["ffn2_norm"][0]),
        const(EPS), const(FOX_D * EPS), const(MLA_D * EPS), column(a["b_forget"][0]),
        column(np.tile(a["fox_q_norm"][0], 2)), column(np.tile(a["fox_k_norm"][0], 2)),
        column(a["mla_q_norm"][0]), column(a["mla_k_norm"][0]),
        _columns(a["mla_ckv_norm"][0]), _columns(a["mla_cq_norm"][0]), _columns(a["b_gate"][0])], axis=1)
    return {n: np.ascontiguousarray(v, dtype=np.float32) for n, v in out.items()}


def kernel(**inputs):
    import concourse.bacc as bacc
    from concourse.bass_utils import run_bass_kernel_spmd
    arrays = layout(inputs)
    nc = bacc.Bacc("TRN2", target_bir_lowering=False, num_devices=1)
    g = Shared()
    for name, a in arrays.items():
        g.dram[name] = nc.dram_tensor(f"in_{name}", a.shape, mybir.dt.from_np(a.dtype), kind="ExternalInput").ap()
    for name, shape in (("hsave", (P, KD, T)), ("krope", (ROPE, T)), ("cum", (2, HEADS, T))):
        g.dram[name] = nc.dram_tensor(f"kept_{name}", shape, F32, kind="Internal").ap()
    g.dram["out"] = nc.dram_tensor("out", (SEQ, D), F32, kind="ExternalOutput").ap()
    build(nc, g)
    r = run_bass_kernel_spmd(nc, [{f"in_{n}": v for n, v in arrays.items()}], core_ids=[0])
    return np.asarray(r.results[0]["out"]).reshape(1, SEQ, D)
```

```python
from contextlib import ExitStack

import numpy as np

import concourse.bass as bass
from concourse import mybir

F32 = mybir.dt.float32
F32R = mybir.dt.float32r
ACT = mybir.ActivationFunctionType
ALU = mybir.AluOpType
AX_X = mybir.AxisListType.X

P = 128
D = 1024
KD = D // P
META = 16
SEQ = 1024
T = META + SEQ
QT = SEQ // P
DFF = 2816
FT = DFF // P
HEADS = 8
PAIRS = HEADS // 2
FOX_D = 64
NOPE, ROPE = 64, 32
MLA_D = NOPE + ROPE
VD = 64
CQ, CKV = 256, 128
EPS = 1e-6
NEG = -1.0e30

ALL_TOKENS = [(0, 348), (348, 346), (694, 346)]
REAL_TOKENS = [(META, 512), (META + 512, 512)]

TOKEN_TILES = [(0, META)] + [(META + P * t, P) for t in range(QT)]


def mm3(nc, out, w_hi, w_lo, x_hi, x_lo, first, last):
    nc.tensor.matmul(out, w_hi, x_hi, start=first, stop=False)
    nc.tensor.matmul(out, w_lo, x_hi, start=False, stop=False)
    return nc.tensor.matmul(out, w_hi, x_lo, start=False, stop=last)


def load_phase(nc, g):
    with ExitStack() as s:
        sb = lambda n, sh, dt=F32: s.enter_context(nc.sbuf_tensor("ld_" + n, sh, dt))
        sem = lambda n: g.semaphore("ld_" + n)
        xin = sb("xin", [P, 3, D])
        metain = sb("metain", [META, D])
        sq = sb("sq", [P, 2, D])
        squared = sem("squared")
        tp = [s.enter_context(nc.psum_tensor(f"ld_tp{i}", [P, 4, P], F32)) for i in range(4)]
        x_in = [sem(f"x_in{i}") for i in range(3)]
        meta_in, transposed, copied, consts_in = sem("meta_in"), sem("transposed"), sem("copied"), sem("consts_in")
        block = s.enter_context(nc.Block())

        @block.sync
        def _(sp):
            sp.dma_start(g.ident[:, :], g.dram["ident"]).then_inc(consts_in, 16)
            sp.dma_start(metain[:, :], g.dram["meta"]).then_inc(meta_in, 16)
            for t in range(QT):
                if t >= 3:
                    sp.wait_ge(transposed, 2 * (t - 2))
                    sp.wait_ge(squared, t - 2)
                sp.dma_start(xin[:, t % 3, :], g.dram["x"][t * P:(t + 1) * P, :]).then_inc(x_in[t % 3], 16)
            sp.dma_start(g.gains[:, :], g.dram["gains"]).then_inc(consts_in, 16)
            sp.dma_start(g.ones[:, :], g.dram["ones"]).then_inc(consts_in, 16)
            sp.wait_ge(consts_in, 48)

        @block.scalar
        def _(act):
            for t in range(QT):
                act.wait_ge(x_in[t % 3], 16 * (t // 3 + 1))
                if t >= 2:
                    act.wait_ge(squared, t - 1)
                nc.scalar.activation(sq[:, t % 2, :], xin[:, t % 3, :], ACT.Square,
                                     accum_out=g.ssum[:, t + 1:t + 2]).then_inc(squared, 1)
            act.wait_ge(meta_in, 16)
            act.wait_ge(squared, QT - 1)
            nc.scalar.activation(sq[0:META, QT % 2, :], metain[:, :], ACT.Square,
                                 accum_out=g.ssum[0:META, 0:1]).then_inc(squared, 1)

        @block.tensor
        def _(pe):
            pe.wait_ge(consts_in, 16)
            for t in range(QT):
                pe.wait_ge(x_in[t % 3], 16 * (t // 3 + 1))
                for half in range(2):
                    n = 2 * t + half
                    if n >= 4:
                        pe.wait_ge(copied, n - 3)
                    for k in range(4):
                        kk = 4 * half + k
                        last = nc.tensor.transpose(tp[n % 4][:, k, :], xin[:, t % 3, kk * P:(kk + 1) * P],
                                                   g.ident[:, :])
                    last.then_inc(transposed, 1)
            pe.wait_ge(meta_in, 16)
            for half in range(2):
                n = 2 * QT + half
                pe.wait_ge(copied, n - 3)
                for k in range(4):
                    kk = 4 * half + k
                    last = nc.tensor.transpose(tp[n % 4][:, k, 0:META], metain[:, kk * P:(kk + 1) * P],
                                               g.ident[0:META, 0:META])
                last.then_inc(transposed, 1)

        @block.vector
        def _(dve):
            for t in range(QT):
                for half in range(2):
                    n = 2 * t + half
                    dve.wait_ge(transposed, n + 1)
                    nc.vector.tensor_copy(g.h[:, 4 * half:4 * half + 4, META + t * P:META + (t + 1) * P],
                                          tp[n % 4][:, :, :]).then_inc(copied, 1)
            for half in range(2):
                n = 2 * QT + half
                dve.wait_ge(transposed, n + 1)
                nc.vector.tensor_copy(g.h[:, 4 * half:4 * half + 4, 0:META],
                                      tp[n % 4][:, :, 0:META]).then_inc(copied, 1)


class Norm:

    def __init__(self, nc, g, tag, s, gain_col, chunks, banks, u32, from_ssum):
        self.nc, self.g, self.gain_col, self.chunks, self.from_ssum = nc, g, gain_col, chunks, from_ssum
        sem = lambda n: g.semaphore(f"{tag}_{n}")
        self.rstd = s.enter_context(nc.sbuf_tensor(f"{tag}_rstd", [P, QT + 1], F32))
        self.u32 = u32
        self.sums, self.bc = banks[0], banks[1:]
        self.summed, self.rooted, self.inverted, self.bc_ready = (sem("summed"), sem("rooted"), sem("inverted"),
                                                                  sem("bc_ready"))
        self.u_done, self.hi_done, self.lo_pool, self.lo_dve = (sem("u_done"), sem("u_hi_done"), sem("lo_pool"),
                                                                sem("lo_dve"))
        self.units = [(c, k) for c in range(len(chunks)) for k in range(KD)]
        self.tiles = [i for i, (t0, n) in enumerate(TOKEN_TILES) if t0 >= chunks[0][0]]

    def by_pool(self, i):
        return i % 2 == 1

    def wait_lo(self, eng, units):
        for sem, mine in ((self.lo_pool, True), (self.lo_dve, False)):
            count = sum(1 for i in range(units) if self.by_pool(i) == mine)
            if count:
                eng.wait_ge(sem, count)

    def wait_chunk(self, eng, c):
        self.wait_lo(eng, KD * (c + 1))

    def pe_broadcast(self, pe):
        nc, g = self.nc, self.g
        if not self.from_ssum:
            for i in self.tiles:
                t0, n = TOKEN_TILES[i]
                last = nc.tensor.matmul(self.sums[0:n, i:i + 1], g.sumsq[:, t0:t0 + n], g.ones[:, 0:1],
                                        start=True, stop=True)
            last.then_inc(self.summed, 1)
        pe.wait_ge(self.inverted, 1)
        for c, (c0, cn) in enumerate(self.chunks):
            for i in self.tiles:
                t0, n = TOKEN_TILES[i]
                a, b = max(c0, t0), min(c0 + cn, t0 + n)
                if a < b:
                    last = nc.tensor.matmul(self.bc[c][:, a - c0:b - c0], self.rstd[0:n, i:i + 1].broadcast_to([n, P]),
                                            g.ident[0:n, a - t0:b - t0], start=True, stop=True)
            last.then_inc(self.bc_ready, 1)

    def act_root(self, act):
        nc, g = self.nc, self.g
        if not self.from_ssum:
            act.wait_ge(self.summed, 1)
        src = g.ssum if self.from_ssum else self.sums
        for rows, cols in ((META, slice(0, 1)), (P, slice(1, QT + 1))):
            if cols.start in self.tiles:
                nc.scalar.activation(self.rstd[0:rows, cols], src[0:rows, cols], ACT.Sqrt, scale=1.0 / D,
                                     bias=g.gains[0:rows, g.EPS_COL:g.EPS_COL + 1]).then_inc(self.rooted, 1)

    def act_hi(self, act, c):
        t0, n = self.chunks[c]
        for i in range(KD * c, KD * (c + 1)):
            act.wait_ge(self.u_done, i + 1)
            self.nc.scalar.copy(self.g.u_hi[:, i % KD, t0:t0 + n], self.u32[i % 4][:, 0:n]).then_inc(self.hi_done, 1)

    def lo(self, eng, i):
        c, k = self.units[i]
        t0, n = self.chunks[c]
        eng.wait_ge(self.hi_done, i + 1)
        return eng.tensor_tensor(self.g.u_lo[:, k, t0:t0 + n], self.u32[i % 4][:, 0:n],
                                 self.g.u_hi[:, k, t0:t0 + n].bitcast(F32), ALU.subtract)

    def pool_lo(self, pool, c):
        for i in range(KD * c, KD * (c + 1)):
            if self.by_pool(i):
                self.lo(pool, i).then_inc(self.lo_pool, 1)

    def dve(self, dve):
        nc, g = self.nc, self.g
        dve.wait_ge(self.rooted, 2 if 0 in self.tiles else 1)
        if 0 in self.tiles:
            nc.vector.reciprocal(self.rstd[0:META, 0:1], self.rstd[0:META, 0:1])
        nc.vector.reciprocal(self.rstd[:, 1:QT + 1], self.rstd[:, 1:QT + 1]).then_inc(self.inverted, 1)
        for i in range(len(self.units) + 2):
            if i < len(self.units):
                c, k = self.units[i]
                t0, n = self.chunks[c]
                dve.wait_ge(self.bc_ready, c + 1)
                self.wait_lo(dve, i - 3)
                nc.vector.scalar_tensor_tensor(self.u32[i % 4][:, 0:n], g.h[:, k, t0:t0 + n],
                                               g.gains[:, self.gain_col + k:self.gain_col + k + 1],
                                               self.bc[c][:, 0:n], ALU.mult, ALU.mult).then_inc(self.u_done, 1)
            if i >= 2 and not self.by_pool(i - 2):
                self.lo(dve, i - 2).then_inc(self.lo_dve, 1)


class SquareSum:

    def __init__(self, nc, g, tag, tokens, sq):
        self.nc, self.g, self.tokens, self.sq = nc, g, tokens, sq
        self.squared, self.added = g.semaphore(f"{tag}_h_squared"), g.semaphore(f"{tag}_sq_added")

    def square(self, act, d):
        if d >= 3:
            act.wait_ge(self.added, d - 2)
        dst = self.g.sumsq[:, self.tokens] if d == 0 else self.sq[d % 2][:, self.tokens]
        self.nc.scalar.activation(dst, self.g.h[:, d, self.tokens], ACT.Square).then_inc(self.squared, 1)

    def add(self, dve, d):
        if d == 0:
            return
        dve.wait_ge(self.squared, d + 1)
        if d >= 2:
            dve.wait_ge(self.added, d - 1)
        total = self.g.sumsq[:, self.tokens]
        self.nc.vector.tensor_tensor(total, total, self.sq[d % 2][:, self.tokens], ALU.add).then_inc(self.added, 1)


class Store:

    def __init__(self, nc, g, banks, rows):
        self.nc, self.g, self.banks, self.rows = nc, g, banks, rows
        self.turned = g.semaphore("st_turned")
        self.copied = [g.semaphore(f"st_copied{i}") for i in range(2)]
        self.stored = [g.semaphore(f"st_stored{i}") for i in range(len(rows))]

    def turn(self, pe, t):
        for half in range(2):
            n = 2 * t + half
            if n >= 4:
                pe.wait_ge(self.copied[half], t - 1)
            for k in range(4):
                last = self.nc.tensor.transpose(self.banks[n % 4][:, k * P:(k + 1) * P],
                                                self.g.h[:, 4 * half + k, META + t * P:META + (t + 1) * P],
                                                self.g.ident[:, :])
            last.then_inc(self.turned, 1)

    def copy_half(self, eng, t, half):
        n = 2 * t + half
        eng.wait_ge(self.turned, n + 1)
        r = t % len(self.rows)
        if t >= len(self.rows):
            eng.wait_ge(self.stored[r], 16)
        dst = self.rows[r][:, 512 * half:512 * half + 512]
        copy = self.nc.scalar.copy if half == 0 else self.nc.vector.tensor_copy
        copy(dst, self.banks[n % 4][:, :]).then_inc(self.copied[half], 1)

    def send(self, sp):
        for t in range(QT):
            for half in range(2):
                sp.wait_ge(self.copied[half], t + 1)
            r = t % len(self.rows)
            sp.dma_start(self.g.dram["out"][t * P:(t + 1) * P, :], self.rows[r][:, 0:D]).then_inc(self.stored[r], 16)
        for r in range(len(self.rows)):
            sp.wait_ge(self.stored[r], 16 * len(range(r, QT, len(self.rows))))


def ffn_phase(nc, g, tag, d_blocks, gain_col, chunks, first=False):
    groups = FT // 2
    C = len(chunks)
    U = 2 * C
    V = KD * C
    n_blocks = 3 * FT
    with ExitStack() as s:
        sb = lambda n, sh, dt=F32: s.enter_context(nc.sbuf_tensor(f"{tag}_{n}", sh, dt))
        sem = lambda n: g.semaphore(f"{tag}_{n}")
        raw = sb("raw", [P, 3, D])
        w_hi = sb("w_hi", [P, 6, D], F32R)
        w_lo = sb("w_lo", [P, 6, D], F32R)
        hid_hi = sb("hid_hi", [P, 2, 2, T], F32R)
        hid_lo = sb("hid_lo", [P, 2, 2, T], F32R)
        work = sb("work", [P, 4, T // 2])
        silu, h32 = work[:, 0:2, :], work[:, 2, :]
        bank = [s.enter_context(nc.psum_tensor(f"{tag}_bank{i}", [P, 512], F32)) for i in range(8)]
        raw_in = [sem(f"raw_in{i}") for i in range(3)]
        whi_done, wlo_done = sem("whi_done"), sem("wlo_done")
        gate_ready, up_ready, silu_done, h32_done = sem("gate_ready"), sem("up_ready"), sem("silu_done"), sem("h32_done")
        hid_hi_done, hid_done = sem("hid_hi_done"), sem("hid_done")
        down_ready, down_added = sem("down_ready"), sem("down_added")
        u32 = [work[:, j, :] for j in range(4)]
        norm = Norm(nc, g, f"{tag}_norm", s, gain_col, chunks, bank[4:4 + C + 1], u32, from_ssum=first)
        squares = [work[:, 2 * j:2 * j + 2, :].rearrange("p a b -> p (a b)") for j in range(2)]
        store = None if first else Store(nc, g, bank[0:4], [raw[:, j, :] for j in range(3)] + squares)
        square_sum = SquareSum(nc, g, tag, slice(0, T), squares) if first else None
        block = s.enter_context(nc.Block())

        @block.sync
        def _(sp):
            for n in range(3):
                sp.dma_start(raw[:, n, :], d_blocks[n]).then_inc(raw_in[n], 16)
            with sp.Fori(1, n_blocks // 3) as r:
                for n in range(3):
                    sp.wait_ge(wlo_done, 3 * r + (n - 2))
                    sp.dma_start(raw[:, n, :], d_blocks[3 * r + n]).then_inc(raw_in[n], 16)
            if store:
                store.send(sp)

        def gu_block(i, j):
            return j if isinstance(i, int) and i == 0 else 6 * i + (j - 2)

        def d_block(i, j):
            last = isinstance(i, int) and i == groups - 1
            return 6 * i + (j + 4 if last else j + 8)

        def down_order(store):
            if store:
                return [(d, c) for c in range(C) for d in range(KD)]
            return [(d, c) for d in range(KD) for c in range(C)]

        @block.scalar
        def _(act):
            def split_hi(n_rem, slot, times):
                act.wait_ge(raw_in[n_rem], 16 * times)
                nc.scalar.copy(w_hi[:, slot, :], raw[:, n_rem, :]).then_inc(whi_done, 1)

            def split_gu(i, f):
                act.wait_ge(up_ready, U * i + (C * (f + 1) - U))
                for j in (2 * f, 2 * f + 1):
                    split_hi((j - 2) % 3, j, 2 * i + ((j - 2) // 3 + 1))

            def split_d(i):
                last = isinstance(i, int) and i == groups - 1
                if last:
                    act.wait_ge(up_ready, U * i + C)
                elif not (isinstance(i, int) and i == 0):
                    act.wait_ge(down_ready, V * i)
                for j in range(2):
                    m = j + (4 if last else 8)
                    split_hi(m % 3, j if last else 4 + j, 2 * i + (m // 3 + 1))

            def group(i, more, parity_first=False):
                for f in range(2):
                    for c, (t0, n) in enumerate(chunks):
                        u = C * f + c
                        act.wait_ge(gate_ready, U * i + (u + 1))
                        if not (parity_first and u < 2):
                            act.wait_ge(h32_done, U * i + (u - 1))
                        nc.scalar.activation(silu[:, u % 2, 0:n], bank[2 * (u % 2)][:, 0:n],
                                             ACT.Silu).then_inc(silu_done, 1)
                    if more:
                        split_gu(i + 1, f)

            norm.act_root(act)
            for c in range(max(C, 3)):
                split_hi(c, c, 1)
                if c < C:
                    norm.act_hi(act, c)
            split_hi(0, 3, 2)
            norm.wait_lo(act, KD * C)
            group(0, True, parity_first=True)
            split_d(0)
            group(1, True)
            with act.Fori(2, groups - 1) as i:
                split_d(i - 1)
                group(i, True)
            split_d(groups - 2)
            group(groups - 1, False)
            split_d(groups - 1)
            if store:
                act.wait_ge(wlo_done, n_blocks)
                for t in range(QT):
                    store.copy_half(act, t, 0)
            if square_sum:
                for d in range(KD):
                    act.wait_ge(down_added, V * (groups - 1) + C * (d + 1))
                    square_sum.square(act, d)

        @block.gpsimd
        def _(pool):
            def split_lo(n, slot, raw_slot):
                pool.wait_ge(whi_done, n + 1)
                nc.gpsimd.tensor_tensor(w_lo[:, slot, :], raw[:, raw_slot, :], w_hi[:, slot, :].bitcast(F32),
                                        ALU.subtract).then_inc(wlo_done, 1)
            for n in range(4):
                split_lo(n, n, n % 3)
                if n < C:
                    norm.pool_lo(pool, n)
            with pool.Fori(1, groups) as i:
                for j in range(6):
                    split_lo(6 * i + (j - 2), j, (j - 2) % 3)
            for j in range(2):
                split_lo(n_blocks - 2 + j, j, (n_blocks - 2 + j) % 3)

        @block.tensor
        def _(pe):
            def gate_up(i, first=False):
                for f in range(2):
                    for c, (t0, n) in enumerate(chunks):
                        u = C * f + c
                        for which, ready, freed in ((0, gate_ready, silu_done), (1, up_ready, h32_done)):
                            slot = 2 * f + which
                            if c == 0:
                                pe.wait_ge(wlo_done, gu_block(i, slot) + 1)
                            if first and f == 0 and which == 0:
                                norm.wait_chunk(pe, c)
                            if not (first and u < 2):
                                pe.wait_ge(freed, U * i + (u - 1))
                            out = bank[2 * (u % 2) + which]
                            for k in range(KD):
                                last = mm3(nc, out[:, 0:n], w_hi[:, slot, k * P:(k + 1) * P],
                                           w_lo[:, slot, k * P:(k + 1) * P], g.u_hi[:, k, t0:t0 + n],
                                           g.u_lo[:, k, t0:t0 + n], k == 0, k == KD - 1)
                            last.then_inc(ready, 1)

            def down(i, parity, first=False, slot=4, store=None):
                pe.wait_ge(hid_done, U * i + U)
                pe.wait_ge(wlo_done, d_block(i, 1) + 1)
                for v, (d, c) in enumerate(down_order(store)):
                    t0, n = chunks[c]
                    if not (first and v < 4):
                        pe.wait_ge(down_added, V * i + (v - 3))
                    for f in range(2):
                        last = mm3(nc, bank[4 + v % 4][:, 0:n], w_hi[:, slot + f, d * P:(d + 1) * P],
                                   w_lo[:, slot + f, d * P:(d + 1) * P], hid_hi[:, parity, f, t0:t0 + n],
                                   hid_lo[:, parity, f, t0:t0 + n], f == 0, f == 1)
                    last.then_inc(down_ready, 1)
                    if store and c == 1 and d % 2:
                        pe.wait_ge(down_added, V * i + KD)
                        store.turn(pe, d // 2)

            norm.pe_broadcast(pe)
            gate_up(0, first=True)
            gate_up(1)
            down(0, 0, first=True)
            with pe.Fori(2, groups - 1, 2) as i:
                gate_up(i)
                down(i - 1, 1)
                gate_up(i + 1)
                down(i, 0)
            gate_up(groups - 1)
            down(groups - 2, 1)
            down(groups - 1, 0, slot=0, store=store)
            if store:
                pe.wait_ge(down_added, V * groups)
                for t in range(QT // 2, QT):
                    store.turn(pe, t)

        @block.vector
        def _(dve):
            def hidden(i, parity, first=False, reuse=True):
                if reuse:
                    dve.wait_ge(down_ready, V * (i - 1))
                for f in range(2):
                    for c, (t0, n) in enumerate(chunks):
                        u = C * f + c
                        dve.wait_ge(silu_done, U * i + (u + 1))
                        dve.wait_ge(up_ready, U * i + (u + 1))
                        if not (first and u == 0):
                            dve.wait_ge(hid_done, U * i + u)
                        nc.vector.tensor_tensor(h32[:, 0:n], silu[:, u % 2, 0:n], bank[2 * (u % 2) + 1][:, 0:n],
                                                ALU.mult).then_inc(h32_done, 1)
                        dve.wait_ge(h32_done, U * i + (u + 1))
                        nc.vector.tensor_copy(hid_hi[:, parity, f, t0:t0 + n], h32[:, 0:n]).then_inc(hid_hi_done, 1)
                        dve.wait_ge(hid_hi_done, U * i + (u + 1))
                        nc.vector.tensor_tensor(hid_lo[:, parity, f, t0:t0 + n], h32[:, 0:n],
                                                hid_hi[:, parity, f, t0:t0 + n].bitcast(F32),
                                                ALU.subtract).then_inc(hid_done, 1)

            def add_down(i, first=False, sum_squares=None, store=None):
                for v, (d, c) in enumerate(down_order(store)):
                    t0, n = chunks[c]
                    dve.wait_ge(down_ready, V * i + (v + 1))
                    if not first:
                        dve.wait_ge(down_added, V * i + (v + 1 - V if store is None else 0))
                    nc.vector.scalar_tensor_tensor(g.h[:, d, t0:t0 + n], bank[4 + v % 4][:, 0:n], 0.5,
                                                   g.h[:, d, t0:t0 + n], ALU.mult, ALU.add).then_inc(down_added, 1)
                    if sum_squares and d and c == C - 1:
                        sum_squares.add(dve, d - 1)
                    if store and c == 1 and d % 2 and d > 1:
                        store.copy_half(dve, d // 2 - 1, 1)
                if sum_squares:
                    sum_squares.add(dve, KD - 1)
                if store:
                    for t in range(QT // 2 - 1, QT):
                        store.copy_half(dve, t, 1)

            norm.dve(dve)
            hidden(0, 0, first=True, reuse=False)
            hidden(1, 1, reuse=False)
            add_down(0, first=True)
            with dve.Fori(2, groups - 1, 2) as i:
                hidden(i, 0)
                add_down(i - 1)
                hidden(i + 1, 1)
                add_down(i)
            hidden(groups - 1, 0)
            add_down(groups - 2)
            add_down(groups - 1, sum_squares=square_sum, store=store)


def wait(eng, sem, p, per_pair, more):
    if isinstance(p, int):
        if per_pair * p + more > 0:
            eng.wait_ge(sem, per_pair * p + more)
    else:
        eng.wait_ge(sem, per_pair * p + more)


def over_pairs(eng, body):
    body(0)
    with eng.Fori(1, PAIRS - 1) as p:
        body(p)
    body(PAIRS - 1, last=True)


QK_TOKENS = [(0, 384), (384, 384), (768, 272)]
QK_TILES = [(0, 128, 256), (0, 128, 256), (0, 128, 144)]
LO_DVE = 4


def lo_counts(units_done):
    return units_done - units_done // LO_DVE, units_done // LO_DVE


ST_UNITS = []
for _c, (_q0, _n) in enumerate(REAL_TOKENS):
    for _kt in range(9):
        _a = max(_q0, P * _kt)
        if _a < _q0 + _n:
            ST_UNITS.append((_c, _kt, min(P * _kt, T - P), _a, _q0 + _n - _a))
NW = len(ST_UNITS)
LAST_OF = [max(w for w in range(NW) if ST_UNITS[w][0] == c) for c in range(2)]

MAX_UNITS = []
for _i in range(QT):
    _end = META + P * (_i + 1)
    _cuts = [0] + [x for x in (400, 912) if x < _end] + [_end]
    for _j in range(len(_cuts) - 1):
        MAX_UNITS.append((_i, _j, _cuts[_j], _cuts[_j + 1] - _cuts[_j]))
NM = len(MAX_UNITS)
SHORT = sum(1 for _u in MAX_UNITS if META + P * (_u[0] + 1) <= QK_TOKENS[2][0])


def forget_phase(nc, g):
    with ExitStack() as s:
        sb = lambda n, sh, dt=F32: s.enter_context(nc.sbuf_tensor("fg_" + n, sh, dt))
        sem = lambda n: g.semaphore("fg_" + n)
        raw = sb("raw", [P, D])
        w_hi, w_lo = sb("w_hi", [P, D], F32R), sb("w_lo", [P, D], F32R)
        cf = sb("cf", [P, 2 * P + META])
        out = sb("out", [P, T])
        mag, lse, zmin = sb("mag", [HEADS, T]), sb("lse", [HEADS, T]), sb("zmin", [HEADS, T])
        one, cum = sb("one", [HEADS, T]), sb("cum", [HEADS, T])
        c_hi, c_lo = sb("c_hi", [HEADS, T], F32R), sb("c_lo", [HEADS, T], F32R)
        acc = [s.enter_context(nc.psum_tensor(f"fg_acc{i}", [P, 512], F32)) for i in range(3)]
        norm_banks = [s.enter_context(nc.psum_tensor(f"fg_norm_bank{i}", [P, 512], F32)) for i in range(4)]
        u32 = sb("u32", [P, 4, 348])
        norm = Norm(nc, g, "fg_norm", s, g.MIX_GAIN, ALL_TOKENS, norm_banks, [u32[:, j, :] for j in range(4)],
                    from_ssum=False)
        h_out, w_in, const_in, spilled = sem("h_out"), sem("w_in"), sem("const_in"), sem("spilled")
        const_done, whi, wlo, ready, copied = sem("const_done"), sem("whi"), sem("wlo"), sem("ready"), sem("copied")
        step_a, step_v, signed = sem("step_a"), sem("step_v"), sem("signed")
        block = s.enter_context(nc.Block())

        @block.sync
        def _(sp):
            sp.dma_start(raw[:, :], g.dram["misc"][0]).then_inc(w_in, 16)
            sp.dma_start(cf[:, :], g.dram["masks"][:, 0:2 * P + META]).then_inc(const_in, 16)
            sp.dma_start(g.head_sum[:, :], g.dram["masks"][:, 2 * P + META:3 * P + META]).then_inc(const_in, 16)
            sp.dma_start(g.rot[:, :], g.dram["masks"][:, 3 * P + META:4 * P + META]).then_inc(const_in, 16)
            sp.dma_start(g.dram["hsave"], g.h[:, :, :]).then_inc(h_out, 16)
            sp.wait_ge(copied, 3)
            sp.dma_start(g.dram["krope"], out[NOPE:MLA_D, :]).then_inc(spilled, 16)
            sp.wait_ge(step_v, 4)
            sp.dma_start(g.dram["cum"][0], c_hi[:, :].bitcast(F32)).then_inc(spilled, 16)
            sp.dma_start(g.dram["cum"][1], c_lo[:, :].bitcast(F32)).then_inc(spilled, 16)
            sp.wait_ge(spilled, 48)
            sp.wait_ge(h_out, 16)

        @block.scalar
        def _(act):
            norm.act_root(act)
            act.preload_act_table_set("natural_log_exp_and_others")
            act.wait_ge(w_in, 16)
            nc.scalar.copy(w_hi[:, :], raw[:, :]).then_inc(whi, 1)
            for c in range(3):
                norm.act_hi(act, c)
            act.wait_ge(const_in, 48)
            nc.scalar.copy(g.ident_r[:, :], g.ident[:, :]).then_inc(const_done, 1)
            nc.scalar.copy(g.masks[:, :], cf[:, :]).then_inc(const_done, 1)
            bias = g.gains[0:HEADS, g.BF_COL:g.BF_COL + 1]
            for c, (t0, n) in enumerate(ALL_TOKENS):
                x = slice(t0, t0 + n)
                act.wait_ge(copied, c + 1)
                nc.scalar.activation(mag[:, x], out[0:HEADS, x], ACT.Abs, bias=bias).then_inc(step_a, 1)
                act.wait_ge(step_a, 3 * c + 1)
                nc.scalar.activation(mag[:, x], mag[:, x], ACT.Exp, scale=-1.0).then_inc(step_a, 1)
                act.wait_ge(step_a, 3 * c + 2)
                nc.scalar.activation(lse[:, x], mag[:, x], ACT.Ln, bias=g.ones[0:HEADS, 0:1]).then_inc(step_a, 1)

        @block.gpsimd
        def _(pool):
            pool.wait_ge(whi, 1)
            nc.gpsimd.tensor_tensor(w_lo[:, :], raw[:, :], w_hi[:, :].bitcast(F32), ALU.subtract).then_inc(wlo, 1)
            for c in range(3):
                norm.pool_lo(pool, c)

        @block.tensor
        def _(pe):
            norm.pe_broadcast(pe)
            pe.wait_ge(wlo, 1)
            for c, (t0, n) in enumerate(ALL_TOKENS):
                norm.wait_chunk(pe, c)
                for k in range(KD):
                    last = mm3(nc, acc[c][:, 0:n], w_hi[:, k * P:(k + 1) * P], w_lo[:, k * P:(k + 1) * P],
                               g.u_hi[:, k, t0:t0 + n], g.u_lo[:, k, t0:t0 + n], k == 0, k == KD - 1)
                last.then_inc(ready, 1)

        @block.vector
        def _(dve):
            nc.vector.memset(one[:, :], 1.0).then_inc(step_v, 1)
            norm.dve(dve)
            for c, (t0, n) in enumerate(ALL_TOKENS):
                x = slice(t0, t0 + n)
                dve.wait_ge(ready, c + 1)
                nc.vector.tensor_copy(out[:, x], acc[c][:, 0:n]).then_inc(copied, 1)
                dve.wait_ge(copied, c + 1)
                nc.vector.tensor_scalar(zmin[:, x], out[0:HEADS, x], g.gains[0:HEADS, g.BF_COL:g.BF_COL + 1], 0.0,
                                        ALU.add, ALU.min).then_inc(signed, 1)
                dve.wait_ge(signed, 2 * c + 1)
                dve.wait_ge(step_a, 3 * (c + 1))
                nc.vector.tensor_tensor(zmin[:, x], lse[:, x], zmin[:, x], ALU.subtract).then_inc(signed, 1)
            dve.wait_ge(signed, 6)
            nc.vector.tensor_tensor_scan(cum[:, :], one[:, :], zmin[:, :], 0.0, ALU.mult, ALU.add).then_inc(step_v, 1)
            dve.wait_ge(step_v, 2)
            nc.vector.tensor_copy(c_hi[:, :], cum[:, :]).then_inc(step_v, 1)
            dve.wait_ge(step_v, 3)
            nc.vector.tensor_tensor(c_lo[:, :], cum[:, :], c_hi[:, :].bitcast(F32), ALU.subtract).then_inc(step_v, 1)


def latent_phase(nc, g):
    with ExitStack() as s:
        sb = lambda n, sh, dt=F32: s.enter_context(nc.sbuf_tensor("lt_" + n, sh, dt))
        sem = lambda n: g.semaphore("lt_" + n)
        raw = sb("raw", [P, 3, D])
        w_hi, w_lo = sb("w_hi", [P, 3, D], F32R), sb("w_lo", [P, 3, D], F32R)
        sq = sb("sq", [P, 2, 348])
        rs = sb("rs", [P, 2, 348])
        kr = sb("kr", [P, T])
        t1 = sb("t1", [P, 348])
        bank = [s.enter_context(nc.psum_tensor(f"lt_bank{i}", [P, 512], F32)) for i in range(8)]
        KR = bank[5:8]
        w_in = [sem(f"w_in{i}") for i in range(3)]
        const_in, whi, wlo, wlo_dve = sem("const_in"), sem("whi"), sem("wlo"), sem("wlo_dve")
        ready, squared, summed, logged, rooted, normed = (sem("ready"), sem("squared"), sem("summed"),
                                                          sem("logged"), sem("rooted"), sem("normed"))
        ksq_done = sem("ksq_done")
        kr_gained, kr_turned, kr_steps = sem("kr_gained"), sem("kr_turned"), sem("kr_steps")
        block = s.enter_context(nc.Block())
        C = ALL_TOKENS

        @block.sync
        def _(sp):
            for j in range(3):
                sp.dma_start(raw[:, j, :], g.dram["misc"][1 + j]).then_inc(w_in[j], 16)
            sp.dma_start(kr[NOPE:MLA_D, :], g.dram["krope"]).then_inc(const_in, 16)
            sp.dma_start(g.cos[NOPE:MLA_D, :], g.dram["cos"]).then_inc(const_in, 16)
            sp.dma_start(g.sin[NOPE:MLA_D, :], g.dram["sin"]).then_inc(const_in, 16)
            sp.wait_ge(const_in, 48)

        @block.gpsimd
        def _(pool):
            for j in range(1, 3):
                pool.wait_ge(whi, j + 1)
                nc.gpsimd.tensor_tensor(w_lo[:, j, :], raw[:, j, :], w_hi[:, j, :].bitcast(F32),
                                        ALU.subtract).then_inc(wlo, 1)

        @block.tensor
        def _(pe):
            for c, (t0, n) in enumerate(C):
                for j in range(3):
                    if j == 0:
                        pe.wait_ge(wlo_dve, 1)
                    else:
                        pe.wait_ge(wlo, j)
                    if c:
                        pe.wait_ge(normed, 3 * (c - 1) + j + 1)
                    for k in range(KD):
                        last = mm3(nc, bank[j][:, 0:n], w_hi[:, j, k * P:(k + 1) * P],
                                   w_lo[:, j, k * P:(k + 1) * P], g.u_hi[:, k, t0:t0 + n],
                                   g.u_lo[:, k, t0:t0 + n], k == 0, k == KD - 1)
                    last.then_inc(ready, 1)
                if c == 0:
                    pe.wait_ge(kr_gained, 1)
                    for i, (k0, m) in enumerate(C):
                        nc.tensor.matmul(KR[i][0:MLA_D, 0:m], g.rot[NOPE:MLA_D, 0:MLA_D], kr[NOPE:MLA_D, k0:k0 + m],
                                         start=True, stop=True).then_inc(kr_turned, 1)
                for j in range(3):
                    pe.wait_ge(squared, 3 * c + j + 1)
                    if c and j < 2:
                        pe.wait_ge(logged, 2 * c - 1 + j)
                    dst = bank[3 if j == 0 else 4]
                    nc.tensor.matmul(dst[:, 0:n], g.ones[:, :], sq[:, (3 * c + j) % 2, 0:n], start=(j != 2),
                                     stop=(j != 1)).then_inc(summed, 1)

        @block.scalar
        def _(act):
            act.preload_act_table_set("natural_log_exp_and_others")
            for j in range(3):
                act.wait_ge(w_in[j], 16)
                nc.scalar.copy(w_hi[:, j, :], raw[:, j, :]).then_inc(whi, 1)
            act.wait_ge(const_in, 48)
            nc.scalar.activation(g.ksq[NOPE:MLA_D, :], kr[NOPE:MLA_D, :], ACT.Square).then_inc(ksq_done, 1)
            for c, (t0, n) in enumerate(C):
                for j in range(3):
                    act.wait_ge(ready, 3 * c + j + 1)
                    if 3 * c + j >= 2:
                        act.wait_ge(summed, 3 * c + j - 1)
                    nc.scalar.activation(sq[:, (3 * c + j) % 2, 0:n], bank[j][:, 0:n], ACT.Square).then_inc(squared, 1)
                for r in range(2):
                    act.wait_ge(summed, 3 * c + (1 if r == 0 else 3))
                    if c:
                        act.wait_ge(normed, 3 * (c - 1) + (1 if r == 0 else 3))
                    nc.scalar.activation(rs[:, r, 0:n], bank[3 + r][:, 0:n], ACT.Ln,
                                         scale=1.0 / (CKV if r == 0 else CQ),
                                         bias=g.gains[:, g.EPS_COL:g.EPS_COL + 1]).then_inc(logged, 1)
                    act.wait_ge(logged, 2 * c + r + 1)
                    nc.scalar.activation(rs[:, r, 0:n], rs[:, r, 0:n], ACT.Exp, scale=-0.5).then_inc(rooted, 1)

        @block.vector
        def _(dve):
            dve.wait_ge(whi, 1)
            nc.vector.tensor_tensor(w_lo[:, 0, :], raw[:, 0, :], w_hi[:, 0, :].bitcast(F32),
                                    ALU.subtract).then_inc(wlo_dve, 1)
            dve.wait_ge(const_in, 48)
            dve.wait_ge(ksq_done, 1)
            gk = g.gains[NOPE:MLA_D, g.MK_COL:g.MK_COL + 1]
            nc.vector.tensor_scalar(kr[NOPE:MLA_D, :], kr[NOPE:MLA_D, :], gk, None, ALU.mult).then_inc(kr_gained, 1)
            dve.wait_ge(kr_gained, 1)
            for c, (t0, n) in enumerate(C):
                r = slice(NOPE, MLA_D)
                nc.vector.tensor_tensor(g.krope[r, t0:t0 + n], kr[r, t0:t0 + n], g.cos[r, t0:t0 + n],
                                        ALU.mult).then_inc(kr_steps, 1)
                dve.wait_ge(kr_turned, c + 1)
                nc.vector.tensor_tensor(t1[r, 0:n], KR[c][r, 0:n], g.sin[r, t0:t0 + n], ALU.mult).then_inc(kr_steps, 1)
                dve.wait_ge(kr_steps, 3 * c + 2)
                nc.vector.tensor_tensor(g.krope[r, t0:t0 + n], g.krope[r, t0:t0 + n], t1[r, 0:n],
                                        ALU.add).then_inc(kr_steps, 1)
                dve.wait_ge(kr_steps, 3 * c + 3)
            for c, (t0, n) in enumerate(C):
                for j in range(3):
                    dve.wait_ge(rooted, 2 * c + (1 if j == 0 else 2))
                    dst = g.ckv[:, t0:t0 + n] if j == 0 else g.cq[:, j - 1, t0:t0 + n]
                    nc.vector.scalar_tensor_tensor(dst, bank[j][:, 0:n],
                                                   g.gains[:, g.CN_COL + j:g.CN_COL + j + 1],
                                                   rs[:, 0 if j == 0 else 1, 0:n], ALU.mult, ALU.mult).then_inc(normed, 1)


def fox_attention_phase(nc, g):
    DK = FOX_D
    KMAX, KALL = DK + 2, DK + 4
    NU = 6
    NH = 2
    with ExitStack() as s:
        sb = lambda n, sh, dt=F32: s.enter_context(nc.sbuf_tensor(f"fox_{n}", sh, dt))
        sem = lambda n: g.semaphore(f"fox_{n}")
        q_hi = [sb(f"q_hi{i}", [KALL, T], F32R) for i in range(2)]
        q_lo = [sb(f"q_lo{i}", [DK, T], F32R) for i in range(2)]
        k_hi = [sb(f"k_hi{i}", [KALL, T], F32R) for i in range(2)]
        k_lo = [sb(f"k_lo{i}", [DK, T], F32R) for i in range(2)]
        v_hi, v_lo = sb("v_hi", [P, 9, 3 * VD], F32R), sb("v_lo", [P, 9, 3 * VD], F32R)
        p32 = sb("p32", [P, 2, 512])
        p_hi, p_lo = sb("p_hi", [P, 3, 512], F32R), sb("p_lo", [P, 3, 512], F32R)
        rs = sb("rs", [P, 2, 384])
        x32 = sb("x32", [FOX_D, 4, 384])
        rden = sb("rden", [P, 512])
        ms, r0, nt = sb("ms", [P, 2, 3 * NH]), sb("r0", [P, 2, 3 * NH]), sb("nt", [P, 2, 3 * NH])
        threes = sb("threes", [P, 3 * NH])
        mpart, nm = sb("mpart", [P, QT, 3]), sb("nm", [P, P])
        m_hi, m_lo = sb("m_hi", [QT, P], F32R), sb("m_lo", [QT, P], F32R)
        vt = sb("vt", [P, T])
        r_wide = sb("r_wide", [P, 2, 3 * NH, FOX_D])
        raw = sb("raw", [P, 3, D])
        w_hi, w_lo = sb("w_hi", [P, 3, D], F32R), sb("w_lo", [P, 3, D], F32R)
        bank = [s.enter_context(nc.psum_tensor(f"fox_bank{i}", [P, 512], F32)) for i in range(8)]
        PROJ, SUM, BC = (bank[0], bank[1], bank[4], bank[5]), bank[2], bank[6:8]
        V_PROJ = (bank[4], bank[5], bank[4])
        VB, MAXB, MT = bank[6:8], (bank[3], bank[0]), bank[1]
        ST, OB = (bank[2], bank[4], bank[5]), bank[6:8]

        small_set, rows_set, ones_set = sem("small_set"), sem("rows_set"), sem("ones_set")
        raw_in = [sem(f"raw_in{i}") for i in range(3)]
        whi_done, wlo_done = sem("whi_done"), sem("wlo_done")
        cum_in, m_in = sem("cum_in"), sem("m_in")
        proj_ready, squared, sum_ready, ms_done, logged, rooted, newton = (
            sem("proj_ready"), sem("squared"), sem("sum_ready"), sem("ms_done"), sem("logged"), sem("rooted"),
            sem("newton"))
        bc_ready, rs_done = sem("bc_ready"), sem("rs_done")
        x_done, xhi_done, qk_done = sem("x_done"), sem("xhi_done"), sem("qk_done")
        vt_done, v_ready, v32_done, vhi_done, v_done = (sem("vt_done"), sem("v_ready"), sem("v32_done"),
                                                        sem("vhi_done"), sem("v_done"))
        max_ready, max_read, nm_done, mt_ready, mhi_done, m_done = (sem("max_ready"), sem("max_read"),
                                                                    sem("nm_done"), sem("mt_ready"),
                                                                    sem("mhi_done"), sem("m_done"))
        st_ready, exp_done, phi_done, plo_pool, plo_dve, pv_done = (sem("st_ready"), sem("exp_done"),
                                                                    sem("phi_done"), sem("plo_pool"),
                                                                    sem("plo_dve"), sem("pv_done"))
        ln_done, rden_done, o_done = sem("ln_done"), sem("rden_done"), sem("o_done")
        block = s.enter_context(nc.Block())
        PW, PM = 2 * NW, 2 * NM
        LO_P, LO_V = lo_counts(PW)

        def wait_split(eng, p, units_done):
            by_pool, by_dve = lo_counts(units_done) if units_done > 0 else (0, 0)
            wait(eng, plo_pool, p, LO_P, by_pool)
            wait(eng, plo_dve, p, LO_V, by_dve)

        W_HI_AT, W_LO_AT = [2, 5, 8, 11, 14, 17], [4, 7, 10, 13, 16, 19]
        units = [(is_q, c) for c in range(3) for is_q in (True, False)]
        NPROJ = NU + 3
        EARLY = 7
        OPEN_AT = (2, 4, 6)
        finish_after = {}
        for h in range(2):
            for c in range(2):
                finish_after.setdefault(min(NW * h + LAST_OF[c] + 4, PW - 1), []).append((h, c))

        def v_columns(v, b):
            return v[:, 3 * b:3 * b + 3, :].rearrange("p t (a b) -> p t a b", a=3)[:, :, 0:3:2, :]

        def v_of_p32(b):
            return p32[:, b % 2, 0:3 * P].rearrange("p (t a b) -> p t a b", t=3, a=2)

        @block.sync
        def _(sp):
            def weights(p):
                for j in range(3):
                    wait(sp, wlo_done, p, 6, 2 * j - 4)
                    sp.dma_start(raw[:, j, :], g.dram["fox"][3 * p + j]).then_inc(raw_in[j], 16)

            def pair(p, last=False):
                for h in range(2):
                    wait(sp, pv_done, p, PW, 0)
                    sp.wait_ge(rows_set, 4)
                    sp.dma_start(k_hi[h][DK:DK + 2, :].bitcast(F32),
                                 g.dram["cum"][:, 2 * p + h, :]).then_inc(cum_in, 16)
                if not last:
                    weights(p + 1)
                for h in range(2):
                    wait(sp, m_done, p, 2, h + 1)
                    for src, r in ((m_hi, KMAX), (m_lo, KMAX + 1)):
                        sp.dma_start(q_hi[h][r:r + 1, META:T].bitcast(F32).rearrange("o (a b) -> o a b", a=QT),
                                     src[:, :].bitcast(F32)).then_inc(m_in, 16)
            weights(0)
            over_pairs(sp, pair)

        @block.gpsimd
        def _(pool):
            for i, x in enumerate((k_hi[0], k_hi[1], q_hi[0], q_hi[1])):
                if i:
                    pool.wait_ge(rows_set, i)
                nc.gpsimd.memset(x[DK:KALL, :].bitcast(F32), 1.0).then_inc(rows_set, 1)
            pool.wait_ge(rows_set, 4)
            pool.wait_ge(small_set, 1)

            def pair(p, last=False):
                for u in range(NU):
                    r, m, t = r0[:, u % 2, :], ms[:, u % 2, :], nt[:, u % 2, :]
                    wait(pool, rooted, p, NU, u + 1)
                    nc.gpsimd.tensor_tensor(t, m, r, ALU.mult).then_inc(newton, 1)
                    wait(pool, newton, p, 4 * NU, 4 * u + 1)
                    nc.gpsimd.tensor_tensor(t, t, r, ALU.mult).then_inc(newton, 1)
                    wait(pool, newton, p, 4 * NU, 4 * u + 2)
                    nc.gpsimd.tensor_tensor(t, threes[:, :], t, ALU.subtract).then_inc(newton, 1)
                    wait(pool, newton, p, 4 * NU, 4 * u + 3)
                    wait(pool, bc_ready, p, NU, u - 1)
                    wide = [P, 3 * NH, FOX_D]
                    nc.gpsimd.tensor_tensor(r_wide[:, u % 2], r.unsqueeze(2).broadcast_to(wide),
                                            t.unsqueeze(2).broadcast_to(wide), ALU.mult).then_inc(newton, 1)
                for b in range(3):
                    wait(pool, vhi_done, p, 3, b + 1)
                    nc.gpsimd.tensor_tensor(v_columns(v_lo, b), v_of_p32(b), v_columns(v_hi, b).bitcast(F32),
                                            ALU.subtract).then_inc(v_done, 1)
                for w in range(PW):
                    if w % LO_DVE == LO_DVE - 1:
                        continue
                    n = ST_UNITS[w % NW][4]
                    wait(pool, phi_done, p, PW, w + 1)
                    nc.gpsimd.tensor_tensor(p_lo[:, w % 3, 0:n], p32[:, w % 2, 0:n], p_hi[:, w % 3, 0:n].bitcast(F32),
                                            ALU.subtract).then_inc(plo_pool, 1)
            over_pairs(pool, pair)

        @block.scalar
        def _(act):
            def weights_hi(p, i):
                j, x = i // 2, slice(512 * (i % 2), 512 * (i % 2) + 512)
                act.wait_ge(raw_in[j], 16 * (p + 1))
                wait(act, proj_ready, p, NPROJ, 0)
                nc.scalar.copy(w_hi[:, j, x], raw[:, j, x]).then_inc(whi_done, 1)

            def pair(p, last=False):
                def evacuate_v(c):
                    t0, n = QK_TOKENS[c]
                    wait(act, proj_ready, p, NPROJ, NU + c + 1)
                    wait(act, v_ready, p, 3, 0)
                    nc.scalar.copy(vt[:, t0:t0 + n], V_PROJ[c][:, 0:n]).then_inc(vt_done, 1)

                def split_hi(u):
                    is_q, c = units[u]
                    t0, n = QK_TOKENS[c]
                    wait(act, x_done, p, NU, u + 1)
                    wait(act, pv_done, p, PW, 0)
                    for j in range(2):
                        last = nc.scalar.copy((q_hi if is_q else k_hi)[j][0:FOX_D, t0:t0 + n],
                                              x32[:, 2 * (u % 2) + j, 0:n])
                    last.then_inc(xhi_done, 1)

                for s_ in range(NU + 2):
                    if 0 <= s_ - 3 < NU - 2:
                        split_hi(s_ - 3)
                    u = s_
                    if u < NU:
                        is_q, c = units[u]
                        t0, n = QK_TOKENS[c]
                        src = PROJ[u % 4]
                        wait(act, proj_ready, p, NPROJ, u + 1)
                        wait(act, sum_ready, p, NU, u - 1)
                        if u < 2:
                            wait_split(act, p, 0)
                        nc.scalar.activation(p32[:, u % 2, 0:n], src[:, 0:n], ACT.Square).then_inc(squared, 1)
                    u = s_ - 1
                    if 0 <= u < NU:
                        wait(act, ms_done, p, NU, u + 1)
                        wait(act, bc_ready, p, NU, u - 1)
                        nc.scalar.activation(r0[:, u % 2, :], ms[:, u % 2, :], ACT.Ln).then_inc(logged, 1)
                        wait(act, logged, p, NU, u + 1)
                        nc.scalar.activation(r0[:, u % 2, :], r0[:, u % 2, :], ACT.Exp, scale=-0.5).then_inc(rooted, 1)
                    u = s_ - 2
                    if u >= 0:
                        n = QK_TOKENS[units[u][1]][1]
                        wait(act, bc_ready, p, NU, u + 1)
                        wait(act, x_done, p, NU, u - 1)
                        nc.scalar.copy(rs[:, u % 2, 0:n], BC[u % 2][:, 0:n]).then_inc(rs_done, 1)
                    if s_ >= NU:
                        split_hi(s_ - 2)
                    if s_ == NU:
                        evacuate_v(0)
                evacuate_v(1)
                for b in range(3):
                    if b == 1:
                        evacuate_v(2)
                    wait(act, v_ready, p, 3, b + 1)
                    wait(act, sum_ready, p, NU, NU)
                    wait(act, v_done, p, 3, b - 1)
                    nc.scalar.copy(p32[:, b % 2, 0:3 * P], VB[b % 2][:, 0:3 * P]).then_inc(v32_done, 1)
                    wait(act, v32_done, p, 3, b + 1)
                    nc.scalar.copy(v_columns(v_hi, b), v_of_p32(b)).then_inc(vhi_done, 1)

                for w in range(PW):
                    n = ST_UNITS[w % NW][4]
                    wait(act, st_ready, p, PW, w + 1)
                    if w < 2:
                        wait(act, v_done, p, 3, 3)
                    wait_split(act, p, w - 1)
                    nc.scalar.activation(p32[:, w % 2, 0:n], ST[w % 3][:, 0:n], ACT.Exp).then_inc(exp_done, 1)
                    for h, c in finish_after.get(w, ()):
                        rows, ones_rows = (slice(0, VD), slice(VD, P))[::1 if h == 0 else -1]
                        f = 2 * h + c
                        wait(act, pv_done, p, PW, NW * h + LAST_OF[c] + 1)
                        wait(act, o_done, p, 4, f)
                        nc.scalar.activation(rden[rows, :], OB[c][ones_rows, :], ACT.Ln).then_inc(ln_done, 1)
                        wait(act, ln_done, p, 4, f + 1)
                        nc.scalar.activation(rden[rows, :], rden[rows, :], ACT.Exp, scale=-1.0).then_inc(rden_done, 1)
                    if not last and w in W_HI_AT:
                        weights_hi(p + 1, W_HI_AT.index(w))
            act.preload_act_table_set("natural_log_exp_and_others")
            for i in range(6):
                weights_hi(0, i)
            over_pairs(act, pair)

        @block.tensor
        def _(pe):
            def pair(p, last=False):
                def products(u, between=None):
                    is_q, c = units[u] if u < NU else (None, u - NU)
                    t0, n = QK_TOKENS[c]
                    out = PROJ[u % 4] if u < NU else V_PROJ[c]
                    if u == 0:
                        wait(pe, max_read, p, PM, 0)
                    elif u == 1:
                        wait(pe, m_done, p, 2, 0)
                    elif u < 4:
                        wait(pe, exp_done, p, PW, 0)
                    elif u < NU + 2:
                        wait(pe, x_done, p, NU, u - 3)
                    else:
                        wait(pe, vt_done, p, 3, 1)
                    j = 2 if u >= NU else 0 if is_q else 1
                    if c == 0:
                        wait(pe, wlo_done, p, 6, 2 * j + 2)
                    for k in range(KD):
                        last = mm3(nc, out[:, 0:n], w_hi[:, j, k * P:(k + 1) * P], w_lo[:, j, k * P:(k + 1) * P],
                                   g.u_hi[:, k, t0:t0 + n], g.u_lo[:, k, t0:t0 + n], k == 0, k == KD - 1)
                        if k == KD - 1:
                            last.then_inc(proj_ready, 1)
                        if between:
                            between(u - NU, k)

                def sums(u):
                    is_q, c = units[u]
                    t0, n = QK_TOKENS[c]
                    wait(pe, squared, p, NU, u + 1)
                    wait(pe, ms_done, p, NU, u)
                    if u == 0:
                        wait(pe, exp_done, p, PW, 0)
                    for i, off in enumerate(QK_TILES[c]):
                        last = nc.tensor.matmul(SUM[:, NH * i:NH * i + NH], p32[:, u % 2, off:off + P],
                                                g.head_sum[:, 0:P:FOX_D], start=True, stop=True)
                    last.then_inc(sum_ready, 1)

                def broadcast(u):
                    c = units[u][1]
                    wait(pe, newton, p, 4 * NU, 4 * u + 4)
                    if u < 2:
                        wait(pe, o_done, p, 4, 0)
                    else:
                        wait(pe, rs_done, p, NU, u - 1)
                    for i, off in enumerate(QK_TILES[c]):
                        r = r_wide[:, u % 2, NH * i:NH * i + NH, :].rearrange("p a b -> p (a b)")
                        last = nc.tensor.matmul(BC[u % 2][:, off:off + P], r, g.ident[:, :], start=True, stop=True)
                    last.then_inc(bc_ready, 1)

                def values(b):
                    if b < 2:
                        wait(pe, rs_done, p, NU, NU)
                    else:
                        wait(pe, v32_done, p, 3, b - 1)
                    wait(pe, vt_done, p, 3, b + 1)
                    for i in range(3):
                        tok = min(P * (3 * b + i), T - P)
                        out = VB[b % 2][:, P * i:P * i + P]
                        last = nc.tensor.transpose(out, vt[:, tok:tok + P], g.ident[:, :])
                    last.then_inc(v_ready, 1)

                def maxima(h, x):
                    i, part, k0, n = MAX_UNITS[x]
                    y = NM * h + x
                    out = MAXB[y % 2]
                    if y == 0:
                        wait(pe, qk_done, p, NU, NU - 2)
                        wait(pe, x_done, p, NU, NU - 1)
                        pe.wait_ge(cum_in, 32 * (p + 1))
                        pe.wait_ge(rows_set, 4)
                    if x == SHORT and h == 0:
                        wait(pe, qk_done, p, NU, NU)
                    wait(pe, max_read, p, PM, y - 1)
                    q0 = META + P * i
                    diagonal = k0 + n == q0 + P
                    last = nc.tensor.matmul(out[:, 0:n], q_hi[h][0:KMAX, q0:q0 + P], k_hi[h][0:KMAX, k0:k0 + n],
                                            start=True, stop=not diagonal)
                    if diagonal:
                        last = nc.tensor.matmul(out[:, n - P:n], g.ident_r[:, :], g.masks[:, P:2 * P],
                                                start=False, stop=True)
                    last.then_inc(max_ready, 1)

                def turn_maxima(h):
                    wait(pe, nm_done, p, 2, h + 1)
                    wait(pe, m_done, p, 2, h)
                    nc.tensor.transpose(MT[:, 0:P], nm[:, :], g.ident[:, :]).then_inc(mt_ready, 1)

                def scores_open(w):
                    h, (c, kt, k0, q0, n) = w // NW, ST_UNITS[w % NW]
                    out = ST[w % 3]
                    wait(pe, exp_done, p, PW, w - 2 if w >= 3 else 0)
                    kh, kl = k_hi[h][0:DK, k0:k0 + P], k_lo[h][0:DK, k0:k0 + P]
                    nc.tensor.matmul(out[:, 0:n], kl, q_hi[h][0:DK, q0:q0 + n], start=True, stop=False)
                    nc.tensor.matmul(out[:, 0:n], kh, q_lo[h][0:DK, q0:q0 + n], start=False, stop=False)
                    d0, d1 = max(q0, P * kt), min(q0 + n, P * kt + P)
                    if d0 < d1:
                        m0 = 2 * P if kt == 8 else d0 - P * kt
                        nc.tensor.matmul(out[:, d0 - q0:d1 - q0], g.ident_r[:, :],
                                         g.masks[:, m0:m0 + d1 - d0], start=False, stop=False)

                def scores_close(w):
                    h, (c, kt, k0, q0, n) = w // NW, ST_UNITS[w % NW]
                    if w % NW == 0:
                        pe.wait_ge(m_in, 64 * p + 32 * (h + 1))
                    nc.tensor.matmul(ST[w % 3][:, 0:n], k_hi[h][0:KALL, k0:k0 + P], q_hi[h][0:KALL, q0:q0 + n],
                                     start=False, stop=True).then_inc(st_ready, 1)

                def weigh(w):
                    h, (c, kt, k0, q0, n) = w // NW, ST_UNITS[w % NW]
                    cq0 = REAL_TOKENS[c][0]
                    out = OB[c][:, q0 - cq0:q0 - cq0 + n]
                    wait_split(pe, p, w + 1)
                    if kt == 0:
                        wait(pe, o_done, p, 4, 2 * h + c - 1)
                        if w == 0:
                            pe.wait_ge(ones_set, 1)
                            wait(pe, v_done, p, 3, 3)
                    cols = slice(VD * h, VD * h + P)
                    last_of = w % NW == LAST_OF[c]
                    nc.tensor.matmul(out, v_hi[:, kt, cols], p_hi[:, w % 3, 0:n], start=(kt == 0), stop=False)
                    nc.tensor.matmul(out, v_lo[:, kt, cols], p_hi[:, w % 3, 0:n], start=False, stop=False)
                    nc.tensor.matmul(out, v_hi[:, kt, cols], p_lo[:, w % 3, 0:n], start=False,
                                     stop=last_of).then_inc(pv_done, 1)

                def between(c, k):
                    if (c, k) == (0, 3):
                        broadcast(NU - 2)
                    elif (c, k) == (0, 2):
                        sums(NU - 1)
                    elif (c, k) == (1, 2):
                        broadcast(NU - 1)
                    elif (c, k) == (2, 1):
                        values(0)
                    x = {0: k - 7, 1: k + 1, 2: 8 + k}[c]
                    if c == 1 and x >= SHORT:
                        x = SHORT if k == KD - 1 else -1
                    if 0 <= x < NM:
                        maxima(0, x)

                for step in range(NU):
                    products(step)
                    if step >= 1:
                        sums(step - 1)
                    if step >= 2:
                        broadcast(step - 2)
                for c in range(3):
                    products(NU + c, between)
                values(1)
                turn_maxima(0)
                for x in range(EARLY):
                    if x == 2:
                        values(2)
                    if x in OPEN_AT:
                        scores_open(OPEN_AT.index(x))
                    maxima(1, x)
                for w in range(PW):
                    if w >= len(OPEN_AT):
                        scores_open(w)
                    scores_close(w)
                    if w < NM - EARLY:
                        maxima(1, EARLY + w)
                    if w == NM - EARLY + 1:
                        turn_maxima(1)
                    if w >= 3:
                        weigh(w - 3)
                for w in range(PW - 3, PW):
                    weigh(w)
            over_pairs(pe, pair)

        @block.vector
        def _(dve):
            nc.vector.memset(nm[:, :], 0.0)
            nc.vector.memset(mpart[:, :, :], NEG)
            nc.vector.memset(threes[:, :], 3.0).then_inc(small_set, 1)

            def weights_lo(p, i):
                j, x = i // 2, slice(512 * (i % 2), 512 * (i % 2) + 512)
                wait(dve, whi_done, p, 6, i + 1)
                nc.vector.tensor_tensor(w_lo[:, j, x], raw[:, j, x], w_hi[:, j, x].bitcast(F32),
                                        ALU.subtract).then_inc(wlo_done, 1)

            def pair(p, last=False):
                def mean_squares(u):
                    is_q = units[u][0]
                    wait(dve, sum_ready, p, NU, u + 1)
                    wait(dve, newton, p, 4 * NU, 4 * u - 4)
                    nc.vector.tensor_scalar(ms[:, u % 2, :], SUM[:, 0:3 * NH], 4.0 if is_q else 4.0 / DK,
                                            4 * DK * EPS if is_q else 4 * EPS, ALU.mult, ALU.add).then_inc(ms_done, 1)

                def scale(u):
                    is_q, c = units[u]
                    t0, n = QK_TOKENS[c]
                    src = PROJ[u % 4]
                    wait(dve, rs_done, p, NU, u + 1)
                    col = g.FQ_COL if is_q else g.FK_COL
                    wait(dve, qk_done, p, NU, u - 1)
                    for j in range(2):
                        r = slice(FOX_D * j, FOX_D * (j + 1))
                        last = nc.vector.scalar_tensor_tensor(x32[:, 2 * (u % 2) + j, 0:n], src[r, 0:n],
                                                              g.gains[r, col:col + 1], rs[r, u % 2, 0:n],
                                                              ALU.mult, ALU.mult)
                    last.then_inc(x_done, 1)

                def split_lo(u):
                    is_q, c = units[u]
                    t0, n = QK_TOKENS[c]
                    hi, lo = (q_hi, q_lo) if is_q else (k_hi, k_lo)
                    wait(dve, xhi_done, p, NU, u + 1)
                    for j in range(2):
                        last = nc.vector.tensor_tensor(lo[j][0:FOX_D, t0:t0 + n], x32[:, 2 * (u % 2) + j, 0:n],
                                                       hi[j][0:FOX_D, t0:t0 + n].bitcast(F32), ALU.subtract)
                    last.then_inc(qk_done, 1)

                def maxima(h, x):
                    i, part, k0, n = MAX_UNITS[x]
                    wait(dve, max_ready, p, PM, NM * h + x + 1)
                    if x == 0:
                        wait(dve, nm_done, p, 2, h)
                    nc.vector.tensor_reduce(mpart[:, i, part:part + 1], MAXB[(NM * h + x) % 2][:, 0:n], AX_X,
                                            ALU.max).then_inc(max_read, 1)

                def join_maxima(h):
                    wait(dve, max_read, p, PM, NM * (h + 1))
                    wait(dve, mt_ready, p, 2, h)
                    nc.vector.tensor_reduce(nm[:, 0:QT], mpart[:, :, :], AX_X, ALU.max, negate=True).then_inc(nm_done, 1)

                def split_maxima(h):
                    wait(dve, mt_ready, p, 2, h + 1)
                    wait(dve, m_in, p, 64, 32 * h)
                    nc.vector.tensor_copy(m_hi[:, :], MT[0:QT, 0:P]).then_inc(mhi_done, 1)
                    wait(dve, mhi_done, p, 2, h + 1)
                    nc.vector.tensor_tensor(m_lo[:, :], MT[0:QT, 0:P], m_hi[:, :].bitcast(F32),
                                            ALU.subtract).then_inc(m_done, 1)

                for step in range(1, NU + 1):
                    mean_squares(step - 1)
                    if step >= 2:
                        scale(step - 2)
                    if step >= 3:
                        split_lo(step - 3)
                for x in range(NM):
                    if x == 1:
                        split_lo(NU - 2)
                    if x == SHORT - 3:
                        scale(NU - 1)
                    if x == SHORT - 1:
                        split_lo(NU - 1)
                    maxima(0, x)
                join_maxima(0)
                split_maxima(0)
                for x in range(EARLY):
                    maxima(1, x)
                for w in range(PW):
                    n = ST_UNITS[w % NW][4]
                    if w < NM - EARLY:
                        maxima(1, EARLY + w)
                    if w == NM - EARLY:
                        join_maxima(1)
                    wait(dve, exp_done, p, PW, w + 1)
                    wait(dve, pv_done, p, PW, w - 2 if w >= 3 else 0)
                    nc.vector.tensor_copy(p_hi[:, w % 3, 0:n], p32[:, w % 2, 0:n]).then_inc(phi_done, 1)
                    if w % LO_DVE == LO_DVE - 1:
                        wait(dve, phi_done, p, PW, w + 1)
                        nc.vector.tensor_tensor(p_lo[:, w % 3, 0:n], p32[:, w % 2, 0:n],
                                                p_hi[:, w % 3, 0:n].bitcast(F32), ALU.subtract).then_inc(plo_dve, 1)
                    if w == NM - EARLY + 1:
                        split_maxima(1)
                    for h, c in finish_after.get(w, ()):
                        rows = slice(VD * h, VD * h + VD)
                        q0 = REAL_TOKENS[c][0] - META
                        wait(dve, rden_done, p, 4, 2 * h + c + 1)
                        nc.vector.tensor_tensor(g.o_fox[rows, p, q0:q0 + 512], OB[c][rows, :], rden[rows, :],
                                                ALU.mult).then_inc(o_done, 1)
                    if not last and w in W_LO_AT:
                        weights_lo(p + 1, W_LO_AT.index(w))
            for i in range(4):
                weights_lo(0, i)
            nc.vector.memset(v_lo[:, :, VD:2 * VD].bitcast(F32), 0.0)
            nc.vector.memset(v_hi[:, :, VD:2 * VD].bitcast(F32), 1.0).then_inc(ones_set, 1)
            for i in range(4, 6):
                weights_lo(0, i)
            dve.wait_ge(small_set, 1)
            over_pairs(dve, pair)


def latent_attention_phase(nc, g):
    DK = MLA_D
    KALL = DK + 2
    NU = 6
    units = [(is_q, c) for c in range(3) for is_q in (True, False)]
    V_TILES = (range(0, 5), range(5, 9))
    MAXIMA_FROM = NU + 2
    TURN_STEP, V_STEP = NW - 1, NW - 1
    FINISH_0, FINISH_1 = 7, 2
    ROPE_ROWS = slice(NOPE, MLA_D)
    with ExitStack() as s:
        sb = lambda n, sh, dt=F32: s.enter_context(nc.sbuf_tensor(f"mla_{n}", sh, dt))
        sem = lambda n: g.semaphore(f"mla_{n}")
        q_hi = [sb(f"q_hi{i}", [KALL, T], F32R) for i in range(2)]
        q_lo = [sb(f"q_lo{i}", [DK, T], F32R) for i in range(2)]
        k_hi = [sb(f"k_hi{i}", [KALL, T], F32R) for i in range(2)]
        k_lo = [sb(f"k_lo{i}", [DK, T], F32R) for i in range(2)]
        v_hi, v_lo = sb("v_hi", [P, 9, 3 * VD], F32R), sb("v_lo", [P, 9, 3 * VD], F32R)
        p32 = sb("p32", [P, 2, 512])
        p_hi, p_lo = sb("p_hi", [P, 2, 512], F32R), sb("p_lo", [P, 2, 512], F32R)
        sq, rs = sb("sq", [P, 384]), sb("rs", [P, 384])
        x32, by_cos, by_sin = sb("x32", [P, 2, 384]), sb("by_cos", [P, 384]), sb("by_sin", [P, 384])
        rden = sb("rden", [P, 512])
        ms, r0, nt = sb("ms", [P, 2, 3]), sb("r0", [P, 2, 3]), sb("nt", [P, 2, 3])
        threes = sb("threes", [P, 3])
        mpart, nm = sb("mpart", [P, QT, 3]), sb("nm", [P, P])
        m_hi, m_lo = sb("m_hi", [QT, P], F32R), sb("m_lo", [QT, P], F32R)
        UK, UV = 2 * MLA_D, 2 * MLA_D + NOPE
        w_head = [sb(f"w_head{i}", [P, UV + VD]) for i in range(2)]
        bank = [s.enter_context(nc.psum_tensor(f"mla_bank{i}", [P, 512], F32)) for i in range(8)]
        ST, OB = bank[0:2], bank[2:4]
        PROJ, BC = bank[4:7], bank[7]
        SUM_AT = 400
        MAXB, MT, VB = (bank[4], bank[7]), bank[5], (bank[6], bank[7])

        small_set, rows_set, ones_set = sem("small_set"), sem("rows_set"), sem("ones_set")
        w_in = [sem(f"w_in{i}") for i in range(2)]
        m_in = sem("m_in")
        proj_ready, squared, sum_ready, ms_done, logged, rooted, newton = (
            sem("proj_ready"), sem("squared"), sem("sum_ready"), sem("ms_done"), sem("logged"), sem("rooted"),
            sem("newton"))
        bc_ready, rs_done = sem("bc_ready"), sem("rs_done")
        x_done, x_turned, rope_steps, xhi_done, qk_done = (sem("x_done"), sem("x_turned"), sem("rope_steps"),
                                                           sem("xhi_done"), sem("qk_done"))
        v_ready, vhi_done, v_done = sem("v_ready"), sem("vhi_done"), sem("v_done")
        max_ready, max_read, nm_done, mt_ready, mhi_done, m_done = (sem("max_ready"), sem("max_read"),
                                                                    sem("nm_done"), sem("mt_ready"),
                                                                    sem("mhi_done"), sem("m_done"))
        st_ready, exp_done, phi_done, plo_done, pv_done = (sem("st_ready"), sem("exp_done"), sem("phi_done"),
                                                           sem("plo_done"), sem("pv_done"))
        ln_done, rden_done, o_done = sem("ln_done"), sem("rden_done"), sem("o_done")
        block = s.enter_context(nc.Block())

        def upto(eng, sem, per_head, p, h, more):
            wait(eng, sem, p, 2 * per_head, per_head * h + more)

        def shifted(p, h, w):
            if w >= 2:
                return h, w - 2
            return None if isinstance(p, int) and p == 0 and h == 0 else (h - 1, w - 2 + NW)

        def maximum_of(w, place):
            x = 3 * (w - MAXIMA_FROM) + place
            return x if 0 <= x < NM else None

        def v_columns(v, h, b):
            t = V_TILES[b]
            return v[:, t[0]:t[-1] + 1, 2 * VD * (h % 2):2 * VD * (h % 2) + VD]

        def v_tiles(b):
            return VB[b][:, 0:VD * len(V_TILES[b])].rearrange("p (t a) -> p t a", a=VD)

        def split_of(h, u):
            return (q_hi if units[u][0] else k_hi)[h % 2], (q_lo if units[u][0] else k_lo)[h % 2]

        @block.sync
        def _(sp):
            def weights(p, i):
                upto(sp, v_ready, 2, p, i - 2, 2)
                sp.dma_start(w_head[i][:, :], g.dram["mla"][2 * p + i]).then_inc(w_in[i], 16)

            def maxima_rows(p, h):
                upto(sp, m_done, 1, p, h, 1)
                sp.wait_ge(rows_set, 4)
                for src, r in ((m_hi, DK), (m_lo, DK + 1)):
                    sp.dma_start(q_hi[h % 2][r:r + 1, META:T].bitcast(F32).rearrange("o (a b) -> o a b", a=QT),
                                 src[:, :].bitcast(F32)).then_inc(m_in, 16)

            def pair(p, last=False):
                if not last:
                    weights(p + 1, 0)
                maxima_rows(p, 1)
                if not last:
                    weights(p + 1, 1)
                    maxima_rows(p, 2)
            weights(0, 0)
            weights(0, 1)
            maxima_rows(0, 0)
            over_pairs(sp, pair)

        @block.gpsimd
        def _(pool):
            pool.wait_ge(small_set, 1)

            def newton_step(p, h, u):
                r, m, t = r0[:, u % 2, :], ms[:, u % 2, :], nt[:, u % 2, :]
                upto(pool, rooted, NU, p, h, u + 1)
                nc.gpsimd.tensor_tensor(t, m, r, ALU.mult).then_inc(newton, 1)
                upto(pool, newton, 4 * NU, p, h, 4 * u + 1)
                nc.gpsimd.tensor_tensor(t, t, r, ALU.mult).then_inc(newton, 1)
                upto(pool, newton, 4 * NU, p, h, 4 * u + 2)
                nc.gpsimd.tensor_tensor(t, threes[:, :], t, ALU.subtract).then_inc(newton, 1)
                upto(pool, newton, 4 * NU, p, h, 4 * u + 3)
                nc.gpsimd.tensor_tensor(r, r, t, ALU.mult).then_inc(newton, 1)

            def head(p, h, more=True):
                for w in range(NW):
                    if more and w < NU:
                        newton_step(p, h + 1, w)
                    n = ST_UNITS[w][4]
                    upto(pool, phi_done, NW, p, h, w + 1)
                    nc.gpsimd.tensor_tensor(p_lo[:, w % 2, 0:n], p32[:, w % 2, 0:n],
                                            p_hi[:, w % 2, 0:n].bitcast(F32), ALU.subtract).then_inc(plo_done, 1)

            def pair(p, last=False):
                head(p, 0)
                head(p, 1, more=not last)
            rows_of_ones = (k_hi[0], q_hi[0], k_hi[1], q_hi[1])
            for u in range(NU):
                newton_step(0, 0, u)
                if u < 4:
                    pool.wait_ge(newton, 4 * (u + 1))
                    nc.gpsimd.memset(rows_of_ones[u][DK:KALL, :].bitcast(F32), 1.0).then_inc(rows_set, 1)
                    pool.wait_ge(rows_set, u + 1)
            over_pairs(pool, pair)

        @block.scalar
        def _(act):
            def early(p, h, w):
                u = w - 3
                if 0 <= u < NU:
                    t0, n = QK_TOKENS[units[u][1]]
                    if units[u][0]:
                        upto(act, rope_steps, 9, p, h, 3 * (u // 2) + 3)
                    else:
                        upto(act, x_done, NU, p, h, u + 1)
                    if u == 0:
                        upto(act, st_ready, NW, p, h - 1, 0)
                    nc.scalar.copy(split_of(h, u)[0][0:DK, t0:t0 + n], x32[0:DK, u % 2, 0:n]).then_inc(xhi_done, 1)
                if w < NU:
                    is_q, c = units[w]
                    t0, n = QK_TOKENS[c]
                    upto(act, proj_ready, NU, p, h, w + 1)
                    upto(act, sum_ready, NU, p, h, w - 1)
                    src = PROJ[w % 3]
                    if is_q:
                        nc.scalar.activation(sq[0:DK, 0:n], src[0:DK, 0:n], ACT.Square).then_inc(squared, 1)
                    else:
                        nc.scalar.activation(g.ksq[0:NOPE, t0:t0 + n], src[0:NOPE, 0:n],
                                             ACT.Square).then_inc(squared, 1)

            def late(p, h, w):
                if w < NU:
                    upto(act, ms_done, NU, p, h, w + 1)
                    upto(act, bc_ready, NU, p, h, w - 1)
                    nc.scalar.activation(r0[:, w % 2, :], ms[:, w % 2, :], ACT.Ln).then_inc(logged, 1)
                    upto(act, logged, NU, p, h, w + 1)
                    nc.scalar.activation(r0[:, w % 2, :], r0[:, w % 2, :], ACT.Exp, scale=-0.5).then_inc(rooted, 1)
                if 1 <= w <= NU:
                    u = w - 1
                    n = QK_TOKENS[units[u][1]][1]
                    upto(act, bc_ready, NU, p, h, u + 1)
                    upto(act, x_done, NU, p, h, u)
                    nc.scalar.copy(rs[0:DK, 0:n], BC[0:DK, 0:n]).then_inc(rs_done, 1)
                if w == V_STEP:
                    upto(act, pv_done, NW, p, h - 1, 0)
                    for b in range(2):
                        upto(act, v_ready, 2, p, h, b + 1)
                        nc.scalar.copy(v_columns(v_hi, h, b), v_tiles(b)).then_inc(vhi_done, 1)

            def exponential(p, h, w):
                n = ST_UNITS[w][4]
                upto(act, st_ready, NW, p, h, w + 1)
                upto(act, plo_done, NW, p, h, w - 1)
                nc.scalar.activation(p32[:, w % 2, 0:n], ST[w % 2][:, 0:n], ACT.Exp).then_inc(exp_done, 1)

            def finish(p, h, c):
                rows, ones_rows = (slice(0, VD), slice(VD, P))[::1 if h % 2 == 0 else -1]
                upto(act, pv_done, NW, p, h, LAST_OF[c] + 1)
                upto(act, o_done, 2, p, h, c)
                nc.scalar.activation(rden[rows, :], OB[c][ones_rows, :], ACT.Ln).then_inc(ln_done, 1)
                upto(act, ln_done, 2, p, h, c + 1)
                nc.scalar.activation(rden[rows, :], rden[rows, :], ACT.Exp, scale=-1.0).then_inc(rden_done, 1)

            def head(p, h, more=True):
                for w in range(NW):
                    if more:
                        early(p, h + 1, w)
                    exponential(p, h, w)
                    if more:
                        late(p, h + 1, w)
                    if w == FINISH_0:
                        finish(p, h, 0)
                    if w == FINISH_1 and shifted(p, h, 1):
                        finish(p, h - 1, 1)

            def pair(p, last=False):
                head(p, 0)
                head(p, 1, more=not last)
            act.preload_act_table_set("natural_log_exp_and_others")
            for w in range(NW):
                early(0, 0, w)
                late(0, 0, w)
            over_pairs(act, pair)
            finish(PAIRS - 1, 1, 1)

        @block.tensor
        def _(pe):
            def products(p, h, u):
                is_q, c = units[u]
                t0, n = QK_TOKENS[c]
                out, w = PROJ[u % 3], w_head[h % 2]
                if u == 0:
                    upto(pe, max_read, NM, p, h, 0)
                    pe.wait_ge(w_in[h % 2], 16 * (p + (h // 2 + 1)))
                elif u == 1:
                    upto(pe, m_done, 1, p, h, 0)
                elif u == 2:
                    upto(pe, v_done, 2, p, h, -1)
                elif units[u - 3][0]:
                    upto(pe, rope_steps, 9, p, h, 3 * ((u - 3) // 2) + 2)
                else:
                    upto(pe, x_done, NU, p, h, u - 2)
                if is_q:
                    for k in range(2):
                        last = nc.tensor.matmul(out[0:DK, 0:n], w[:, k * DK:(k + 1) * DK], g.cq[:, k, t0:t0 + n],
                                                start=(k == 0), stop=(k == 1))
                else:
                    last = nc.tensor.matmul(out[0:NOPE, 0:n], w[:, UK:UK + NOPE], g.ckv[:, t0:t0 + n],
                                            start=True, stop=True)
                last.then_inc(proj_ready, 1)

            def sums(p, h, u):
                is_q, c = units[u]
                t0, n = QK_TOKENS[c]
                upto(pe, squared, NU, p, h, u + 1)
                src = sq[0:DK, 0:n] if is_q else g.ksq[0:DK, t0:t0 + n]
                for i, off in enumerate(QK_TILES[c]):
                    last = nc.tensor.matmul(PROJ[u % 3][:, SUM_AT + i:SUM_AT + i + 1], src[:, off:off + P],
                                            g.ones[0:DK, 0:1], start=True, stop=True)
                last.then_inc(sum_ready, 1)

            def broadcast(p, h, u):
                upto(pe, newton, 4 * NU, p, h, 4 * u + 4)
                if u == 0:
                    upto(pe, v_done, 2, p, h, 0)
                else:
                    upto(pe, rs_done, NU, p, h, u)
                for i, off in enumerate(QK_TILES[units[u][1]]):
                    last = nc.tensor.matmul(BC[0:DK, off:off + P], r0[:, u % 2, i:i + 1].broadcast_to([P, DK]),
                                            g.ident[:, :], start=True, stop=True)
                last.then_inc(bc_ready, 1)

            def turn(p, h, u):
                n = QK_TOKENS[units[u][1]][1]
                upto(pe, x_done, NU, p, h, u + 1)
                nc.tensor.matmul(PROJ[u % 3][0:DK, 0:n], g.rot[NOPE:DK, 0:DK], x32[NOPE:DK, u % 2, 0:n],
                                 start=True, stop=True).then_inc(x_turned, 1)

            def values(p, h, b):
                if b == 0:
                    upto(pe, x_done, NU, p, h, NU)
                else:
                    upto(pe, max_read, NM, p, h, NM)
                for i, t in enumerate(V_TILES[b]):
                    tok = min(P * t, T - P)
                    last = nc.tensor.matmul(VB[b][:, VD * i:VD * i + VD], g.ckv[:, tok:tok + P],
                                            w_head[h % 2][:, UV:UV + VD], start=True, stop=True)
                last.then_inc(v_ready, 1)

            def maxima(p, h, w, place):
                x = maximum_of(w, place)
                if x is None:
                    return
                i, part, k0, n = MAX_UNITS[x]
                out = MAXB[x % 2]
                if x == 0:
                    upto(pe, qk_done, NU, p, h, NU - 2)
                elif x == 1:
                    upto(pe, rs_done, NU, p, h, NU)
                else:
                    upto(pe, max_read, NM, p, h, x - 1)
                if x == SHORT:
                    upto(pe, qk_done, NU, p, h, NU)
                q0 = META + P * i
                diagonal = k0 + n == q0 + P
                last = nc.tensor.matmul(out[:, 0:n], q_hi[h % 2][0:DK, q0:q0 + P], k_hi[h % 2][0:DK, k0:k0 + n],
                                        start=True, stop=not diagonal)
                if diagonal:
                    last = nc.tensor.matmul(out[:, n - P:n], g.ident_r[:, :], g.masks[:, P:2 * P],
                                            start=False, stop=True)
                last.then_inc(max_ready, 1)

            def turn_maxima(p, h):
                upto(pe, nm_done, 1, p, h, 1)
                nc.tensor.transpose(MT[:, 0:P], nm[:, :], g.ident[:, :]).then_inc(mt_ready, 1)

            def scores(p, h, w):
                c, kt, k0, q0, n = ST_UNITS[w]
                out = ST[w % 2]
                upto(pe, exp_done, NW, p, h, w - 1)
                kh, kl = k_hi[h % 2][:, k0:k0 + P], k_lo[h % 2][:, k0:k0 + P]
                qh, ql = q_hi[h % 2], q_lo[h % 2]
                nc.tensor.matmul(out[:, 0:n], kl[0:DK], qh[0:DK, q0:q0 + n], start=True, stop=False)
                nc.tensor.matmul(out[:, 0:n], kh[0:DK], ql[0:DK, q0:q0 + n], start=False, stop=False)
                d0, d1 = max(q0, P * kt), min(q0 + n, P * kt + P)
                if d0 < d1:
                    m0 = 2 * P if kt == 8 else d0 - P * kt
                    nc.tensor.matmul(out[:, d0 - q0:d1 - q0], g.ident_r[:, :],
                                     g.masks[:, m0:m0 + d1 - d0], start=False, stop=False)
                if w == 0:
                    upto(pe, m_in, 32, p, h, 32)
                    pe.wait_ge(rows_set, 4)
                nc.tensor.matmul(out[:, 0:n], kh[0:KALL], qh[0:KALL, q0:q0 + n], start=False,
                                 stop=True).then_inc(st_ready, 1)

            def weigh(p, h, w):
                c, kt, k0, q0, n = ST_UNITS[w]
                cq0 = REAL_TOKENS[c][0]
                out = OB[c][:, q0 - cq0:q0 - cq0 + n]
                upto(pe, plo_done, NW, p, h, w + 1)
                if kt == 0:
                    upto(pe, o_done, 2, p, h, c - 1)
                    if c == 0:
                        pe.wait_ge(ones_set, 1)
                        upto(pe, v_done, 2, p, h, 2)
                cols = slice(VD * (h % 2), VD * (h % 2) + P)
                nc.tensor.matmul(out, v_hi[:, kt, cols], p_hi[:, w % 2, 0:n], start=(kt == 0), stop=False)
                nc.tensor.matmul(out, v_lo[:, kt, cols], p_hi[:, w % 2, 0:n], start=False, stop=False)
                nc.tensor.matmul(out, v_hi[:, kt, cols], p_lo[:, w % 2, 0:n], start=False,
                                 stop=w == LAST_OF[c]).then_inc(pv_done, 1)

            def prepare(p, h, w):
                if w < NU:
                    sums(p, h, w)
                if 1 <= w <= NU:
                    broadcast(p, h, w - 1)
                maxima(p, h, w, 2)
                if w == TURN_STEP:
                    turn_maxima(p, h)
                if w == V_STEP:
                    values(p, h, 0)
                    values(p, h, 1)

            def head(p, h, more=True):
                for w in range(NW):
                    if more and w < NU:
                        products(p, h + 1, w)
                    if more:
                        maxima(p, h + 1, w, 0)
                    scores(p, h, w)
                    if more:
                        maxima(p, h + 1, w, 1)
                    if more and 0 <= w - 2 < NU and units[w - 2][0]:
                        turn(p, h + 1, w - 2)
                    if shifted(p, h, w):
                        weigh(p, *shifted(p, h, w))
                    if more:
                        prepare(p, h + 1, w)

            def pair(p, last=False):
                head(p, 0)
                head(p, 1, more=not last)
            for w in range(NW):
                if w < NU:
                    products(0, 0, w)
                maxima(0, 0, w, 0)
                maxima(0, 0, w, 1)
                if 0 <= w - 2 < NU and units[w - 2][0]:
                    turn(0, 0, w - 2)
                prepare(0, 0, w)
            over_pairs(pe, pair)
            for w in range(NW - 2, NW):
                weigh(PAIRS - 1, 1, w)

        @block.vector
        def _(dve):
            nc.vector.memset(nm[:, :], 0.0)
            nc.vector.memset(mpart[:, :, :], NEG)
            nc.vector.memset(threes[:, :], 3.0).then_inc(small_set, 1)
            dve.wait_ge(small_set, 1)

            def mean_squares(p, h, u):
                is_q = units[u][0]
                upto(dve, sum_ready, NU, p, h, u + 1)
                upto(dve, newton, 4 * NU, p, h, 4 * u - 4)
                nc.vector.tensor_scalar(ms[:, u % 2, :], PROJ[u % 3][:, SUM_AT:SUM_AT + 3],
                                        4.0 if is_q else 4.0 / DK, 4 * DK * EPS if is_q else 4 * EPS,
                                        ALU.mult, ALU.add).then_inc(ms_done, 1)

            def scale(p, h, u):
                is_q, c = units[u]
                t0, n = QK_TOKENS[c]
                src, x = PROJ[u % 3], x32[:, u % 2, 0:n]
                upto(dve, rs_done, NU, p, h, u + 1)
                upto(dve, qk_done, NU, p, h, u - 1)
                if is_q:
                    nc.vector.scalar_tensor_tensor(x[0:DK], src[0:DK, 0:n], g.gains[0:DK, g.MQ_COL:g.MQ_COL + 1],
                                                   rs[0:DK, 0:n], ALU.mult, ALU.mult).then_inc(x_done, 1)
                    upto(dve, x_done, NU, p, h, u + 1)
                    nc.vector.tensor_tensor(by_cos[ROPE_ROWS, 0:n], x[ROPE_ROWS], g.cos[ROPE_ROWS, t0:t0 + n],
                                            ALU.mult).then_inc(rope_steps, 1)
                else:
                    nc.vector.tensor_tensor(x[ROPE_ROWS], g.krope[ROPE_ROWS, t0:t0 + n], rs[ROPE_ROWS, 0:n], ALU.mult)
                    nc.vector.scalar_tensor_tensor(x[0:NOPE], src[0:NOPE, 0:n], g.gains[0:NOPE, g.MK_COL:g.MK_COL + 1],
                                                   rs[0:NOPE, 0:n], ALU.mult, ALU.mult).then_inc(x_done, 1)

            def rope(p, h, u):
                t0, n = QK_TOKENS[units[u][1]]
                x, q_count = x32[ROPE_ROWS, u % 2, 0:n], u // 2
                upto(dve, x_turned, 3, p, h, q_count + 1)
                nc.vector.tensor_tensor(by_sin[ROPE_ROWS, 0:n], PROJ[u % 3][ROPE_ROWS, 0:n],
                                        g.sin[ROPE_ROWS, t0:t0 + n], ALU.mult).then_inc(rope_steps, 1)
                upto(dve, rope_steps, 9, p, h, 3 * q_count + 2)
                nc.vector.tensor_tensor(x, by_cos[ROPE_ROWS, 0:n], by_sin[ROPE_ROWS, 0:n],
                                        ALU.add).then_inc(rope_steps, 1)

            def split_lo(p, h, u):
                t0, n = QK_TOKENS[units[u][1]]
                hi, lo = split_of(h, u)
                upto(dve, xhi_done, NU, p, h, u + 1)
                nc.vector.tensor_tensor(lo[0:DK, t0:t0 + n], x32[0:DK, u % 2, 0:n],
                                        hi[0:DK, t0:t0 + n].bitcast(F32), ALU.subtract).then_inc(qk_done, 1)

            def maxima(p, h, w, place):
                x = maximum_of(w, place)
                if x is None:
                    return
                i, part, k0, n = MAX_UNITS[x]
                upto(dve, max_ready, NM, p, h, x + 1)
                nc.vector.tensor_reduce(mpart[:, i, part:part + 1], MAXB[x % 2][:, 0:n], AX_X,
                                        ALU.max).then_inc(max_read, 1)
                if x == NM - 1:
                    upto(dve, max_read, NM, p, h, NM)
                    upto(dve, mt_ready, 1, p, h, 0)
                    nc.vector.tensor_reduce(nm[:, 0:QT], mpart[:, :, :], AX_X, ALU.max,
                                            negate=True).then_inc(nm_done, 1)

            def early(p, h, w):
                maxima(p, h, w, 0)
                maxima(p, h, w, 1)
                if 0 <= w - 2 < NU and units[w - 2][0]:
                    rope(p, h, w - 2)
                if w < NU:
                    mean_squares(p, h, w)

            def prepare(p, h, w):
                if 0 <= w - 3 < NU:
                    split_lo(p, h, w - 3)
                if 1 <= w <= NU:
                    scale(p, h, w - 1)
                maxima(p, h, w, 2)
                if w == TURN_STEP:
                    upto(dve, mt_ready, 1, p, h, 1)
                    upto(dve, m_in, 32, p, h, 0)
                    nc.vector.tensor_copy(m_hi[:, :], MT[0:QT, 0:P]).then_inc(mhi_done, 1)
                    upto(dve, mhi_done, 1, p, h, 1)
                    nc.vector.tensor_tensor(m_lo[:, :], MT[0:QT, 0:P], m_hi[:, :].bitcast(F32),
                                            ALU.subtract).then_inc(m_done, 1)
                if w == V_STEP:
                    for b in range(2):
                        upto(dve, vhi_done, 2, p, h, b + 1)
                        nc.vector.tensor_tensor(v_columns(v_lo, h, b), v_tiles(b), v_columns(v_hi, h, b).bitcast(F32),
                                                ALU.subtract).then_inc(v_done, 1)

            def finish(p, h, c):
                rows = slice(VD * (h % 2), VD * (h % 2) + VD)
                q0 = REAL_TOKENS[c][0] - META
                upto(dve, rden_done, 2, p, h, c + 1)
                nc.vector.tensor_tensor(g.o_mla[rows, p if h >= 0 else p - 1, q0:q0 + 512], OB[c][rows, :],
                                        rden[rows, :], ALU.mult).then_inc(o_done, 1)

            def head(p, h, more=True):
                for w in range(NW):
                    n = ST_UNITS[w][4]
                    if more:
                        early(p, h + 1, w)
                    upto(dve, exp_done, NW, p, h, w + 1)
                    upto(dve, pv_done, NW, p, h, w - 1)
                    nc.vector.tensor_copy(p_hi[:, w % 2, 0:n], p32[:, w % 2, 0:n]).then_inc(phi_done, 1)
                    if more:
                        prepare(p, h + 1, w)
                    if w == FINISH_0:
                        finish(p, h, 0)
                    if w == FINISH_1 and shifted(p, h, 1):
                        finish(p, h - 1, 1)

            def pair(p, last=False):
                head(p, 0)
                head(p, 1, more=not last)
            for w in range(NW):
                early(0, 0, w)
                prepare(0, 0, w)
                if w == 0:
                    nc.vector.memset(v_lo[:, :, VD:2 * VD].bitcast(F32), 0.0)
                    nc.vector.memset(v_hi[:, :, VD:2 * VD].bitcast(F32), 1.0).then_inc(ones_set, 1)
            over_pairs(dve, pair)
            finish(PAIRS - 1, 1, 1)


def gate_phase(nc, g):
    with ExitStack() as s:
        sb = lambda n, sh, dt=F32: s.enter_context(nc.sbuf_tensor("gt_" + n, sh, dt))
        sem = lambda n: g.semaphore("gt_" + n)
        raw = sb("raw", [P, 3, D])
        w_hi, w_lo = sb("w_hi", [P, 3, D], F32R), sb("w_lo", [P, 3, D], F32R)
        o_hi, o_lo = sb("o_hi", [P, KD, SEQ], F32R), sb("o_lo", [P, KD, SEQ], F32R)
        sg = sb("sg", [P, 3, 512])
        bank = [s.enter_context(nc.psum_tensor(f"gt_bank{i}", [P, 512], F32)) for i in range(8)]
        raw_in = [sem(f"raw_in{i}") for i in range(3)]
        whi_done, wlo_done, ohi_done, olo_done = sem("whi_done"), sem("wlo_done"), sem("ohi_done"), sem("olo_done")
        ready, opened, shut, mult_done = sem("ready"), sem("opened"), sem("shut"), sem("mult_done")
        uhi_done, ulo_done = sem("uhi_done"), sem("ulo_done")
        block = s.enter_context(nc.Block())
        o_tile = lambda t: (g.o_fox if t < PAIRS else g.o_mla)[:, t % PAIRS, :]
        UNITS = [("gf", 0), ("gf", 1), ("gm", 0), ("bf", 0), ("bm", 0), ("gm", 1), ("bf", 1), ("bm", 1)]

        def over_tiles(eng, body):
            body(0)
            with eng.Fori(1, KD) as m:
                body(m)

        @block.sync
        def _(sp):
            def tile(m):
                for j in range(3):
                    wait(sp, wlo_done, m, 3, j - 2)
                    sp.dma_start(raw[:, j, :], g.dram["gate"][3 * m + j]).then_inc(raw_in[j], 16)
            over_tiles(sp, tile)

        @block.gpsimd
        def _(pool):
            def split_lo(m, j):
                wait(pool, whi_done, m, 3, j + 1)
                nc.gpsimd.tensor_tensor(w_lo[:, j, :], raw[:, j, :], w_hi[:, j, :].bitcast(F32),
                                        ALU.subtract).then_inc(wlo_done, 1)
            for j in range(2):
                split_lo(0, j)
            for t in range(0, KD, 2):
                pool.wait_ge(ohi_done, t + 1)
                nc.gpsimd.tensor_tensor(o_lo[:, t, :], o_tile(t), o_hi[:, t, :].bitcast(F32),
                                        ALU.subtract).then_inc(olo_done, 1)
            split_lo(0, 2)
            with pool.Fori(1, KD) as m:
                for j in range(3):
                    split_lo(m, j)

        @block.scalar
        def _(act):
            def split_hi(m, j, used):
                act.wait_ge(raw_in[j], 16 * (m + 1))
                wait(act, ready, m, 8, used - 8)
                nc.scalar.copy(w_hi[:, j, :], raw[:, j, :]).then_inc(whi_done, 1)

            def sigmoid(m, which, c, slot, unit):
                wait(act, ready, m, 8, unit + 1)
                wait(act, shut, m, 4, {0: -2 + 0, 1: 0, 2: 0, 5: 2}[unit])
                bias = g.gains[:, bass.ds(m + (g.BG_COL + KD * which), 1)]
                nc.scalar.activation(sg[:, slot, :], bank[unit][:, :], ACT.Sigmoid, bias=bias).then_inc(opened, 1)

            def mixed_hi(c):
                act.wait_ge(ready, 8 * (KD - 1) + (3, 6)[c])
                for t in range(KD):
                    act.wait_ge(shut, 4 * t + 2 * (c + 1))
                    nc.scalar.copy(g.u_hi[:, t, META + 512 * c:META + 512 * c + 512],
                                   o_tile(t)[:, 512 * c:512 * c + 512]).then_inc(uhi_done, 1)

            def tile(m, more=True):
                if not (isinstance(m, int) and m == 0):
                    split_hi(m, 2, 8)
                sigmoid(m, 0, 0, 0, 0)
                sigmoid(m, 0, 1, 1, 1)
                if more:
                    split_hi(m + 1, 0, 2)
                sigmoid(m, 1, 0, 2, 2)
                if not more:
                    mixed_hi(0)
                sigmoid(m, 1, 1, 2, 5)
                if more:
                    split_hi(m + 1, 1, 6)
                else:
                    mixed_hi(1)

            split_hi(0, 0, 0)
            split_hi(0, 1, 0)
            for t in range(KD):
                nc.scalar.copy(o_hi[:, t, :], o_tile(t)).then_inc(ohi_done, 1)
            split_hi(0, 2, 0)
            for m in range(KD):
                tile(m, more=m < KD - 1)
        @block.tensor
        def _(pe):
            def tile(m):
                for u, (kind, c) in enumerate(UNITS):
                    t0 = REAL_TOKENS[c][0]
                    out = bank[u]
                    if kind[0] == "g":
                        wait(pe, opened, m, 4, {0: -3, 1: -2, 2: -1, 5: 0}[u])
                        j = 0 if kind == "gf" else 1
                        if c == 0:
                            wait(pe, wlo_done, m, 3, j + 1)
                        for k in range(KD):
                            last = mm3(nc, out[:, :], w_hi[:, j, k * P:(k + 1) * P], w_lo[:, j, k * P:(k + 1) * P],
                                       g.u_hi[:, k, t0:t0 + 512], g.u_lo[:, k, t0:t0 + 512], k == 0, k == KD - 1)
                    else:
                        wait(pe, shut, m, 4, {3: -3, 4: -2, 6: -1, 7: 0}[u])
                        if u == 3:
                            wait(pe, wlo_done, m, 3, 3)
                            pe.wait_ge(olo_done, KD)
                        first = 0 if kind == "bf" else PAIRS
                        for k in range(first, first + PAIRS):
                            x = slice(512 * c, 512 * c + 512)
                            last = mm3(nc, out[:, :], w_hi[:, 2, k * P:(k + 1) * P], w_lo[:, 2, k * P:(k + 1) * P],
                                       o_hi[:, k, x], o_lo[:, k, x], k == first, k == first + PAIRS - 1)
                    last.then_inc(ready, 1)
            over_tiles(pe, tile)

        @block.vector
        def _(dve):
            def mixed_lo(c):
                for t in range(KD):
                    dve.wait_ge(uhi_done, KD * c + t + 1)
                    x = slice(META + 512 * c, META + 512 * c + 512)
                    nc.vector.tensor_tensor(g.u_lo[:, t, x], o_tile(t)[:, 512 * c:512 * c + 512],
                                            g.u_hi[:, t, x].bitcast(F32), ALU.subtract).then_inc(ulo_done, 1)

            def tile(m, dst, m_dst, last=False):
                for c in range(2):
                    base = (3, 6)[c]
                    for which in range(2):
                        slot = c if which == 0 else 2
                        wait(dve, ready, m, 8, base + which + 1)
                        wait(dve, opened, m, 4, {(0, 0): 1, (0, 1): 3, (1, 0): 2, (1, 1): 4}[(c, which)])
                        ins = nc.vector.tensor_tensor(sg[:, slot, :], bank[base + which][:, :], sg[:, slot, :], ALU.mult)
                        if which == 0:
                            ins.then_inc(shut, 1)
                        else:
                            ins.then_inc(mult_done, 1)
                    wait(dve, mult_done, m, 2, c + 1)
                    wait(dve, shut, m, 4, 2 * c + 1)
                    nc.vector.tensor_tensor(dst[:, m_dst, 512 * c:512 * c + 512], sg[:, c, :], sg[:, 2, :],
                                            ALU.add).then_inc(shut, 1)
                    if last:
                        mixed_lo(c)

            for t in range(1, KD, 2):
                dve.wait_ge(ohi_done, t + 1)
                nc.vector.tensor_tensor(o_lo[:, t, :], o_tile(t), o_hi[:, t, :].bitcast(F32),
                                        ALU.subtract).then_inc(olo_done, 1)
            dve.wait_ge(olo_done, KD)
            tile(0, g.o_fox, 0)
            with dve.Fori(1, PAIRS) as m:
                tile(m, g.o_fox, m)
            with dve.Fori(PAIRS, KD - 1) as m:
                tile(m, g.o_mla, m - PAIRS)
            tile(KD - 1, g.o_mla, PAIRS - 1, last=True)


def out_proj_phase(nc, g):
    with ExitStack() as s:
        sb = lambda n, sh, dt=F32: s.enter_context(nc.sbuf_tensor("op_" + n, sh, dt))
        sem = lambda n: g.semaphore("op_" + n)
        raw = sb("raw", [P, 3, D])
        w_hi, w_lo = sb("w_hi", [P, 3, D], F32R), sb("w_lo", [P, 3, D], F32R)
        bank = [s.enter_context(nc.psum_tensor(f"op_bank{i}", [P, 512], F32)) for i in range(4)]
        raw_in = [sem(f"raw_in{i}") for i in range(3)]
        h_in = [sem(f"h_in{i}") for i in range(KD)]
        whi_done, wlo_done, ready, added = sem("whi_done"), sem("wlo_done"), sem("ready"), sem("added")
        sq = sb("sq", [P, 2, T])
        square_sum = SquareSum(nc, g, "op", slice(META, T), [sq[:, j, :] for j in range(2)])
        block = s.enter_context(nc.Block())

        @block.sync
        def _(sp):
            for m in range(KD):
                if m >= 3:
                    sp.wait_ge(wlo_done, m - 2)
                sp.dma_start(raw[:, m % 3, :], g.dram["wout"][m]).then_inc(raw_in[m % 3], 16)
                sp.dma_start(g.h[:, m, :], g.dram["hsave"][:, m, :]).then_inc(h_in[m], 16)

        @block.scalar
        def _(act):
            for m in range(KD):
                act.wait_ge(raw_in[m % 3], 16 * (m // 3 + 1))
                if m >= 3:
                    act.wait_ge(ready, 2 * (m - 2))
                nc.scalar.copy(w_hi[:, m % 3, :], raw[:, m % 3, :]).then_inc(whi_done, 1)
                if m >= 3:
                    act.wait_ge(added, 2 * (m - 2))
                    square_sum.square(act, m - 3)
            for m in range(KD - 3, KD):
                act.wait_ge(added, 2 * (m + 1))
                square_sum.square(act, m)

        @block.gpsimd
        def _(pool):
            for m in range(KD):
                pool.wait_ge(whi_done, m + 1)
                nc.gpsimd.tensor_tensor(w_lo[:, m % 3, :], raw[:, m % 3, :], w_hi[:, m % 3, :].bitcast(F32),
                                        ALU.subtract).then_inc(wlo_done, 1)

        @block.tensor
        def _(pe):
            for m in range(KD):
                pe.wait_ge(wlo_done, m + 1)
                for c, (t0, n) in enumerate(REAL_TOKENS):
                    u = 2 * m + c
                    if u >= 4:
                        pe.wait_ge(added, u - 3)
                    for k in range(KD):
                        last = mm3(nc, bank[u % 4][:, :], w_hi[:, m % 3, k * P:(k + 1) * P],
                                   w_lo[:, m % 3, k * P:(k + 1) * P], g.u_hi[:, k, t0:t0 + n],
                                   g.u_lo[:, k, t0:t0 + n], k == 0, k == KD - 1)
                    last.then_inc(ready, 1)

        @block.vector
        def _(dve):
            for m in range(KD):
                dve.wait_ge(h_in[m], 16)
                for c, (t0, n) in enumerate(REAL_TOKENS):
                    u = 2 * m + c
                    dve.wait_ge(ready, u + 1)
                    nc.vector.tensor_tensor(g.h[:, m, t0:t0 + n], g.h[:, m, t0:t0 + n], bank[u % 4][:, :],
                                            ALU.add).then_inc(added, 1)
                if m >= 4:
                    square_sum.add(dve, m - 4)
            for m in range(KD - 4, KD):
                square_sum.add(dve, m)




class Shared:
    FFN1_GAIN, MIX_GAIN, FFN2_GAIN = 0, KD, 2 * KD
    EPS_COL, BF_COL = 3 * KD, 3 * KD + 1
    FQ_COL, FK_COL, MQ_COL, MK_COL, CN_COL, BG_COL = [3 * KD + x for x in (2, 3, 4, 5, 6, 9)]

    def __init__(self):
        self.dram = {}


def build(nc, g):
    with ExitStack() as s:
        first_half = []

        def of_first_half(name):
            first_half.append(nc.alloc_semaphore(name))
            return first_half[-1]
        g.semaphore = of_first_half
        sb = lambda n, sh, dt=F32: s.enter_context(nc.sbuf_tensor(n, sh, dt))
        g.ident = sb("ident", [P, P])
        g.ones = sb("ones", [P, P])
        g.gains = sb("gains", [P, g.dram["gains"].shape[1]])
        g.ssum = sb("ssum", [P, QT + 1])
        g.u_hi = sb("u_hi", [P, KD, T], F32R)
        g.u_lo = sb("u_lo", [P, KD, T], F32R)
        with ExitStack() as mix:
            mb = lambda n, sh, dt=F32: mix.enter_context(nc.sbuf_tensor(n, sh, dt))
            g.ident_r = mb("ident_r", [P, P], F32R)
            g.masks = mb("masks", [P, 2 * P + META], F32R)
            g.head_sum = mb("head_sum", [P, P])
            g.rot = mb("rot", [P, P])
            with nc.sbuf_tensor("h_in", [P, KD, T], F32) as h, nc.sbuf_tensor("sumsq_in", [P, T], F32) as sumsq:
                g.h, g.sumsq = h, sumsq
                load_phase(nc, g)
                ffn_phase(nc, g, "f1", g.dram["ffn1"], g.FFN1_GAIN, ALL_TOKENS, first=True)
                forget_phase(nc, g)
            g.o_fox = mb("o_fox", [P, PAIRS, SEQ])
            fox_attention_phase(nc, g)
            nc.clear_and_free_semaphores(first_half)
            nc.all_engine_barrier()
            g.semaphore = lambda name: s.enter_context(nc.semaphore(name))
            g.o_mla = mb("o_mla", [P, PAIRS, SEQ])
            with ExitStack() as lat:
                lb = lambda n, sh, dt=F32: lat.enter_context(nc.sbuf_tensor(n, sh, dt))
                g.cq, g.ckv = lb("cq", [P, 2, T]), lb("ckv", [P, T])
                g.krope, g.ksq = lb("krope", [P, T]), lb("ksq", [P, T])
                g.cos, g.sin = lb("cos", [P, T]), lb("sin", [P, T])
                latent_phase(nc, g)
                latent_attention_phase(nc, g)
            gate_phase(nc, g)
        with nc.sbuf_tensor("h_out", [P, KD, T], F32) as h, nc.sbuf_tensor("sumsq_out", [P, T], F32) as sumsq:
            g.h, g.sumsq = h, sumsq
            out_proj_phase(nc, g)
            ffn_phase(nc, g, "f2", g.dram["ffn2"], g.FFN2_GAIN, REAL_TOKENS)


def _k_blocks(w):
    n = w.shape[1] // P
    return w.reshape(KD, P, n, P).transpose(2, 1, 0, 3).reshape(n, P, D)


def _ffn_blocks(w_gu, w_down):
    gate, up = _k_blocks(w_gu[:, :DFF]), _k_blocks(w_gu[:, DFF:])
    down = w_down.reshape(FT, P, D)
    gu = lambda i: [gate[2 * i], up[2 * i], gate[2 * i + 1], up[2 * i + 1]]
    dn = lambda i: [down[2 * i], down[2 * i + 1]]
    order = gu(0)
    for i in range(1, FT // 2):
        order += gu(i) + dn(i - 1)
    return np.stack(order + dn(FT // 2 - 1))


def _columns(v):
    return v.reshape(-1, P).T


def layout(i):
    a = {n: np.asarray(v) for n, v in i.items()}
    out = {"x": a["x"][0], "meta": a["meta_tokens"]}
    out["ffn1"] = _ffn_blocks(a["ffn1_w_gu"][0], a["ffn1_w_down"][0])
    out["ident"] = np.eye(P, dtype=np.float32)
    out["ones"] = np.ones((P, P), np.float32)
    w_in = a["w_in"][0]
    cuts = np.cumsum([FOX_D * HEADS] * 3 + [HEADS, CQ, CKV, ROPE, 2 * D])
    fq, fk, fv, fl, cq, ckv, kr, gates = np.split(w_in, cuts[:-1], axis=1)
    out["fox"] = np.stack([_k_blocks(w)[p] for p in range(PAIRS) for w in (fq, fk, fv)])
    shared = np.zeros((D, P), np.float32)
    shared[:, 0:HEADS] = fl
    shared[:, NOPE:MLA_D] = kr
    out["misc"] = np.concatenate([_k_blocks(shared), _k_blocks(ckv), _k_blocks(cq)])
    uq = a["mla_w_uq"][0].reshape(2, P, HEADS, MLA_D).transpose(2, 1, 0, 3).reshape(HEADS, P, 2 * MLA_D)
    ukv = a["mla_w_ukv"][0].reshape(P, HEADS, 2 * NOPE).transpose(1, 0, 2)
    out["mla"] = np.concatenate([uq, ukv], axis=2)
    branch = np.concatenate([a["w_branch_fox"][0], a["w_branch_mla"][0]])
    gate_blocks, branch_blocks = _k_blocks(gates), _k_blocks(branch)
    out["gate"] = np.stack([w for m in range(KD) for w in (gate_blocks[m], gate_blocks[KD + m], branch_blocks[m])])
    out["wout"] = _k_blocks(a["w_out"][0])
    out["ffn2"] = _ffn_blocks(a["ffn2_w_gu"][0], a["ffn2_w_down"][0])

    r, c = np.arange(P)[:, None], np.arange(P)[None, :]
    masks = np.zeros((P, 4 * P + META), np.float32)
    masks[:, 0:P] = np.where(r > c, NEG, 0)
    masks[:, P:2 * P] = np.where(c > r, NEG, 0)
    last = r - (P - META)
    masks[:, 2 * P:2 * P + META] = np.where((last < 0) | (last > c[:, :META]), NEG, 0)
    masks[:, 2 * P + META:3 * P + META] = (r // FOX_D == c // FOX_D)
    half = ROPE // 2
    for i in range(half):
        masks[NOPE + half + i, 3 * P + META + NOPE + i] = -1.0
        masks[NOPE + i, 3 * P + META + NOPE + half + i] = 1.0
    out["masks"] = masks
    freq = np.float32(10000.0) ** (-np.arange(0, ROPE, 2, dtype=np.float32) / np.float32(ROPE))
    angle = np.arange(T, dtype=np.float32)[None, :] * np.tile(freq, 2)[:, None]
    out["cos"], out["sin"] = np.cos(angle), np.sin(angle)

    def column(v):
        full = np.zeros((P, 1), np.float32)
        full[:len(v), 0] = v
        return full

    const = lambda x: np.full((P, 1), x, np.float32)
    out["gains"] = np.concatenate([
        _columns(a["ffn1_norm"][0]), _columns(a["mix_norm"][0]), _columns(a["ffn2_norm"][0]),
        const(EPS), column(a["b_forget"][0]),
        column(np.tile(a["fox_q_norm"][0], 2)), column(np.tile(a["fox_k_norm"][0], 2)),
        column(a["mla_q_norm"][0]), column(a["mla_k_norm"][0]),
        _columns(a["mla_ckv_norm"][0]), _columns(a["mla_cq_norm"][0]), _columns(a["b_gate"][0])], axis=1)
    return {n: np.ascontiguousarray(v, dtype=np.float32) for n, v in out.items()}


def kernel(**inputs):
    import concourse.bacc as bacc
    from concourse.bass_utils import run_bass_kernel_spmd
    arrays = layout(inputs)
    nc = bacc.Bacc("TRN2", target_bir_lowering=False, num_devices=1)
    g = Shared()
    for name, a in arrays.items():
        g.dram[name] = nc.dram_tensor(f"in_{name}", a.shape, mybir.dt.from_np(a.dtype), kind="ExternalInput").ap()
    for name, shape in (("hsave", (P, KD, T)), ("krope", (ROPE, T)), ("cum", (2, HEADS, T))):
        g.dram[name] = nc.dram_tensor(f"kept_{name}", shape, F32, kind="Internal").ap()
    g.dram["out"] = nc.dram_tensor("out", (SEQ, D), F32, kind="ExternalOutput").ap()
    build(nc, g)
    r = run_bass_kernel_spmd(nc, [{f"in_{n}": v for n, v in arrays.items()}], core_ids=[0])
    return np.asarray(r.results[0]["out"]).reshape(1, SEQ, D)
```
